# Optimizing a Trainium2 kernel written in Bass

```python
import math
import jax, jax.numpy as jnp
from jax import lax
import numpy as np

D_MODEL = 1024
BATCH = 1
SEQ = 1024
DEPTH = 1

GRID_W = 64
CTX_LEN = 256
MIX_DIM = D_MODEL
ATT_DIM = MIX_DIM // 2
CONV_DIM = MIX_DIM - ATT_DIM
HEAD_DIM = 64
N_HEADS = ATT_DIM // HEAD_DIM
NA_ROWS = 8
NA_COLS = 16
CONV_WIDTH = 31
D_FF = 4 * D_MODEL
IN_PROJ_DIM = 3 * ATT_DIM + 2 * CONV_DIM
N_MOD = 6
ROPE_BASE = 10000.0
EPS = 1e-6


def rms_norm(x, g):
    xf = x.astype(jnp.float32)
    y = xf * lax.rsqrt(jnp.mean(xf * xf, axis=-1, keepdims=True) + EPS)
    return (y * g.astype(jnp.float32)).astype(x.dtype)

def modulate(h, shift, scale):
    return h * (1 + scale) + shift

def split_heads(t):
    b, l, _ = t.shape
    return t.reshape(b, l, N_HEADS, HEAD_DIM)

def split_proj(p):
    q = split_heads(p[..., :ATT_DIM])
    k = split_heads(p[..., ATT_DIM:2 * ATT_DIM])
    v = split_heads(p[..., 2 * ATT_DIM:3 * ATT_DIM])
    u = p[..., 3 * ATT_DIM:]
    return q, k, v, u

def rope_half(xh, pos):
    n_pairs = xh.shape[-1] // 2
    inv_freq = ROPE_BASE ** (-jnp.arange(n_pairs, dtype=jnp.float32) / n_pairs)
    ang = pos.astype(jnp.float32)[:, None] * inv_freq[None, :]
    cos = jnp.cos(ang)[None, :, None, :]
    sin = jnp.sin(ang)[None, :, None, :]
    x1 = xh[..., :n_pairs].astype(jnp.float32)
    x2 = xh[..., n_pairs:].astype(jnp.float32)
    return jnp.concatenate([x1 * cos - x2 * sin, x2 * cos + x1 * sin], axis=-1).astype(xh.dtype)

def axial_rope(x, row_pos, col_pos):
    half = HEAD_DIM // 2
    return jnp.concatenate([rope_half(x[..., :half], row_pos),
                            rope_half(x[..., half:], col_pos)], axis=-1)

def conformer_conv(u, kernel, bias, ln_g, ln_b):
    a, b = jnp.split(u, 2, axis=-1)
    h = a * jax.nn.sigmoid(b)
    pad = CONV_WIDTH // 2
    h = lax.conv_general_dilated(h, kernel[:, None, :].astype(h.dtype), window_strides=(1,),
                                 padding=[(pad, pad)], dimension_numbers=('NWC', 'WIO', 'NWC'),
                                 feature_group_count=CONV_DIM) + bias
    hf = h.astype(jnp.float32)
    mu = jnp.mean(hf, axis=-1, keepdims=True)
    var = jnp.mean(jnp.square(hf - mu), axis=-1, keepdims=True)
    hn = (hf - mu) * lax.rsqrt(var + EPS) * ln_g + ln_b
    return jax.nn.silu(hn).astype(u.dtype)

def sq_relu_mlp(h, w1, w2):
    return jnp.square(jax.nn.relu(h @ w1)) @ w2

def context_attention(q, k, v):
    b, lc = q.shape[0], q.shape[1]
    s = jnp.einsum('bqhd,bkhd->bhqk', q, k).astype(jnp.float32) * HEAD_DIM ** -0.5
    p = jax.nn.softmax(s, axis=-1).astype(v.dtype)
    o = jnp.einsum('bhqk,bkhd->bqhd', p, v)
    return o.reshape(b, lc, ATT_DIM)

def neighbourhood_attention(q_rot, q, k_rot, v, k_ctx, v_ctx, rpb):
    b, l, h, dh = q.shape
    rows = l // GRID_W
    kr = min(NA_ROWS, rows)
    scale = dh ** -0.5
    q_rot_g = q_rot.reshape(b, rows, GRID_W, h, dh).transpose(1, 0, 2, 3, 4)
    q_g = q.reshape(b, rows, GRID_W, h, dh).transpose(1, 0, 2, 3, 4)
    k_g = k_rot.reshape(b, rows, GRID_W, h, dh)
    v_g = v.reshape(b, rows, GRID_W, h, dh)
    row_start = np.clip(np.arange(rows) - kr // 2, 0, rows - kr).astype(np.int32)
    col_start = np.clip(np.arange(GRID_W) - NA_COLS // 2, 0, GRID_W - NA_COLS)
    col_idx = (col_start[:, None] + np.arange(NA_COLS)[None, :]).astype(np.int32)
    col_off = (col_idx - np.arange(GRID_W)[:, None] + (NA_COLS - 1)).astype(np.int32)
    rpb_cols = rpb[:, :, col_off]

    def one_row(args):
        qr_rot, qr, r, rs = args
        k_rows = lax.dynamic_slice_in_dim(k_g, rs, kr, axis=1)
        v_rows = lax.dynamic_slice_in_dim(v_g, rs, kr, axis=1)
        kw = k_rows[:, :, col_idx]
        vw = v_rows[:, :, col_idx]
        row_off = rs + jnp.arange(kr) - r + (NA_ROWS - 1)
        bias = rpb_cols[:, row_off].transpose(0, 2, 1, 3)
        s_win = jnp.einsum('bqhd,biqjhd->bhqij', qr_rot, kw).astype(jnp.float32) * scale
        s_win = (s_win + bias.astype(jnp.float32)[None]).reshape(b, h, GRID_W, kr * NA_COLS)
        s_ctx = jnp.einsum('bqhd,bchd->bhqc', qr, k_ctx).astype(jnp.float32) * scale
        p = jax.nn.softmax(jnp.concatenate([s_win, s_ctx], axis=-1), axis=-1).astype(v.dtype)
        p_win = p[..., :kr * NA_COLS].reshape(b, h, GRID_W, kr, NA_COLS)
        p_ctx = p[..., kr * NA_COLS:]
        return (jnp.einsum('bhqij,biqjhd->bqhd', p_win, vw)
                + jnp.einsum('bhqc,bchd->bqhd', p_ctx, v_ctx))

    out = lax.map(one_row, (q_rot_g, q_g, jnp.arange(rows, dtype=jnp.int32), jnp.asarray(row_start)))
    return out.transpose(1, 0, 2, 3, 4).reshape(b, l, h * dh)

def first_inputs(seed: int = 0) -> dict:
    key = jax.random.key(seed)
    ks = jax.random.split(key, 18)
    n = jax.random.normal
    return {
        'x': n(ks[0], (BATCH, SEQ, D_MODEL), jnp.float32),
        'c': n(ks[1], (BATCH, D_MODEL), jnp.float32),
        'ctx': n(ks[2], (BATCH, CTX_LEN, D_MODEL), jnp.float32),
        'c_ctx': n(ks[3], (D_MODEL,), jnp.float32),
        'w_ada': n(ks[4], (DEPTH, D_MODEL, N_MOD * D_MODEL), jnp.float32) * (0.5 * D_MODEL ** -0.5),
        'b_ada': 0.02 * n(ks[5], (DEPTH, N_MOD * D_MODEL), jnp.float32),
        'norm1_g': 1.0 + 0.02 * n(ks[6], (DEPTH, D_MODEL), jnp.float32),
        'norm2_g': 1.0 + 0.02 * n(ks[7], (DEPTH, D_MODEL), jnp.float32),
        'w_in': n(ks[8], (DEPTH, D_MODEL, IN_PROJ_DIM), jnp.float32) * D_MODEL ** -0.5,
        'dw_kernel': n(ks[9], (DEPTH, CONV_WIDTH, CONV_DIM), jnp.float32) * CONV_WIDTH ** -0.5,
        'dw_bias': 0.02 * n(ks[10], (DEPTH, CONV_DIM), jnp.float32),
        'conv_ln_g': 1.0 + 0.02 * n(ks[11], (DEPTH, CONV_DIM), jnp.float32),
        'conv_ln_b': 0.02 * n(ks[12], (DEPTH, CONV_DIM), jnp.float32),
        'rpb': 0.5 * n(ks[13], (DEPTH, N_HEADS, 2 * NA_ROWS - 1, 2 * NA_COLS - 1), jnp.float32),
        'w_out': n(ks[14], (DEPTH, MIX_DIM, D_MODEL), jnp.float32) * MIX_DIM ** -0.5,
        'w_mlp1': n(ks[15], (DEPTH, D_MODEL, D_FF), jnp.float32) * D_MODEL ** -0.5,
        'w_mlp2': n(ks[16], (DEPTH, D_FF, D_MODEL), jnp.float32) * D_FF ** -0.5,
        'final_g': 1.0 + 0.02 * n(ks[17], (D_MODEL,), jnp.float32),
    }

def first_block(x, c, ctx, c_ctx, w_ada, b_ada, norm1_g, norm2_g, w_in, dw_kernel, dw_bias,
              conv_ln_g, conv_ln_b, rpb, w_out, w_mlp1, w_mlp2, final_g):
    l = x.shape[1]
    t = jnp.arange(l, dtype=jnp.int32)
    row_pos = t // GRID_W
    col_pos = t % GRID_W
    silu_c = jax.nn.silu(c)
    silu_cc = jax.nn.silu(c_ctx)[None]
    for i in range(DEPTH):
        last = i == DEPTH - 1
        mod_x = (silu_c @ w_ada[i] + b_ada[i])[:, None, :]
        mod_c = (silu_cc @ w_ada[i] + b_ada[i])[:, None, :]
        sh1, sc1, g1, sh2, sc2, g2 = jnp.split(mod_x, N_MOD, axis=-1)
        csh1, csc1, cg1, csh2, csc2, cg2 = jnp.split(mod_c, N_MOD, axis=-1)

        hx = modulate(rms_norm(x, norm1_g[i]), sh1, sc1)
        hc = modulate(rms_norm(ctx, norm1_g[i]), csh1, csc1)
        qx, kx, vx, ux = split_proj(hx @ w_in[i])
        if last:
            kvc = hc @ w_in[i][:, ATT_DIM:3 * ATT_DIM]
            kc, vc = split_heads(kvc[..., :ATT_DIM]), split_heads(kvc[..., ATT_DIM:])
        else:
            qc, kc, vc, uc = split_proj(hc @ w_in[i])

        qx_rot = axial_rope(qx, row_pos, col_pos)
        kx_rot = axial_rope(kx, row_pos, col_pos)
        attn_x = neighbourhood_attention(qx_rot, qx, kx_rot, vx, kc, vc, rpb[i])
        conv_x = conformer_conv(ux, dw_kernel[i], dw_bias[i], conv_ln_g[i], conv_ln_b[i])
        x_new = x + g1 * (jnp.concatenate([attn_x, conv_x], axis=-1) @ w_out[i])

        hx2 = modulate(rms_norm(x_new, norm2_g[i]), sh2, sc2)
        x_new = x_new + g2 * sq_relu_mlp(hx2, w_mlp1[i], w_mlp2[i])

        if not last:
            attn_c = context_attention(qc, kc, vc)
            conv_c = conformer_conv(uc, dw_kernel[i], dw_bias[i], conv_ln_g[i], conv_ln_b[i])
            ctx = ctx + cg1 * (jnp.concatenate([attn_c, conv_c], axis=-1) @ w_out[i])
            hc2 = modulate(rms_norm(ctx, norm2_g[i]), csh2, csc2)
            ctx = ctx + cg2 * sq_relu_mlp(hc2, w_mlp1[i], w_mlp2[i])
        x = x_new
    return rms_norm(x, final_g)


MEM_LEN = 256
N_HEADS_MLA = 8
QK_NOPE_DIM = 64
QK_ROPE_DIM = 32
QK_HEAD_DIM = QK_NOPE_DIM + QK_ROPE_DIM
V_HEAD_DIM = 64
Q_LORA_RANK = 3 * D_MODEL // 8
KV_LORA_RANK = D_MODEL // 4
MLA_WIDTH = N_HEADS_MLA * V_HEAD_DIM
CONV_WIDTH_2 = D_MODEL // 2
CONV_K = 3
N_HEADS_MEM = 4
MEM_HEAD_DIM = 128
MEM_WIDTH = N_HEADS_MEM * MEM_HEAD_DIM

N_BRANCH = 3
Q_BLOCK = 128

IN_SIZES = (Q_LORA_RANK, KV_LORA_RANK, QK_ROPE_DIM,
            CONV_WIDTH_2, CONV_WIDTH_2, CONV_WIDTH_2,
            MEM_WIDTH,
            MLA_WIDTH, CONV_WIDTH_2, MEM_WIDTH,
            N_BRANCH * D_MODEL)
IN_WIDTH = sum(IN_SIZES)


def rmsnorm(t, g):
    tf = t.astype(jnp.float32)
    tf = tf * lax.rsqrt(jnp.mean(tf * tf, axis=-1, keepdims=True) + EPS)
    return tf.astype(t.dtype) * g

def split_cols(t, sizes):
    return jnp.split(t, np.cumsum(sizes)[:-1].tolist(), axis=-1)

def rope_tables(positions, dtype):
    inv_freq = ROPE_BASE ** (-jnp.arange(0, QK_ROPE_DIM, 2, dtype=jnp.float32) / QK_ROPE_DIM)
    ang = positions.astype(jnp.float32)[..., None] * inv_freq
    return (jnp.cos(ang)[:, :, None, :].astype(dtype),
            jnp.sin(ang)[:, :, None, :].astype(dtype))

def rope_tail(t, cos, sin):
    t_nope, t1, t2 = split_cols(t, (QK_NOPE_DIM, QK_ROPE_DIM // 2, QK_ROPE_DIM // 2))
    return jnp.concatenate([t_nope, t1 * cos - t2 * sin, t2 * cos + t1 * sin], axis=-1)

def blocked_bidirectional_attention(q, k, v):
    B, S, H, Dh = q.shape
    nblk = S // Q_BLOCK
    qb = q.reshape(B, nblk, Q_BLOCK, H, Dh).transpose(1, 0, 2, 3, 4)
    scale = Dh ** -0.5

    def one_block(q_blk):
        s = jnp.einsum('bqhd,bkhd->bhqk', q_blk, k).astype(jnp.float32) * scale
        p = jax.nn.softmax(s, axis=-1).astype(v.dtype)
        return jnp.einsum('bhqk,bkhd->bqhd', p, v)

    out = lax.map(one_block, qb)
    return out.transpose(1, 0, 2, 3, 4).reshape(B, S, H * v.shape[-1])

def centred_short_conv(z, w, b):
    out = lax.conv_general_dilated(
        z, w[:, None, :], window_strides=(1,),
        padding=((CONV_K // 2, CONV_K // 2),),
        dimension_numbers=('NWC', 'WIO', 'NWC'),
        feature_group_count=z.shape[-1])
    return out + b

def hybrid_layer(x, mem, cos, sin, norm_g, w_in, b_gate, q_norm_g, w_uq, kv_norm_g, w_ukv,
                 q_head_g, k_head_g, conv_w, conv_b, mem_norm_g, w_mkv, mem_q_g, mem_k_g,
                 w_br_attn, w_br_conv, w_br_mem, w_out):
    B, S, _ = x.shape
    M = mem.shape[1]
    h = rmsnorm(x, norm_g)
    proj = h @ w_in
    (q_lat, kv_lat, k_pe, c_b, c_c, c_u, q_mem,
     g_attn, g_conv, g_mem, r) = split_cols(proj, IN_SIZES)

    q = (rmsnorm(q_lat, q_norm_g) @ w_uq).reshape(B, S, N_HEADS_MLA, QK_HEAD_DIM)
    kv = (rmsnorm(kv_lat, kv_norm_g) @ w_ukv).reshape(B, S, N_HEADS_MLA, QK_NOPE_DIM + V_HEAD_DIM)
    k_nope, v = split_cols(kv, (QK_NOPE_DIM, V_HEAD_DIM))
    k_rope = jnp.broadcast_to(k_pe[:, :, None, :], (B, S, N_HEADS_MLA, QK_ROPE_DIM))
    k = jnp.concatenate([k_nope, k_rope], axis=-1)
    q = rope_tail(rmsnorm(q, q_head_g), cos, sin)
    k = rope_tail(rmsnorm(k, k_head_g), cos, sin)
    o_attn = blocked_bidirectional_attention(q, k, v) * jax.nn.silu(g_attn)

    o_conv = c_b * centred_short_conv(c_c * c_u, conv_w, conv_b) * jax.nn.silu(g_conv)

    mkv = (rmsnorm(mem, mem_norm_g) @ w_mkv).reshape(B, M, N_HEADS_MEM, 2 * MEM_HEAD_DIM)
    m_k, m_v = split_cols(mkv, (MEM_HEAD_DIM, MEM_HEAD_DIM))
    mq = rmsnorm(q_mem.reshape(B, S, N_HEADS_MEM, MEM_HEAD_DIM), mem_q_g)
    m_k = rmsnorm(m_k, mem_k_g)
    s = jnp.einsum('bshd,bmhd->bhsm', mq, m_k).astype(jnp.float32) * (MEM_HEAD_DIM ** -0.5)
    p = jax.nn.softmax(s, axis=-1).astype(m_v.dtype)
    o_mem = jnp.einsum('bhsm,bmhd->bshd', p, m_v).reshape(B, S, MEM_WIDTH) * jax.nn.silu(g_mem)

    r_attn, r_conv, r_mem = split_cols(jax.nn.sigmoid(r + b_gate), (D_MODEL, D_MODEL, D_MODEL))
    y = r_attn * (o_attn @ w_br_attn) + r_conv * (o_conv @ w_br_conv) + r_mem * (o_mem @ w_br_mem)
    return x + y @ w_out

def second_inputs(seed: int = 0) -> dict:
    key = jax.random.key(seed)
    ks = jax.random.split(key, 24)

    def nrm(k, shape, scale):
        return jax.random.normal(k, shape, jnp.float32) * scale

    def gain(k, shape):
        return 1.0 + 0.1 * jax.random.normal(k, shape, jnp.float32)

    x = nrm(ks[0], (BATCH, SEQ, D_MODEL), 1.0)
    mem = nrm(ks[1], (BATCH, MEM_LEN, D_MODEL), 1.0)
    offset = jax.random.randint(ks[2], (BATCH, 1), 0, 1024, dtype=jnp.int32)
    positions = jnp.arange(SEQ, dtype=jnp.int32)[None, :] + offset
    return {
        'x': x,
        'mem': mem,
        'positions': positions,
        'norm_g': gain(ks[3], (DEPTH, D_MODEL)),
        'w_in': nrm(ks[4], (DEPTH, D_MODEL, IN_WIDTH), D_MODEL ** -0.5),
        'b_gate': nrm(ks[5], (DEPTH, N_BRANCH * D_MODEL), 0.1),
        'q_norm_g': gain(ks[6], (DEPTH, Q_LORA_RANK)),
        'w_uq': nrm(ks[7], (DEPTH, Q_LORA_RANK, N_HEADS_MLA * QK_HEAD_DIM), Q_LORA_RANK ** -0.5),
        'kv_norm_g': gain(ks[8], (DEPTH, KV_LORA_RANK)),
        'w_ukv': nrm(ks[9], (DEPTH, KV_LORA_RANK, N_HEADS_MLA * (QK_NOPE_DIM + V_HEAD_DIM)), KV_LORA_RANK ** -0.5),
        'q_head_g': gain(ks[10], (DEPTH, QK_HEAD_DIM)),
        'k_head_g': gain(ks[11], (DEPTH, QK_HEAD_DIM)),
        'conv_w': nrm(ks[12], (DEPTH, CONV_K, CONV_WIDTH_2), CONV_K ** -0.5),
        'conv_b': nrm(ks[13], (DEPTH, CONV_WIDTH_2), 0.1),
        'mem_norm_g': gain(ks[14], (DEPTH, D_MODEL)),
        'w_mkv': nrm(ks[15], (DEPTH, D_MODEL, 2 * MEM_WIDTH), D_MODEL ** -0.5),
        'mem_q_g': gain(ks[16], (DEPTH, MEM_HEAD_DIM)),
        'mem_k_g': gain(ks[17], (DEPTH, MEM_HEAD_DIM)),
        'w_br_attn': nrm(ks[18], (DEPTH, MLA_WIDTH, D_MODEL), MLA_WIDTH ** -0.5),
        'w_br_conv': nrm(ks[19], (DEPTH, CONV_WIDTH_2, D_MODEL), CONV_WIDTH_2 ** -0.5),
        'w_br_mem': nrm(ks[20], (DEPTH, MEM_WIDTH, D_MODEL), MEM_WIDTH ** -0.5),
        'w_out': nrm(ks[21], (DEPTH, D_MODEL, D_MODEL), D_MODEL ** -0.5),
    }

def second_block(x, mem, positions, norm_g, w_in, b_gate, q_norm_g, w_uq, kv_norm_g, w_ukv,
              q_head_g, k_head_g, conv_w, conv_b, mem_norm_g, w_mkv, mem_q_g, mem_k_g,
              w_br_attn, w_br_conv, w_br_mem, w_out):
    cos, sin = rope_tables(positions, x.dtype)
    for i in range(DEPTH):
        x = hybrid_layer(x, mem, cos, sin, norm_g[i], w_in[i], b_gate[i], q_norm_g[i], w_uq[i],
                         kv_norm_g[i], w_ukv[i], q_head_g[i], k_head_g[i], conv_w[i], conv_b[i],
                         mem_norm_g[i], w_mkv[i], mem_q_g[i], mem_k_g[i],
                         w_br_attn[i], w_br_conv[i], w_br_mem[i], w_out[i])
    return x


def setup_inputs(seed=0):
    out = dict(first_inputs(seed))
    for name, value in second_inputs(seed + 1).items():
        if name != "x":
            out[name + "_2"] = value
    return out


def reference(
    x, c, ctx, c_ctx, w_ada, b_ada, norm1_g, norm2_g, w_in, dw_kernel, dw_bias, conv_ln_g,
    conv_ln_b, rpb, w_out, w_mlp1, w_mlp2, final_g, mem_2, positions_2, norm_g_2, w_in_2,
    b_gate_2, q_norm_g_2, w_uq_2, kv_norm_g_2, w_ukv_2, q_head_g_2, k_head_g_2, conv_w_2,
    conv_b_2, mem_norm_g_2, w_mkv_2, mem_q_g_2, mem_k_g_2, w_br_attn_2, w_br_conv_2, w_br_mem_2,
    w_out_2,
):
    x = first_block(
        x, c, ctx, c_ctx, w_ada, b_ada, norm1_g, norm2_g, w_in, dw_kernel, dw_bias, conv_ln_g,
        conv_ln_b, rpb, w_out, w_mlp1, w_mlp2, final_g,
    )
    return second_block(
        x, mem_2, positions_2, norm_g_2, w_in_2, b_gate_2, q_norm_g_2, w_uq_2, kv_norm_g_2,
        w_ukv_2, q_head_g_2, k_head_g_2, conv_w_2, conv_b_2, mem_norm_g_2, w_mkv_2, mem_q_g_2,
        mem_k_g_2, w_br_attn_2, w_br_conv_2, w_br_mem_2, w_out_2,
    )


_drawn_inputs = setup_inputs


def setup_inputs(seed=0):
    import zlib

    import numpy as np

    out = dict(_drawn_inputs(seed))
    spreads = {}
    factors = {'ctx': 2.682,
     'norm1_g': 8.0,
     'norm2_g': 5.147,
     'dw_bias': 8.0,
     'conv_ln_g': 8.0,
     'conv_ln_b': 8.0,
     'rpb': 6.693,
     'b_gate_2': 4.6,
     'q_norm_g_2': 8.0,
     'kv_norm_g_2': 7.921,
     'q_head_g_2': 8.0,
     'k_head_g_2': 8.0,
     'mem_norm_g_2': 8.0,
     'mem_q_g_2': 8.0,
     'mem_k_g_2': 8.0,
     'conv_b_2': 6.959}
    for name, (base, spread) in spreads.items():
        noise = np.random.default_rng([zlib.crc32(name.encode()), seed]).standard_normal(out[name].shape)
        drawn = base * np.exp(spread * noise) if base else spread * noise
        out[name] = __import__('jax').numpy.asarray(drawn.astype(out[name].dtype))
    for name, factor in factors.items():
        out[name] = (out[name] * factor).astype(out[name].dtype)
    return out
```

```python
from contextlib import ExitStack

import numpy as np

import concourse.bass as bass
from concourse import mybir

F32 = mybir.dt.float32
F32R = mybir.dt.float32r
I32 = mybir.dt.int32
ALU = mybir.AluOpType
ACT = mybir.ActivationFunctionType
AX = mybir.AxisListType.X

P = 128
T = 1024
TT = T // P
HALF = 512
D = 1024
KD = D // P
CTX = 256
EPS = 1e-6
W_GRID = 64
ROWS = T // W_GRID
HEADS = 8
HD = 64
NA_R, NA_C = 8, 16
TAPS = 31
PAD = TAPS // 2
FF_GROUPS = 4
KEYS = 10 * W_GRID
NKT = (KEYS + CTX) // P
VARIANT = [0, 1, 2, 2, 2, 2, 3, 4]
SHIFT = [0, -2, -4, -6, -8]
QK = 96
NOPE = 64
ROPE = 32
NQL, NKVL = 3, 2
MH = 4
TABLE = 2 * W_GRID - 1
TWO_PI = 2.0 * np.pi

SMALL = {}
_at = 0
for _name, _n in [("c", 16), ("b_ada", 48), ("norm1", 8), ("norm2", 8), ("final", 8), ("norm_2", 8),
                  ("memn", 8), ("ln_g", 4), ("ln_b", 4), ("dwb", 4), ("dww", 4 * TAPS), ("b_gate", 24),
                  ("qn", 3), ("kvn", 2), ("qh", 1), ("kh", 1), ("cw", 12), ("cb", 4), ("mq", 1), ("mk", 1),
                  ("invf", 1), ("sign", 1)]:
    SMALL[_name] = _at
    _at += _n
N_SMALL = _at

STAGE_UNITS = [("q", 4), ("k", 4), ("v", 4), ("u", 8), ("out1", 8), ("mlp", 16 * FF_GROUPS), ("lat", 6),
               ("uq", 3), ("uk", 2), ("uv", 1), ("gattn", 4), ("br0", 12), ("cv", 16), ("br1", 12),
               ("mkv", 8), ("qm", 4), ("gmem", 4), ("br2", 12), ("out2", 8)]
N_UNITS = sum(n for _, n in STAGE_UNITS)
UNIT0 = {}
_at = 0
for _name, _n in STAGE_UNITS:
    UNIT0[_name] = _at
    _at += _n
ATTN_SPLIT = UNIT0["out1"] + 2


KINDS = {
    "rms": [("rc", 8), ("r1", 8), ("lnv", 4), ("r2", 8), ("nf", 8), ("r3", 8), ("rq", 3), ("rk", 2), ("rm", 8)],
    "norm": [("nc", 8), ("n1", 8), ("lnn", 4), ("n2", 8), ("n3", 8), ("nq", 3), ("nk", 2), ("nm", 8)],
    "head": [("hq", 8), ("hk", 8), ("mk", 4), ("qm", 4)],
    "att": [("na", 64), ("mla", 64), ("ma", 32)],
    "gate": [("ga", 4), ("gm", 4)],
    "branch": [("br0", 8), ("br1", 8), ("br2", 8)],
}
SHARED = {tag: (kind, stages[:i]) for kind, stages in KINDS.items() for i, (tag, _) in enumerate(stages)}
COUNTS = {f"{tag}_rt": 1 for tag, _ in KINDS["rms"]} | {f"br{b}_part": 4 for b in range(3)} \
    | {"hq_part": 5, "hk_part": 6}


def build(nc, x_t, ctx_t, mem_t, w_ada, units, small, rope_c, rope_s, rpb_pad, mask, positions, out, x_spill):
    def sbuf_map():
        at = (nc.sbuf_base + 63) // 64 * 64
        return at, at + 43 * 1024 + 512

    base, arena = sbuf_map()

    def fixed(name, shape, offset, dt=F32):
        return nc.alloc_sbuf_tensor_at(name, [P, *shape], dt, offset=base + offset)

    def place(name, shape, kib, dt=F32):
        return nc.alloc_sbuf_tensor_at(name, [P, *shape], dt, offset=arena + int(kib * 1024))

    KIB = 1024
    w_raw = fixed("w_raw", [2, 1024], 0)
    w_hi = fixed("w_hi", [2, 1024], 8 * KIB, F32R)
    w_lo = fixed("w_lo", [2, 1024], 16 * KIB, F32R)
    tmp = fixed("tmp", [4, T], 24 * KIB)
    ident = fixed("ident", [P], 40 * KIB)
    ones = fixed("ones", [P], 40 * KIB + 512)
    par = fixed("par", [N_SMALL], 41 * KIB)
    der = fixed("der", [256], 41 * KIB + (4 * N_SMALL + 31) // 32 * 32)
    assert 4 * N_SMALL + 32 + 1024 <= 2560

    def sp_(name, n=1, k=0):
        return par[:, SMALL[name] + k:SMALL[name] + k + n]

    mod_x, mod_c = der[:, 0:48], der[:, 48:64]
    a1, a1c, a2 = der[:, 64:72], der[:, 72:80], der[:, 80:88]
    silu_c = der[:, 88:104]
    qh_s, mq_s = der[:, 104:105], der[:, 105:106]
    one_col = der[:, 106:107]
    eps_col = der[:, 107:108]
    row_max, neg_max, row_sum, inv_sum = (der[:, 112 + 2 * i:114 + 2 * i] for i in range(4))

    ada_buf = place("ada_buf", [2, KD, HALF], 0)
    ada_row = place("ada_row", [2, HALF], 32)
    ctx_sb = place("ctx_sb", [KD, CTX], 36)
    hc_hi = place("hc_hi", [KD, CTX], 44, F32R)
    hc_lo = place("hc_lo", [KD, CTX], 52, F32R)
    x_sb = place("x_sb", [KD, T], 64)
    h_hi = place("h_hi", [KD, T], 96, F32R)
    h_lo = place("h_lo", [KD, T], 128, F32R)
    q_t = place("q_t", [4, T], 0)
    q_rot = place("q_rot", [4, T], 16)
    k_ctx = place("k_ctx", [4, CTX], 32)
    v_ctx = place("v_ctx", [2, HALF], 36)
    cos1 = place("cos1", [T], 40)
    sin1 = place("sin1", [T], 60)
    k_rot = place("k_rot", [4, T], 64)
    v_tok = place("v_tok", [TT, HALF], 80)
    glu = place("glu", [4, T + 2 * PAD], 40)
    conv = place("conv", [4, T], 96)
    o_tok = place("o_tok", [TT, HALF], 112)
    bias_t = place("bias_t", [5, KEYS + CTX], 128)
    mask_t = place("mask_t", [5, KEYS], 145.5)
    toep = [place("toep0", [18, W_GRID], 57), place("toep1", [18, W_GRID], 158)]
    mix_hi = place("mix_hi", [KD, T], 0, F32R)
    mix_lo = place("mix_lo", [KD, T], 64, F32R)
    x1 = place("x1", [KD, T], 128)
    h2_hi = place("h2_hi", [KD, T], 96, F32R)
    h2_lo = place("h2_lo", [KD, T], 32, F32R)
    ff_hi = place("ff_hi", [KD, T], 0, F32R)
    ff_lo = place("ff_lo", [KD, T], 64, F32R)
    q_h = place("q_h", [HEADS, T], 0)
    k_h = place("k_h", [HEADS, T], 64)
    v2 = place("v2", [TT, HALF], 128)
    q_lat = place("q_lat", [NQL, T], 64)
    ql_hi = place("ql_hi", [NQL, T], 76, F32R)
    ql_lo = place("ql_lo", [NQL, T], 144, F32R)
    kv_lat = place("kv_lat", [NKVL, T], 128)
    kvl_hi = place("kvl_hi", [NKVL, T], 144, F32R)
    kvl_lo = place("kvl_lo", [NKVL, T], 152, F32R)
    k_pe = place("k_pe", [T], 136)
    cos2 = place("cos2", [T], 140)
    sin2 = place("sin2", [T], 160)
    pos_i = nc.alloc_sbuf_tensor_at("pos_i", [P, T], I32, offset=arena + 160 * 1024)
    o_tok2 = place("o_tok2", [TT, HALF], 144)
    o_hi = place("o_hi", [4, T], 0, F32R)
    o_lo = place("o_lo", [4, T], 16, F32R)
    y = place("y", [KD, T], 64)
    z_pad = place("z_pad", [T + 2], 128)
    mem_sb = place("mem_sb", [KD, CTX], 133)
    hm_hi = place("hm_hi", [KD, CTX], 141, F32R)
    hm_lo = place("hm_lo", [KD, CTX], 149, F32R)
    m_k = place("m_k", [MH, CTX], 157)
    m_v = place("m_v", [2, HALF], 133)
    q_mem = place("q_mem", [MH, T], 0)
    o_mem = place("o_mem", [TT, HALF], 137)
    y_hi = place("y_hi", [KD, T], 96, F32R)
    y_lo = place("y_lo", [KD, T], 32, F32R)
    x3 = place("x3", [KD, T], 128)

    prob = nc.alloc_sbuf_tensor_at("prob", [P, 2, T], F32, offset=base + 24 * KIB)
    prob_t = nc.alloc_sbuf_tensor_at("prob_t", [P, 2, TT, P], F32, offset=base + 32 * KIB)

    region = nc.alloc_psum_tensor("region", [P, 2, T], F32)
    aux = nc.alloc_psum_tensor("aux", [P, T], F32)
    pv = nc.alloc_psum_tensor("pv", [P, 2, HALF], F32)

    sems = {}

    def sem(name):
        tag, _, what = name.partition("_")
        if tag in SHARED:
            name = f"{SHARED[tag][0]}_{what}"
        if name not in sems:
            sems[name] = nc.alloc_semaphore(name)
        return sems[name]

    def reach(e, name, value):
        tag, _, what = name.partition("_")
        if tag in SHARED:
            kind, before = SHARED[tag]
            value = value + sum(COUNTS.get(f"{t}_{what}", n) for t, n in before)
        e.wait_ge(sem(name), value)

    raw_loaded = [sem("raw_loaded_0"), sem("raw_loaded_1")]
    free = [sem("region_free_0"), sem("region_free_1")]
    unit_split, unit_done = sem("unit_split"), sem("unit_done")

    class Pos:

        def __init__(self):
            self.use = 0
            self.count = {}

        def next_use(self):
            self.use += 1
            return self.use - 1

        def add(self, name, n=1):
            self.count[name] = self.count.get(name, 0) + n
            return self.count[name]

    def wait_region(e, use):
        if use >= 2:
            e.wait_ge(free[use % 2], use // 2)

    def copy(e, dst, src, **kw):
        return e.activation(dst, src, ACT.Copy, **kw)

    def mm3(pe, dst, wh, wl, xh, xl, first, last):
        pe.matmul(dst, wh, xh, start=first, stop=False)
        pe.matmul(dst, wh, xl, start=False, stop=False)
        return pe.matmul(dst, wl, xh, start=False, stop=last)

    def project(pe, use, unit, xh, xl, nk, width=T, m=P, off=0, step=P, wait_k=None):
        r, s = use % 2, unit % 2
        pe.wait_ge(unit_split, unit + 1)
        wait_region(pe, use)
        for lo in range(0, width, HALF):
            n = min(HALF, width - lo)
            for k in range(nk):
                if wait_k is not None and lo == 0:
                    wait_k(k)
                w = slice(off + k * step, off + k * step + m)
                last = mm3(pe, region[0:m, r, lo:lo + n], w_hi[:, s, w], w_lo[:, s, w],
                           xh[:, k, lo:lo + n], xl[:, k, lo:lo + n], k == 0, k == nk - 1)
        return last

    def project_tokens(pe, use, units, xh, xl, nk, tiles, cols, rhs):
        r = use % 2
        wait_region(pe, use)
        for i, t in enumerate(tiles):
            for k in range(nk):
                xs = slice(t * P, t * P + P)
                dst = region[:, r, i * cols:(i + 1) * cols]
                pe.matmul(dst, xh[:, k, xs], rhs(w_hi, k), start=(k == 0), stop=False)
                pe.matmul(dst, xl[:, k, xs], rhs(w_hi, k), start=False, stop=False)
                last = pe.matmul(dst, xh[:, k, xs], rhs(w_lo, k), start=False, stop=(k == nk - 1))
        return last

    def column_sums(pe, tag, src, nk, width, rows=P, ready=None):
        for k in range(nk):
            reach(pe, f"{tag}_sq", k + 1)
            for lo in range(0, width, HALF):
                n = min(HALF, width - lo)
                last = pe.matmul(aux[0:rows, lo:lo + n], ones[0:rows, 0:rows], src(k)[:, lo:lo + n],
                                 start=(k == 0), stop=(k == nk - 1))
            last.then_inc(sem(f"{tag}_sqmm"), 1)

    class Chain:
        def __init__(self, e, name):
            self.e, self.s, self.n = e, sem(name), 0

        def __call__(self, ins):
            self.n += 1
            ins.then_inc(self.s, 1)
            self.e.wait_ge(self.s, self.n)

    def meet(e, pos, engines=2):
        n = pos.add(f"meet{engines}")
        e.drain().then_inc(sem(f"stage_end_{engines}"), 1)
        reach(e, f"stage_end_{engines}", engines * n)

    def rms_act(e, ch, tag, src, nk, width, n, scale_from_ready=None):
        for k in range(nk):
            if k >= 2:
                reach(e, f"{tag}_sqmm", k - 1)
            if scale_from_ready:
                scale_from_ready(k)
            e.activation(tmp[:, k % 2, 0:width], src(k), ACT.Square).then_inc(sem(f"{tag}_sq"), 1)
        reach(e, f"{tag}_sqmm", nk)
        e.activation(tmp[:, 2, 0:width], aux[:, 0:width], ACT.Sqrt, scale=1.0 / n,
                     bias=eps_col).then_inc(sem(f"{tag}_rt"), 1)

    def rms_pe(e, tag, nk, width):
        column_sums(e, tag, lambda k: tmp[:, k % 2], nk, width)

    def rms_dve(e, ch, tag, width):
        reach(e, f"{tag}_rt", 1)
        ch(e.reciprocal(tmp[:, 3, 0:width], tmp[:, 2, 0:width]))

    def norm_act(e, ch, tag, nk, width, hi, scale, bias, func=ACT.Identity):
        for k in range(nk):
            t = tmp[:, k % 2, 0:width]
            reach(e, f"{tag}_nm", k + 1)
            e.activation(t, t, func, scale=scale(k), bias=bias(k) if bias else 0.0).then_inc(sem(f"{tag}_af"), 1)
            reach(e, f"{tag}_af", k + 1)
            copy(e, hi[:, k, 0:width], t).then_inc(sem(f"{tag}_hi"), 1)

    def norm_dve(e, ch, tag, nk, width, src, hi, lo):
        def low(k):
            reach(e, f"{tag}_hi", k + 1)
            e.tensor_tensor(lo[:, k, 0:width], tmp[:, k % 2, 0:width], hi[:, k, 0:width].bitcast(F32),
                            ALU.subtract).then_inc(sem(f"{tag}_lo"), 1)

        for k in range(nk):
            if k >= 2:
                reach(e, f"{tag}_lo", k - 1)
            e.tensor_tensor(tmp[:, k % 2, 0:width], src(k), tmp[:, 3, 0:width], ALU.mult).then_inc(sem(f"{tag}_nm"), 1)
            if k:
                low(k - 1)
        low(nk - 1)

    def split_act(e, tag, k, dst, src):
        copy(e, dst, src).then_inc(sem(f"{tag}_hi"), 1)

    N_ADA = 12

    def ada_sp(e, pos):
        for g in range(N_ADA):
            if g >= 2:
                reach(e, "ada_mm", g - 1)
            e.dma_start(ada_buf[:, g % 2], w_ada[g]).then_inc(sem(f"ada_ld{g % 2}"), 16)

    def ada_pe(e, pos):
        def turn(g):
            reach(e, "ada_row", g + 1)
            for j in range(4):
                m = 4 * g + j
                last = e.transpose(aux[:, 2 * m:2 * m + 2], ada_row[0:2, g % 2, j * P:(j + 1) * P], ident[0:2, 0:2])
            last.then_inc(sem("ada_tr"), 1)

        reach(e, "silu_c", 1)
        for g in range(N_ADA):
            use = pos.next_use()
            wait_region(e, use)
            reach(e, f"ada_ld{g % 2}", 16 * (g // 2 + 1))
            for k in range(KD):
                last = e.matmul(region[0:2, use % 2, 0:HALF], silu_c[:, 2 * k:2 * k + 2], ada_buf[:, g % 2, k],
                                start=(k == 0), stop=(k == KD - 1))
            last.then_inc(sem("ada_mm"), 1)
            if g:
                turn(g - 1)
        turn(N_ADA - 1)

    def ada_act(e, pos, ch):
        reach(e, "small_ld", 16)
        e.activation(silu_c, sp_("c", 16), ACT.Silu).then_inc(sem("silu_c"), 1)
        for g in range(N_ADA):
            use = pos.next_use()
            reach(e, "ada_mm", g + 1)
            if g >= 2:
                reach(e, "ada_tr", g - 1)
            copy(e, ada_row[0:2, g % 2], region[0:2, use % 2, 0:HALF]).then_inc(free[use % 2], 1)
            e.wait_ge(free[use % 2], use // 2 + 1)
            e.sem_inc(sem("ada_row"), 1)

    def ada_dve(e, pos, ch):
        for _ in range(N_ADA):
            pos.next_use()
        reach(e, "small_ld", 16)
        ch(e.memset(eps_col, EPS))
        ch(e.tensor_scalar(qh_s, sp_("qh"), QK ** -0.5, None, ALU.mult))
        ch(e.tensor_scalar(mq_s, sp_("mq"), P ** -0.5, None, ALU.mult))
        reach(e, "ada_tr", N_ADA)
        both = aux[:, 0:96].rearrange("p (m two) -> p m two", two=2)
        ch(e.tensor_tensor(mod_x, both[:, :, 0], sp_("b_ada", 48), ALU.add))
        ch(e.tensor_tensor(mod_c, both[:, 0:16, 1], sp_("b_ada", 16), ALU.add))
        ch(e.scalar_tensor_tensor(out=a1, in0=mod_x[:, 8:16], scalar=1.0, in1=sp_("norm1", 8), op0=ALU.add, op1=ALU.mult))
        ch(e.scalar_tensor_tensor(out=a1c, in0=mod_c[:, 8:16], scalar=1.0, in1=sp_("norm1", 8), op0=ALU.add, op1=ALU.mult))
        ch(e.scalar_tensor_tensor(out=a2, in0=mod_x[:, 32:40], scalar=1.0, in1=sp_("norm2", 8), op0=ALU.add, op1=ALU.mult))

    SWAP = [(i + 16) % 32 for i in range(32)]

    def proj1_pe(e, pos):
        for j in range(4):
            use = pos.next_use()
            project(e, use, UNIT0["q"] + j, h_hi, h_lo, KD,
                    wait_k=(lambda k: reach(e, "n1_lo", k + 1)) if j == 0 else None).then_inc(unit_done, 1)
        for j in range(4):
            use = pos.next_use()
            project(e, use, UNIT0["k"] + j, h_hi, h_lo, KD).then_inc(sem("k_part"), 1)
            use = pos.next_use()
            project(e, use, UNIT0["k"] + j, hc_hi, hc_lo, KD, width=CTX,
                    wait_k=(lambda k: reach(e, "nc_lo", k + 1)) if j == 0 else None).then_inc(unit_done, 1)
        for p in range(2):
            e.wait_ge(unit_split, UNIT0["v"] + 2 * p + 2)
            pair = lambda w, k: w[:, 0:2, k * P:(k + 1) * P]
            for g in range(2):
                use = pos.next_use()
                project_tokens(e, use, None, h_hi, h_lo, KD, range(4 * g, 4 * g + 4), 256, pair).then_inc(sem("v_part"), 1)
            use = pos.next_use()
            project_tokens(e, use, None, hc_hi, hc_lo, KD, range(2), 256, pair).then_inc(unit_done, 2)
        for j in range(8):
            use = pos.next_use()
            project(e, use, UNIT0["u"] + j, h_hi, h_lo, KD).then_inc(unit_done, 1)

    def proj1_act(e, pos, ch):
        for j in range(4):
            use = pos.next_use()
            e.wait_ge(unit_done, UNIT0["q"] + j + 1)
            e.activation(q_t[:, j], region[:, use % 2], ACT.Copy, scale=HD ** -0.5).then_inc(free[use % 2], 1)
        for j in range(4):
            use = pos.next_use()
            reach(e, "k_part", j + 1)
            if j >= 2:
                reach(e, "k_rot", j - 1)
            copy(e, tmp[:, 2 + j % 2], region[:, use % 2]).then_inc(free[use % 2], 1)
            use = pos.next_use()
            e.wait_ge(unit_done, UNIT0["k"] + j + 1)
            copy(e, k_ctx[:, j], region[:, use % 2, 0:CTX]).then_inc(free[use % 2], 1)
        for p in range(2):
            cols = slice(256 * p, 256 * p + 256)
            for g in range(2):
                use = pos.next_use()
                reach(e, "v_part", 2 * p + g + 1)
                copy(e, v_tok[:, 4 * g:4 * g + 4, cols],
                     region[:, use % 2].rearrange("p (t c) -> p t c", c=256)).then_inc(free[use % 2], 1)
            use = pos.next_use()
            e.wait_ge(unit_done, UNIT0["v"] + 2 * p + 2)
            copy(e, v_ctx[:, :, cols],
                 region[:, use % 2, 0:512].rearrange("p (t c) -> p t c", c=256)).then_inc(free[use % 2], 1)
        reach(e, "k_rot", 4)
        for j in range(4):
            use = pos.next_use()
            e.wait_ge(unit_done, UNIT0["u"] + 2 * j + 1)
            if j >= 2:
                reach(e, "glu", j - 1)
            copy(e, tmp[:, j % 2], region[:, use % 2]).then_inc(free[use % 2], 1)
            use = pos.next_use()
            e.wait_ge(unit_done, UNIT0["u"] + 2 * j + 2)
            e.activation(tmp[:, 2 + j % 2], region[:, use % 2], ACT.Sigmoid).then_inc(free[use % 2], 1)

    def proj1_dve(e, pos, ch):
        def rotate(dst, src, done=None):
            ch(e.stream_shuffle(tmp[:, 0], src, SWAP))
            ch(e.tensor_tensor(tmp[:, 0], tmp[:, 0], sin1[:], ALU.mult))
            ch(e.tensor_tensor(dst, src, cos1[:], ALU.mult))
            last = e.tensor_tensor(dst, dst, tmp[:, 0], ALU.add)
            if done:
                last.then_inc(done, 1)
            else:
                ch(last)

        reach(e, "rope1_ld", 32)
        for j in range(4):
            use = pos.next_use()
            e.wait_ge(free[use % 2], use // 2 + 1)
            rotate(q_rot[:, j], q_t[:, j])
        for j in range(4):
            use = pos.next_use()
            pos.next_use()
            e.wait_ge(free[use % 2], use // 2 + 1)
            rotate(k_rot[:, j], tmp[:, 2 + j % 2], sem("k_rot"))
            reach(e, "k_rot", j + 1)
        last_v = 0
        for _ in range(6):
            last_v = pos.next_use()
        e.wait_ge(unit_done, UNIT0["u"] + 1)
        for j in range(4):
            ch(e.memset(glu[:, j, 0:PAD], 0.0))
            ch(e.memset(glu[:, j, PAD + T:], 0.0))
        for j in range(4):
            pos.next_use()
            use = pos.next_use()
            e.wait_ge(free[use % 2], use // 2 + 1)
            e.tensor_tensor(glu[:, j, PAD:PAD + T], tmp[:, j % 2], tmp[:, 2 + j % 2], ALU.mult).then_inc(sem("glu"), 1)
        reach(e, "glu", 4)

    class Attention:

        def __init__(self, tag, heads, nkeys, out_cols, score, v_of, store, front=None, bias=None, extra=None):
            self.tag, self.n, self.nkeys, self.nkt = tag, heads * TT, nkeys, nkeys // P
            self.score, self.v_of, self.store, self.bias, self.extra = score, v_of, store, bias, extra
            self.split = min(self.nkt, 4)
            self.out_cols = out_cols
            self.before = front

        def s(self, what):
            return sem(f"{self.tag}_{what}")

        def pe(self, e, pos):
            uses = {}

            def scores(i):
                use = uses[i] = pos.next_use()
                wait_region(e, use)
                if self.before:
                    self.before(e, i)
                self.score(e, i, region[:, use % 2]).then_inc(self.s("scored"), 1)

            def turn(i):
                reach(e, self.tag + "_" + "prob", i + 1)
                if i:
                    reach(e, self.tag + "_" + "pt_a", i)
                    if self.nkt > self.split:
                        reach(e, self.tag + "_" + "pt_b", i)
                for b in range(self.nkt):
                    last = e.transpose(aux[:, b * P:(b + 1) * P], prob[:, i % 2, b * P:(b + 1) * P], ident[:])
                last.then_inc(self.s("turned"), 1)

            def values(i):
                reach(e, self.tag + "_" + "pt_a", i + 1)
                if self.nkt > self.split:
                    reach(e, self.tag + "_" + "pt_b", i + 1)
                if i >= 2:
                    reach(e, self.tag + "_" + "stored", i - 1)
                for b in range(self.nkt):
                    last = e.matmul(pv[:, i % 2, 0:P], prob_t[:, i % 2, b], self.v_of(i, b),
                                    start=(b == 0), stop=(b == self.nkt - 1))
                last.then_inc(self.s("summed"), 1)

            for i in range(self.n + 2):
                if i < self.n:
                    scores(i)
                if 1 <= i <= self.n:
                    turn(i - 1)
                if i >= 2:
                    values(i - 2)

        def act(self, e, pos, ch):
            def exps(i):
                use = pos.next_use()
                src = prob[:, i % 2, 0:self.nkeys] if self.bias else region[:, use % 2, 0:self.nkeys]
                reach(e, self.tag + "_" + "maxed", i + 1)
                if i >= 2:
                    reach(e, self.tag + "_" + "turned", i - 1)
                    reach(e, self.tag + "_" + "stored", i - 1)
                e.activation(prob[:, i % 2, 0:self.nkeys], src, ACT.Exp, bias=neg_max[:, i % 2:i % 2 + 1],
                             accum_out=row_sum[:, i % 2:i % 2 + 1]).then_inc(self.s("prob"), 1)
                if not self.bias:
                    reach(e, self.tag + "_" + "prob", i + 1)
                    e.sem_inc(free[use % 2], 1)

            def move(i):
                reach(e, self.tag + "_" + "turned", i + 1)
                if i >= 2:
                    reach(e, self.tag + "_" + "summed", i - 1)
                copy(e, prob_t[:, i % 2, 0:self.split], aux[:, 0:self.split * P].rearrange("p (b k) -> p b k", k=P))\
                    .then_inc(self.s("pt_a"), 1)

            for i in range(self.n + 1):
                if i < self.n:
                    exps(i)
                if i:
                    move(i - 1)

        def dve(self, e, pos, ch):
            def maxes(i):
                use = pos.next_use()
                reach(e, self.tag + "_" + "scored", i + 1)
                if i >= 2:
                    reach(e, self.tag + "_" + "prob", i - 1)
                if self.bias:
                    if i >= 2:
                        reach(e, self.tag + "_" + "turned", i - 1)
                    reach(e, self.tag + "_" + "bias", self.bias_count(i))
                    e.tensor_tensor_reduce(prob[:, i % 2, 0:self.nkeys], region[:, use % 2, 0:self.nkeys], self.bias(i),
                                           1.0, -3.0e38, ALU.add, ALU.max, row_max[:, i % 2:i % 2 + 1])\
                        .then_inc(free[use % 2], 1)
                    e.wait_ge(free[use % 2], use // 2 + 1)
                    e.tensor_scalar(neg_max[:, i % 2:i % 2 + 1], row_max[:, i % 2:i % 2 + 1], -1.0, None,
                                    ALU.mult).then_inc(self.s("maxed"), 1)
                else:
                    e.tensor_reduce(neg_max[:, i % 2:i % 2 + 1], region[:, use % 2, 0:self.nkeys], AX, ALU.max,
                                    negate=True).then_inc(self.s("maxed"), 1)

            def move(i):
                if self.nkt > self.split:
                    reach(e, self.tag + "_" + "turned", i + 1)
                    if i >= 2:
                        reach(e, self.tag + "_" + "summed", i - 1)
                    e.tensor_copy(prob_t[:, i % 2, self.split:self.nkt],
                                  aux[:, self.split * P:self.nkt * P].rearrange("p (b k) -> p b k", k=P))\
                        .then_inc(self.s("pt_b"), 1)

            def store(i):
                reach(e, self.tag + "_" + "summed", i + 1)
                ch(e.reciprocal(inv_sum[:, i % 2:i % 2 + 1], row_sum[:, i % 2:i % 2 + 1]))
                dst, cols = self.store(i)
                e.tensor_scalar(dst, pv[:, i % 2, cols], inv_sum[:, i % 2:i % 2 + 1], None, ALU.mult)\
                    .then_inc(self.s("stored"), 1)

            for i in range(self.n + 2):
                if i < self.n:
                    maxes(i)
                if 1 <= i <= self.n:
                    move(i - 1)
                if i >= 2:
                    store(i - 2)
                if self.extra:
                    self.extra(e, ch, i)
            reach(e, self.tag + "_" + "stored", self.n)

    def first_key_row(t):
        return 2 * t + SHIFT[VARIANT[t]]

    def na_score(e, i, dst):
        h, t = divmod(i, TT)
        rows = slice(64 * (h % 2), 64 * (h % 2) + 64)
        j, qs, k0 = h // 2, slice(t * P, t * P + P), first_key_row(t) * W_GRID
        e.matmul(dst[:, 0:512], q_rot[rows, j, qs], k_rot[rows, j, k0:k0 + 512], start=True, stop=True)
        e.matmul(dst[:, 512:KEYS], q_rot[rows, j, qs], k_rot[rows, j, k0 + 512:k0 + KEYS], start=True, stop=True)
        return e.matmul(dst[:, KEYS:KEYS + CTX], q_t[rows, j, qs], k_ctx[rows, j], start=True, stop=True)

    def na_v(i, b):
        h, t = divmod(i, TT)
        cols = slice(P * (h // 2), P * (h // 2) + P)
        if b < KEYS // P:
            return v_tok[:, first_key_row(t) // 2 + b, cols]
        return v_ctx[:, b - KEYS // P, cols]

    def head_store(buf):
        def store(i):
            h, t = divmod(i, TT)
            return buf[:, t, h * 64:h * 64 + 64], slice(64 * (h % 2), 64 * (h % 2) + 64)
        return store

    def conv_tap(e, ch, n):
        j, k = divmod(n, TAPS)
        src, w = glu[:, j, k:k + T], sp_("dww", 1, j * TAPS + k)
        if k == 0:
            ch(e.tensor_scalar(conv[:, j], src, w, sp_("dwb", 1, j), ALU.mult, ALU.add))
        else:
            ch(e.scalar_tensor_tensor(out=conv[:, j], in0=src, scalar=w, in1=conv[:, j], op0=ALU.mult, op1=ALU.add))

    def conv_extra(e, ch, i):
        for n in range(2 * i, min(2 * i + 2, 4 * TAPS)):
            conv_tap(e, ch, n)

    na = Attention("na", HEADS, KEYS + CTX, HALF, na_score, na_v, head_store(o_tok),
                   bias=lambda i: bias_t[:, VARIANT[i % TT]], extra=conv_extra)
    na.bias_count = lambda i: 5 * (i // TT) + VARIANT[i % TT] + 1

    def bias_pool(e, pos):
        e.wait_ge(unit_done, UNIT0["u"] + 8)

        def load_toep(h):
            for a in range(2):
                start = (h * 19 + 1 - a) * TABLE * W_GRID + W_GRID - 1
                src = bass.AP(rpb_pad.tensor, start, [[TABLE - 1, W_GRID], [TABLE * W_GRID, 18], [1, W_GRID]])
                e.dma_start(toep[h % 2][a * 64:a * 64 + 64], src).then_inc(sem(f"toep_ld{h % 2}"), 16)

        load_toep(0)
        e.dma_start(mask_t[:].rearrange("p v k -> p (v k)"), mask).then_inc(sem("mask_ld"), 16)
        load_toep(1)
        for v in range(5):
            e.memset(bias_t[:, v, KEYS:], 0.0).then_inc(sem("bias_tail"), 1)
        reach(e, "bias_tail", 5)
        reach(e, "mask_ld", 16)
        for h in range(HEADS):
            reach(e, f"toep_ld{h % 2}", 32 * (h // 2 + 1))
            for v in range(5):
                if h:
                    last_tile = max(t for t in range(TT) if VARIANT[t] == v)
                    reach(e, "na_maxed", TT * (h - 1) + last_tile + 1)
                r0 = SHIFT[v] + 8
                e.tensor_tensor(bias_t[:, v, 0:KEYS].rearrange("p (r c) -> p r c", c=W_GRID),
                                toep[h % 2][:, r0:r0 + 10],
                                mask_t[:, v].rearrange("p (r c) -> p r c", c=W_GRID), ALU.add)\
                    .then_inc(sem("na_bias"), 1)
            if h + 2 < HEADS:
                reach(e, "na_bias", 5 * (h + 1))
                load_toep(h + 2)

    def turn_back_pe(e, pos, tag, src):
        for j in range(4):
            use = pos.next_use()
            wait_region(e, use)
            for t in range(TT):
                last = e.transpose(region[:, use % 2, t * P:(t + 1) * P], src[:, t, j * P:(j + 1) * P], ident[:])
            last.then_inc(sem(f"{tag}_tb"), 1)

    def turn_back_act(e, pos, tag, hi):
        for j in range(4):
            use = pos.next_use()
            reach(e, f"{tag}_tb", j + 1)
            copy(e, hi[:, j], region[:, use % 2]).then_inc(sem(f"{tag}_tbhi"), 1)

    def turn_back_dve(e, pos, tag, hi, lo):
        for j in range(4):
            use = pos.next_use()
            reach(e, f"{tag}_tbhi", j + 1)
            e.tensor_tensor(lo[:, j], region[:, use % 2], hi[:, j].bitcast(F32), ALU.subtract).then_inc(free[use % 2], 1)

    def ln_pe(e, pos):
        for j in range(4):
            for lo in range(0, T, HALF):
                last = e.matmul(aux[:, lo:lo + HALF], ones[:], conv[:, j, lo:lo + HALF], start=(j == 0), stop=(j == 3))
        last.then_inc(sem("ln_sum"), 1)
        rms_pe(e, "lnv", 4, T)

    def ln_dve(e, pos, ch):
        reach(e, "ln_sum", 1)
        for j in range(4):
            e.scalar_tensor_tensor(out=conv[:, j], in0=aux[:], scalar=-1.0 / 512, in1=conv[:, j],
                                   op0=ALU.mult, op1=ALU.add).then_inc(sem("ln_dev"), 1)
        rms_dve(e, ch, "lnv", T)
        norm_dve(e, ch, "lnn", 4, T, lambda k: conv[:, k], mix_hi[:, 4:8], mix_lo[:, 4:8])

    def ln_act(e, pos, ch):
        rms_act(e, ch, "lnv", lambda k: conv[:, k], 4, T, 512,
                scale_from_ready=lambda k: reach(e, "ln_dev", 4 if k == 0 else k + 1))
        norm_act(e, ch, "lnn", 4, T, mix_hi[:, 4:8], lambda k: sp_("ln_g", 1, k), lambda k: sp_("ln_b", 1, k), ACT.Silu)

    def out1_pe(e, pos):
        for j in range(8):
            use = pos.next_use()
            project(e, use, UNIT0["out1"] + j, mix_hi, mix_lo, KD).then_inc(unit_done, 1)

    def out1_dve(e, pos, ch):
        reach(e, "x_again", 16)
        for j in range(8):
            use = pos.next_use()
            e.wait_ge(unit_done, UNIT0["out1"] + j + 1)
            e.scalar_tensor_tensor(out=x1[:, j], in0=region[:, use % 2], scalar=mod_x[:, 16 + j:17 + j],
                                   in1=x1[:, j], op0=ALU.mult, op1=ALU.add).then_inc(free[use % 2], 1)

    def mlp_pe(e, pos):
        u0, c0 = UNIT0["mlp"], pos.use
        assert c0 % 2 == 0 and u0 % 2 == 0
        with e.Fori(0, FF_GROUPS) as g:
            def unit(n, xh, xl, wait_k=None):
                r = s = n % 2
                e.wait_ge(unit_split, g * 16 + (u0 + n + 1))
                e.wait_ge(free[r], g * 8 + (c0 + n) // 2)
                for lo in (0, HALF):
                    for k in range(KD):
                        if wait_k and lo == 0:
                            wait_k(k)
                        w = slice(k * P, k * P + P)
                        last = mm3(e, region[:, r, lo:lo + HALF], w_hi[:, s, w], w_lo[:, s, w],
                                   xh[:, k, lo:lo + HALF], xl[:, k, lo:lo + HALF], k == 0, k == KD - 1)
                last.then_inc(unit_done, 1)
            for f in range(KD):
                unit(f, h2_hi, h2_lo)
            for d in range(KD):
                unit(KD + d, ff_hi, ff_lo, (lambda k: reach(e, "ff_lo", g * 8 + (k + 1))) if d == 0 else None)
        pos.use += 16 * FF_GROUPS

    def mlp_act(e, pos, ch):
        u0 = UNIT0["mlp"]
        with e.Fori(0, FF_GROUPS) as g:
            def hi(f):
                reach(e, "ff_sq", g * 8 + (f + 1))
                copy(e, ff_hi[:, f], tmp[:, 2 + f % 2]).then_inc(sem("ff_hi"), 1)

            for f in range(KD):
                e.wait_ge(unit_done, g * 16 + (u0 + f + 1))
                if f >= 2:
                    reach(e, "ff_sq", g * 8 + (f - 1))
                e.activation(tmp[:, f % 2], region[:, f % 2], ACT.Relu).then_inc(free[f % 2], 1)
                if f:
                    hi(f - 1)
            hi(KD - 1)
        pos.use += 16 * FF_GROUPS

    def mlp_dve(e, pos, ch):
        u0, c0 = UNIT0["mlp"], pos.use
        with e.Fori(0, FF_GROUPS) as g:
            def low(f):
                reach(e, "ff_hi", g * 8 + (f + 1))
                e.tensor_tensor(ff_lo[:, f], tmp[:, 2 + f % 2], ff_hi[:, f].bitcast(F32), ALU.subtract)\
                    .then_inc(sem("ff_lo"), 1)

            for f in range(KD):
                e.wait_ge(free[f % 2], g * 8 + (c0 + f) // 2 + 1)
                if f >= 2:
                    reach(e, "ff_lo", g * 8 + (f - 1))
                e.tensor_tensor(tmp[:, 2 + f % 2], tmp[:, f % 2], tmp[:, f % 2], ALU.mult).then_inc(sem("ff_sq"), 1)
                if f:
                    low(f - 1)
            low(KD - 1)
            for d in range(KD):
                e.wait_ge(unit_done, g * 16 + (u0 + KD + d + 1))
                e.scalar_tensor_tensor(out=x1[:, d], in0=region[:, d % 2], scalar=mod_x[:, 40 + d:41 + d],
                                       in1=x1[:, d], op0=ALU.mult, op1=ALU.add).then_inc(free[d % 2], 1)
        pos.use += 16 * FF_GROUPS

    def final_dve(e, pos, ch):
        rms_dve(e, ch, "nf", T)
        for k in range(KD):
            e.scalar_tensor_tensor(out=x1[:, k], in0=x1[:, k], scalar=sp_("final", 1, k), in1=tmp[:, 3],
                                   op0=ALU.mult, op1=ALU.mult).then_inc(sem("x2_ready"), 1)
        reach(e, "x2_ready", KD)

    def lat_pe(e, pos):
        for j in range(6):
            use = pos.next_use()
            project(e, use, UNIT0["lat"] + j, h2_hi, h2_lo, KD, m=QK if j == 5 else P, step=QK if j == 5 else P)\
                .then_inc(unit_done, 1)

    def lat_act(e, pos, ch):
        for j in range(6):
            use = pos.next_use()
            e.wait_ge(unit_done, UNIT0["lat"] + j + 1)
            if j < 3:
                last = copy(e, q_lat[:, j], region[:, use % 2])
            elif j < 5:
                last = copy(e, kv_lat[:, j - 3], region[:, use % 2])
            else:
                last = copy(e, k_pe[NOPE:QK], region[NOPE:QK, use % 2])
            last.then_inc(free[use % 2], 1)

    def tables_dve(e, pos, ch):
        r = slice(NOPE, QK)
        reach(e, "pos_ld", 16)
        ch(e.tensor_copy(tmp[r, 0], pos_i[r]))
        ch(e.tensor_scalar(tmp[r, 0], tmp[r, 0], par[r, SMALL["invf"]:SMALL["invf"] + 1], None, ALU.mult))
        c1 = 6.28125
        c2 = float(np.float32(np.round((TWO_PI - c1) * 2 ** 21) / 2 ** 21))
        c3 = float(TWO_PI - c1 - c2)
        magic = 1.5 * 2 ** 23
        for which, (quarter, shift) in enumerate([(0.0, 0.0), (0.25, np.pi / 2)]):
            ch(e.tensor_scalar(tmp[r, 1], tmp[r, 0], 1.0 / TWO_PI, quarter, ALU.mult, ALU.add))
            ch(e.tensor_scalar(tmp[r, 1], tmp[r, 1], magic, magic, ALU.add, ALU.subtract))
            ch(e.scalar_tensor_tensor(out=tmp[r, 2], in0=tmp[r, 1], scalar=-c1, in1=tmp[r, 0], op0=ALU.mult, op1=ALU.add))
            ch(e.scalar_tensor_tensor(out=tmp[r, 2], in0=tmp[r, 1], scalar=-c2, in1=tmp[r, 2], op0=ALU.mult, op1=ALU.add))
            ch(e.scalar_tensor_tensor(out=tmp[r, 2], in0=tmp[r, 1], scalar=-c3, in1=tmp[r, 2], op0=ALU.mult, op1=ALU.add))
            ch(e.tensor_scalar(tmp[r, 2], tmp[r, 2], shift, 3.1415925, ALU.add, ALU.min))
            e.tensor_scalar(tmp[r, 2], tmp[r, 2], -3.1415925, None, ALU.max).then_inc(sem("angle"), 1)
            reach(e, "table", which + 1)
        ch(e.tensor_scalar(sin2[r], sin2[r], par[r, SMALL["sign"]:SMALL["sign"] + 1], None, ALU.mult))

    def tables_act(e, pos, ch):
        r = slice(NOPE, QK)
        for which, dst in enumerate((sin2, cos2)):
            reach(e, "angle", which + 1)
            e.activation(dst[r], tmp[r, 2], ACT.Sin).then_inc(sem("table"), 1)

    def heads_pe(e, pos, tag, first_unit, xh, xl, nk, per_unit):
        def sums(h):
            reach(e, f"{tag}_sq", h + 1)
            if h:
                reach(e, f"{tag}_rt", h)
            for lo in (0, HALF):
                last = e.matmul(aux[0:QK, lo:lo + HALF], ones[0:QK, 0:QK], tmp[0:QK, 2, lo:lo + HALF], start=True, stop=True)
            last.then_inc(sem(f"{tag}_ss"), 1)

        for h in range(HEADS):
            use = pos.next_use()
            last = project(e, use, UNIT0[first_unit] + h // per_unit, xh, xl, nk, m=QK,
                           off=(h % per_unit) * nk * QK, step=QK)
            if h % per_unit == per_unit - 1 or h == HEADS - 1:
                last.then_inc(unit_done, 1)
            else:
                last.then_inc(sem(f"{tag}_part"), 1)
            if h:
                sums(h - 1)
        sums(HEADS - 1)

    def heads_act(e, pos, ch, tag, first_unit, per_unit, rows):
        parts = 0
        for h in range(HEADS):
            use = pos.next_use()
            if h % per_unit == per_unit - 1 or h == HEADS - 1:
                e.wait_ge(unit_done, UNIT0[first_unit] + h // per_unit + 1)
            else:
                parts += 1
                reach(e, f"{tag}_part", parts)
            if h >= 2:
                reach(e, f"{tag}_sc", h - 1)
            copy(e, tmp[0:rows, h % 2], region[0:rows, use % 2]).then_inc(free[use % 2], 1)
            e.wait_ge(free[use % 2], use // 2 + 1)
            if h:
                reach(e, f"{tag}_ss", h)
            e.activation(tmp[0:QK, 2], tmp[0:QK, h % 2], ACT.Square).then_inc(sem(f"{tag}_sq"), 1)
            reach(e, f"{tag}_ss", h + 1)
            if h:
                reach(e, f"{tag}_sc", h)
            e.activation(tmp[0:QK, 3], aux[0:QK], ACT.Sqrt, scale=1.0 / QK, bias=eps_col[0:QK]).then_inc(sem(f"{tag}_rt"), 1)

    def heads_dve(e, pos, ch, tag, dst, gain, rot_tmp):
        r = slice(NOPE, QK)
        for h in range(HEADS):
            pos.next_use()
            reach(e, f"{tag}_rt", h + 1)
            ch(e.reciprocal(tmp[0:QK, 3], tmp[0:QK, 3]))
            e.scalar_tensor_tensor(out=dst[0:QK, h], in0=tmp[0:QK, h % 2], scalar=gain[0:QK], in1=tmp[0:QK, 3],
                                   op0=ALU.mult, op1=ALU.mult).then_inc(sem(f"{tag}_sc"), 1)
            reach(e, f"{tag}_sc", h + 1)
            ch(e.stream_shuffle(rot_tmp[r], dst[r, h], SWAP))
            ch(e.tensor_tensor(rot_tmp[r], rot_tmp[r], sin2[r], ALU.mult))
            ch(e.tensor_tensor(dst[r, h], dst[r, h], cos2[r], ALU.mult))
            ch(e.tensor_tensor(dst[r, h], dst[r, h], rot_tmp[r], ALU.add))

    rot_q = place("rot_q", [T], 64)
    rot_k = place("rot_k", [T], 132)

    def uv_pe(e, pos):
        e.wait_ge(unit_split, UNIT0["uv"] + 1)
        s = UNIT0["uv"] % 2
        for g in range(4):
            use = pos.next_use()
            last = project_tokens(e, use, None, kvl_hi, kvl_lo, NKVL, range(2 * g, 2 * g + 2), HALF,
                                  lambda w, k: w[:, s, k * HALF:(k + 1) * HALF])
            last.then_inc(unit_done if g == 3 else sem("uv_part"), 1)

    def uv_act(e, pos, ch):
        for g in range(4):
            use = pos.next_use()
            if g < 3:
                reach(e, "uv_part", g + 1)
            else:
                e.wait_ge(unit_done, UNIT0["uv"] + 1)
            copy(e, v2[:, 2 * g:2 * g + 2], region[:, use % 2].rearrange("p (t c) -> p t c", c=HALF))\
                .then_inc(free[use % 2], 1)

    def mla_score(e, i, dst):
        h, t = divmod(i, TT)
        for lo in (0, HALF):
            last = e.matmul(dst[:, lo:lo + HALF], q_h[0:QK, h, t * P:(t + 1) * P], k_h[0:QK, h, lo:lo + HALF],
                            start=True, stop=True)
        return last

    mla = Attention("mla", HEADS, T, HALF, mla_score,
                    lambda i, b: v2[:, b, P * (i // TT // 2):P * (i // TT // 2) + P], head_store(o_tok2))

    def gate_pe(e, pos, tag, units, src):
        for j in range(4):
            if j:
                reach(e, f"{tag}_gated", j)
            for t in range(TT):
                last = e.transpose(aux[:, t * P:(t + 1) * P], src[:, t, j * P:(j + 1) * P], ident[:])
            last.then_inc(sem(f"{tag}_tb"), 1)
            use = pos.next_use()
            project(e, use, UNIT0[units] + j, h2_hi, h2_lo, KD).then_inc(unit_done, 1)

    def gate_act(e, pos, ch, tag, units):
        for j in range(4):
            use = pos.next_use()
            e.wait_ge(unit_done, UNIT0[units] + j + 1)
            if j >= 2:
                reach(e, f"{tag}_gated", j - 1)
            e.activation(tmp[:, j % 2], region[:, use % 2], ACT.Silu).then_inc(free[use % 2], 1)
            reach(e, f"{tag}_gated", j + 1)
            copy(e, o_hi[:, j], tmp[:, 2 + j % 2]).then_inc(sem(f"{tag}_hi"), 1)

    def gate_dve(e, pos, ch, tag):
        for j in range(4):
            use = pos.next_use()
            e.wait_ge(free[use % 2], use // 2 + 1)
            reach(e, f"{tag}_tb", j + 1)
            e.tensor_tensor(tmp[:, 2 + j % 2], aux[:], tmp[:, j % 2], ALU.mult).then_inc(sem(f"{tag}_gated"), 1)
            reach(e, f"{tag}_hi", j + 1)
            e.tensor_tensor(o_lo[:, j], tmp[:, 2 + j % 2], o_hi[:, j].bitcast(F32), ALU.subtract).then_inc(sem(f"{tag}_lo"), 1)
        reach(e, f"{tag}_lo", 4)

    def branch_pe(e, pos, b, lo_tag):
        u0 = UNIT0[f"br{b}"]
        for p in range(4):
            for dd in range(2):
                use = pos.next_use()
                project(e, use, u0 + 3 * p + dd, h2_hi, h2_lo, KD).then_inc(unit_done, 1)
            for dd in range(2):
                use = pos.next_use()
                last = project(e, use, u0 + 3 * p + 2, o_hi, o_lo, 4, off=dd * HALF,
                               wait_k=(lambda k: reach(e, lo_tag, k + 1)) if p == dd == 0 else None)
                last.then_inc(unit_done if dd else sem(f"br{b}_part"), 1)

    def branch_act(e, pos, ch, b):
        u0 = UNIT0[f"br{b}"]
        for p in range(4):
            for dd in range(2):
                use = pos.next_use()
                e.wait_ge(unit_done, u0 + 3 * p + dd + 1)
                if p:
                    reach(e, f"br{b}_used", 2 * (p - 1) + dd + 1)
                e.activation(tmp[:, dd], region[:, use % 2], ACT.Sigmoid, bias=sp_("b_gate", 1, 8 * b + 2 * p + dd))\
                    .then_inc(free[use % 2], 1)
            pos.next_use(), pos.next_use()

    def branch_dve(e, pos, ch, b):
        u0 = UNIT0[f"br{b}"]
        for p in range(4):
            gates = [pos.next_use(), pos.next_use()]
            for dd in range(2):
                use = pos.next_use()
                e.wait_ge(free[gates[dd] % 2], gates[dd] // 2 + 1)
                if dd:
                    e.wait_ge(unit_done, u0 + 3 * p + 3)
                else:
                    reach(e, f"br{b}_part", p + 1)
                d = 2 * p + dd
                dst = tmp[:, 2 + dd] if b else y[:, d]
                if b and p:
                    reach(e, f"br{b}_used", 2 * (p - 1) + dd + 1)
                e.tensor_tensor(dst, region[:, use % 2], tmp[:, dd], ALU.mult).then_inc(free[use % 2], 1)
                e.wait_ge(free[use % 2], use // 2 + 1)
                if b:
                    e.tensor_tensor(y[:, d], y[:, d], dst, ALU.add).then_inc(sem(f"br{b}_used"), 1)
                else:
                    e.sem_inc(sem(f"br{b}_used"), 1)
        if b:
            reach(e, f"br{b}_used", 8)

    def cv_pe(e, pos):
        for j in range(16):
            use = pos.next_use()
            project(e, use, UNIT0["cv"] + j, h2_hi, h2_lo, KD).then_inc(unit_done, 1)

    def cv_act(e, pos, ch):
        for j in range(4):
            u = UNIT0["cv"] + 4 * j
            use = pos.next_use()
            e.wait_ge(unit_done, u + 1)
            if j:
                reach(e, "cv_z", j)
            copy(e, tmp[:, 0], region[:, use % 2]).then_inc(free[use % 2], 1)
            pos.next_use(), pos.next_use()
            use = pos.next_use()
            e.wait_ge(unit_done, u + 4)
            if j:
                reach(e, "cv_o", j)
            e.activation(tmp[:, 2], region[:, use % 2], ACT.Silu).then_inc(free[use % 2], 1)
            reach(e, "cv_o", j + 1)
            copy(e, o_hi[:, j], tmp[:, 3]).then_inc(sem("cv_hi"), 1)

    def cv_dve(e, pos, ch):
        ch(e.memset(z_pad[:, 0:1], 0.0))
        ch(e.memset(z_pad[:, T + 1:T + 2], 0.0))
        for j in range(4):
            u = UNIT0["cv"] + 4 * j
            w = lambda k: sp_("cw", 1, 3 * j + k)
            use = pos.next_use()
            e.wait_ge(free[use % 2], use // 2 + 1)
            use = pos.next_use()
            e.wait_ge(unit_done, u + 2)
            e.tensor_tensor(z_pad[:, 1:T + 1], region[:, use % 2], tmp[:, 0], ALU.mult).then_inc(free[use % 2], 1)
            e.wait_ge(free[use % 2], use // 2 + 1)
            e.sem_inc(sem("cv_z"), 1)
            ch(e.tensor_scalar(tmp[:, 1], z_pad[:, 0:T], w(0), sp_("cb", 1, j), ALU.mult, ALU.add))
            for k in (1, 2):
                ch(e.scalar_tensor_tensor(out=tmp[:, 1], in0=z_pad[:, k:k + T], scalar=w(k), in1=tmp[:, 1],
                                          op0=ALU.mult, op1=ALU.add))
            use = pos.next_use()
            e.wait_ge(unit_done, u + 3)
            e.tensor_tensor(tmp[:, 1], region[:, use % 2], tmp[:, 1], ALU.mult).then_inc(free[use % 2], 1)
            e.wait_ge(free[use % 2], use // 2 + 1)
            use = pos.next_use()
            e.wait_ge(free[use % 2], use // 2 + 1)
            if j:
                reach(e, "cv_lo", j)
            e.tensor_tensor(tmp[:, 3], tmp[:, 1], tmp[:, 2], ALU.mult).then_inc(sem("cv_o"), 1)
            reach(e, "cv_hi", j + 1)
            e.tensor_tensor(o_lo[:, j], tmp[:, 3], o_hi[:, j].bitcast(F32), ALU.subtract).then_inc(sem("cv_lo"), 1)
        reach(e, "cv_lo", 4)

    def mkv_pe(e, pos):
        def sums(h):
            reach(e, "mk_sq", h + 1)
            if h:
                reach(e, "mk_rt", h)
            e.matmul(aux[:, 0:CTX], ones[:], tmp[:, 2, 0:CTX], start=True, stop=True).then_inc(sem("mk_ss"), 1)

        for h in range(MH):
            use = pos.next_use()
            project(e, use, UNIT0["mkv"] + h, hm_hi, hm_lo, KD, width=CTX,
                    wait_k=(lambda k: reach(e, "nm_lo", k + 1)) if h == 0 else None).then_inc(unit_done, 1)
            if h:
                sums(h - 1)
        sums(MH - 1)
        for p in range(2):
            use = pos.next_use()
            u = UNIT0["mkv"] + 4 + 2 * p
            assert u % 2 == 0
            e.wait_ge(unit_split, u + 2)
            project_tokens(e, use, None, hm_hi, hm_lo, KD, range(2), 256,
                           lambda w, k: w[:, 0:2, k * P:(k + 1) * P]).then_inc(unit_done, 2)

    def head_norm_act(e, pos, tag, units, width):
        for h in range(MH):
            use = pos.next_use()
            e.wait_ge(unit_done, UNIT0[units] + h + 1)
            if h >= 2:
                reach(e, f"{tag}_sc", h - 1)
            copy(e, tmp[:, h % 2, 0:width], region[:, use % 2, 0:width]).then_inc(free[use % 2], 1)
            e.wait_ge(free[use % 2], use // 2 + 1)
            if h:
                reach(e, f"{tag}_ss", h)
            e.activation(tmp[:, 2, 0:width], tmp[:, h % 2, 0:width], ACT.Square).then_inc(sem(f"{tag}_sq"), 1)
            reach(e, f"{tag}_ss", h + 1)
            if h:
                reach(e, f"{tag}_sc", h)
            e.activation(tmp[:, 3, 0:width], aux[:, 0:width], ACT.Sqrt, scale=1.0 / P, bias=eps_col)\
                .then_inc(sem(f"{tag}_rt"), 1)

    def head_norm_dve(e, pos, ch, tag, dst, gain, width):
        for h in range(MH):
            pos.next_use()
            reach(e, f"{tag}_rt", h + 1)
            ch(e.reciprocal(tmp[:, 3, 0:width], tmp[:, 3, 0:width]))
            e.scalar_tensor_tensor(out=dst[:, h, 0:width], in0=tmp[:, h % 2, 0:width], scalar=gain,
                                   in1=tmp[:, 3, 0:width], op0=ALU.mult, op1=ALU.mult).then_inc(sem(f"{tag}_sc"), 1)
            reach(e, f"{tag}_sc", h + 1)

    def mv_act(e, pos):
        for p in range(2):
            use = pos.next_use()
            e.wait_ge(unit_done, UNIT0["mkv"] + 6 + 2 * p)
            copy(e, m_v[:, :, 256 * p:256 * p + 256],
                 region[:, use % 2, 0:512].rearrange("p (t c) -> p t c", c=256)).then_inc(free[use % 2], 1)

    def qm_pe(e, pos):
        def sums(h):
            reach(e, "qm_sq", h + 1)
            if h:
                reach(e, "qm_rt", h)
            for lo in (0, HALF):
                last = e.matmul(aux[:, lo:lo + HALF], ones[:], tmp[:, 2, lo:lo + HALF], start=True, stop=True)
            last.then_inc(sem("qm_ss"), 1)

        for h in range(MH):
            use = pos.next_use()
            project(e, use, UNIT0["qm"] + h, h2_hi, h2_lo, KD).then_inc(unit_done, 1)
            if h:
                sums(h - 1)
        sums(MH - 1)

    def mem_score(e, i, dst):
        h, t = divmod(i, TT)
        return e.matmul(dst[:, 0:CTX], q_mem[:, h, t * P:(t + 1) * P], m_k[:, h], start=True, stop=True)

    mem_att = Attention("ma", MH, CTX, HALF, mem_score, lambda i, b: m_v[:, b, P * (i // TT):P * (i // TT) + P],
                        lambda i: (o_mem[:, i % TT, P * (i // TT):P * (i // TT) + P], slice(0, P)))

    def out2_pe(e, pos):
        for j in range(8):
            use = pos.next_use()
            project(e, use, UNIT0["out2"] + j, y_hi, y_lo, KD,
                    wait_k=(lambda k: reach(e, "y_lo", k + 1)) if j == 0 else None).then_inc(unit_done, 1)

    def out2_act(e, pos, ch):
        for k in range(KD):
            copy(e, y_hi[:, k], y[:, k]).then_inc(sem("y_hi"), 1)

    def out2_dve(e, pos, ch):
        for k in range(KD):
            reach(e, "y_hi", k + 1)
            e.tensor_tensor(y_lo[:, k], y[:, k], y_hi[:, k].bitcast(F32), ALU.subtract).then_inc(sem("y_lo"), 1)
        reach(e, "x3_ld", 16)
        for j in range(8):
            use = pos.next_use()
            e.wait_ge(unit_done, UNIT0["out2"] + j + 1)
            e.tensor_tensor(x3[:, j], region[:, use % 2], x3[:, j], ALU.add).then_inc(sem("out_ready"), 1)
            reach(e, "out_ready", j + 1)
            e.sem_inc(free[use % 2], 1)

    with nc.Block() as block:
        @block.sync
        def _(sp):
            def load(u, s):
                sp.dma_start(w_raw[:, s], units[u]).then_inc(raw_loaded[s], 16)

            sp.dma_start(par[:], small).then_inc(sem("small_ld"), 16)
            load(0, 0)
            load(1, 1)
            ada_sp(sp, None)
            with sp.Fori(1, N_UNITS // 2) as i:
                for s in range(2):
                    sp.wait_ge(unit_split, i * 2 + (s - 1))
                    sp.dma_start(w_raw[:, s], units[i * 2 + s]).then_inc(raw_loaded[s], 16)
            for j in range(KD):
                reach(sp, "out_ready", j + 1)
                sp.dma_start(out[:, j], x3[:, j]).then_inc(sem("out_st"), 16)
            reach(sp, "out_st", 16 * KD)

        @block.gpsimd
        def _(pool):
            def split(i, s):
                pool.wait_ge(raw_loaded[s], i * 16 + 16)
                pool.tensor_tensor(w_hi[:, s], w_raw[:, s], one_col.broadcast_to([P, 1024]), ALU.mult)\
                    .then_inc(sem("hi_split"), 1)
                reach(pool, "hi_split", i * 2 + (s + 1))
                pool.tensor_tensor(w_lo[:, s], w_raw[:, s], w_hi[:, s].bitcast(F32), ALU.subtract)\
                    .then_inc(unit_split, 1)

            def split_range(a, b):
                with pool.Fori(a // 2, b // 2) as i:
                    for s in range(2):
                        pool.wait_ge(unit_done, i * 2 + (s - 1))
                        split(i, s)

            pool.memset(one_col, 1.0).then_inc(sem("consts"), 1)
            pool.memset(ones[:], 1.0).then_inc(sem("consts"), 1)
            pool.memset(ident[:], 0.0).then_inc(sem("consts"), 1)
            reach(pool, "consts", 3)
            pool.affine_select(out=ident[:], in_=ident[:], compare_op=ALU.not_equal, fill=1.0, base=0,
                               pattern=[[-1, P]], channel_multiplier=1).then_inc(sem("consts"), 1)
            split(0, 0)
            split(0, 1)
            split_range(2, ATTN_SPLIT)
            bias_pool(pool, None)
            split_range(ATTN_SPLIT, N_UNITS)

        @block.scalar
        def _(act):
            pos = Pos()
            ch = Chain(act, "scalar_step")
            act.dma_start(ctx_sb[:], ctx_t).then_inc(sem("ctx_ld"), 16)
            act.dma_start(x_sb[:], x_t).then_inc(sem("x_ld"), 16)
            ada_act(act, pos, ch)
            reach(act, "ctx_ld", 16)
            meet(act, pos)
            rms_act(act, ch, "rc", lambda k: ctx_sb[:, k], KD, CTX, D)
            norm_act(act, ch, "nc", KD, CTX, hc_hi, lambda k: a1c[:, k:k + 1], lambda k: mod_c[:, k:k + 1])
            reach(act, "x_ld", 16)
            meet(act, pos)
            act.dma_start(sin1[:], rope_s).then_inc(sem("rope1_ld"), 16)
            act.dma_start(cos1[:], rope_c).then_inc(sem("rope1_ld"), 16)
            rms_act(act, ch, "r1", lambda k: x_sb[:, k], KD, T, D)
            norm_act(act, ch, "n1", KD, T, h_hi, lambda k: a1[:, k:k + 1], lambda k: mod_x[:, k:k + 1])
            meet(act, pos)
            proj1_act(act, pos, ch)
            meet(act, pos, 3)
            na.act(act, pos, ch)
            meet(act, pos, 3)
            act.dma_start(x1[:], x_t).then_inc(sem("x_again"), 16)
            turn_back_act(act, pos, "nt", mix_hi)
            ln_act(act, pos, ch)
            meet(act, pos, 3)
            for _ in range(8):
                pos.next_use()
            meet(act, pos, 3)
            rms_act(act, ch, "r2", lambda k: x1[:, k], KD, T, D)
            norm_act(act, ch, "n2", KD, T, h2_hi, lambda k: a2[:, k:k + 1], lambda k: mod_x[:, 24 + k:25 + k])
            meet(act, pos, 3)
            mlp_act(act, pos, ch)
            meet(act, pos, 3)
            rms_act(act, ch, "nf", lambda k: x1[:, k], KD, T, D)
            reach(act, "x2_ready", KD)
            act.dma_start(x_spill, x1[:]).then_inc(sem("spill"), 16)
            meet(act, pos)
            rms_act(act, ch, "r3", lambda k: x1[:, k], KD, T, D)
            norm_act(act, ch, "n3", KD, T, h2_hi, lambda k: sp_("norm_2", 1, k), None)
            reach(act, "spill", 16)
            act.dma_start(pos_i[NOPE:QK], positions.partition_broadcast(ROPE)).then_inc(sem("pos_ld"), 16)
            meet(act, pos, 3)
            lat_act(act, pos, ch)
            tables_act(act, pos, ch)
            meet(act, pos)
            rms_act(act, ch, "rq", lambda k: q_lat[:, k], NQL, T, P * NQL)
            norm_act(act, ch, "nq", NQL, T, ql_hi, lambda k: sp_("qn", 1, k), None)
            meet(act, pos, 3)
            heads_act(act, pos, ch, "hq", "uq", 3, QK)
            meet(act, pos, 3)
            rms_act(act, ch, "rk", lambda k: kv_lat[:, k], NKVL, T, P * NKVL)
            norm_act(act, ch, "nk", NKVL, T, kvl_hi, lambda k: sp_("kvn", 1, k), None)
            meet(act, pos, 3)
            copy(act, tmp[NOPE:QK, 0], k_pe[NOPE:QK]).then_inc(sem("kpe_in"), 1)
            copy(act, tmp[NOPE:QK, 1], k_pe[NOPE:QK]).then_inc(sem("kpe_in"), 1)
            reach(act, "kpe_in", 2)
            heads_act(act, pos, ch, "hk", "uk", 4, NOPE)
            meet(act, pos, 3)
            uv_act(act, pos, ch)
            meet(act, pos, 3)
            mla.act(act, pos, ch)
            meet(act, pos, 3)
            gate_act(act, pos, ch, "ga", "gattn")
            meet(act, pos, 3)
            branch_act(act, pos, ch, 0)
            act.dma_start(mem_sb[:], mem_t).then_inc(sem("mem_ld"), 16)
            meet(act, pos, 3)
            cv_act(act, pos, ch)
            meet(act, pos, 3)
            branch_act(act, pos, ch, 1)
            reach(act, "mem_ld", 16)
            meet(act, pos, 3)
            rms_act(act, ch, "rm", lambda k: mem_sb[:, k], KD, CTX, D)
            norm_act(act, ch, "nm", KD, CTX, hm_hi, lambda k: sp_("memn", 1, k), None)
            meet(act, pos, 3)
            head_norm_act(act, pos, "mk", "mkv", CTX)
            mv_act(act, pos)
            meet(act, pos, 3)
            head_norm_act(act, pos, "qm", "qm", T)
            meet(act, pos, 3)
            mem_att.act(act, pos, ch)
            meet(act, pos, 3)
            gate_act(act, pos, ch, "gm", "gmem")
            meet(act, pos, 3)
            branch_act(act, pos, ch, 2)
            meet(act, pos, 3)
            act.dma_start(x3[:], x_spill).then_inc(sem("x3_ld"), 16)
            out2_act(act, pos, ch)

        @block.vector
        def _(dve):
            pos = Pos()
            ch = Chain(dve, "vector_step")
            ada_dve(dve, pos, ch)
            meet(dve, pos)
            rms_dve(dve, ch, "rc", CTX)
            norm_dve(dve, ch, "nc", KD, CTX, lambda k: ctx_sb[:, k], hc_hi, hc_lo)
            meet(dve, pos)
            rms_dve(dve, ch, "r1", T)
            norm_dve(dve, ch, "n1", KD, T, lambda k: x_sb[:, k], h_hi, h_lo)
            meet(dve, pos)
            proj1_dve(dve, pos, ch)
            meet(dve, pos, 3)
            na.dve(dve, pos, ch)
            meet(dve, pos, 3)
            turn_back_dve(dve, pos, "nt", mix_hi, mix_lo)
            ln_dve(dve, pos, ch)
            meet(dve, pos, 3)
            out1_dve(dve, pos, ch)
            meet(dve, pos, 3)
            rms_dve(dve, ch, "r2", T)
            norm_dve(dve, ch, "n2", KD, T, lambda k: x1[:, k], h2_hi, h2_lo)
            meet(dve, pos, 3)
            mlp_dve(dve, pos, ch)
            meet(dve, pos, 3)
            final_dve(dve, pos, ch)
            meet(dve, pos)
            rms_dve(dve, ch, "r3", T)
            norm_dve(dve, ch, "n3", KD, T, lambda k: x1[:, k], h2_hi, h2_lo)
            meet(dve, pos, 3)
            for _ in range(6):
                pos.next_use()
            tables_dve(dve, pos, ch)
            meet(dve, pos)
            rms_dve(dve, ch, "rq", T)
            norm_dve(dve, ch, "nq", NQL, T, lambda k: q_lat[:, k], ql_hi, ql_lo)
            meet(dve, pos, 3)
            heads_dve(dve, pos, ch, "hq", q_h, qh_s, rot_q)
            meet(dve, pos, 3)
            rms_dve(dve, ch, "rk", T)
            norm_dve(dve, ch, "nk", NKVL, T, lambda k: kv_lat[:, k], kvl_hi, kvl_lo)
            meet(dve, pos, 3)
            heads_dve(dve, pos, ch, "hk", k_h, sp_("kh"), rot_k)
            meet(dve, pos, 3)
            for _ in range(4):
                pos.next_use()
            meet(dve, pos, 3)
            mla.dve(dve, pos, ch)
            meet(dve, pos, 3)
            gate_dve(dve, pos, ch, "ga")
            meet(dve, pos, 3)
            branch_dve(dve, pos, ch, 0)
            meet(dve, pos, 3)
            cv_dve(dve, pos, ch)
            meet(dve, pos, 3)
            branch_dve(dve, pos, ch, 1)
            meet(dve, pos, 3)
            rms_dve(dve, ch, "rm", CTX)
            norm_dve(dve, ch, "nm", KD, CTX, lambda k: mem_sb[:, k], hm_hi, hm_lo)
            meet(dve, pos, 3)
            head_norm_dve(dve, pos, ch, "mk", m_k, sp_("mk"), CTX)
            pos.next_use(), pos.next_use()
            meet(dve, pos, 3)
            head_norm_dve(dve, pos, ch, "qm", q_mem, mq_s, T)
            meet(dve, pos, 3)
            mem_att.dve(dve, pos, ch)
            meet(dve, pos, 3)
            gate_dve(dve, pos, ch, "gm")
            meet(dve, pos, 3)
            branch_dve(dve, pos, ch, 2)
            meet(dve, pos, 3)
            out2_dve(dve, pos, ch)

        @block.tensor
        def _(pe):
            pos = Pos()
            reach(pe, "consts", 4)
            ada_pe(pe, pos)
            rms_pe(pe, "rc", KD, CTX)
            rms_pe(pe, "r1", KD, T)
            proj1_pe(pe, pos)
            meet(pe, pos, 3)
            na.pe(pe, pos)
            meet(pe, pos, 3)
            turn_back_pe(pe, pos, "nt", o_tok)
            ln_pe(pe, pos)
            meet(pe, pos, 3)
            out1_pe(pe, pos)
            meet(pe, pos, 3)
            rms_pe(pe, "r2", KD, T)
            meet(pe, pos, 3)
            mlp_pe(pe, pos)
            meet(pe, pos, 3)
            rms_pe(pe, "nf", KD, T)
            rms_pe(pe, "r3", KD, T)
            meet(pe, pos, 3)
            lat_pe(pe, pos)
            rms_pe(pe, "rq", NQL, T)
            meet(pe, pos, 3)
            heads_pe(pe, pos, "hq", "uq", ql_hi, ql_lo, NQL, 3)
            meet(pe, pos, 3)
            rms_pe(pe, "rk", NKVL, T)
            meet(pe, pos, 3)
            heads_pe(pe, pos, "hk", "uk", kvl_hi, kvl_lo, NKVL, 4)
            meet(pe, pos, 3)
            uv_pe(pe, pos)
            meet(pe, pos, 3)
            mla.pe(pe, pos)
            meet(pe, pos, 3)
            gate_pe(pe, pos, "ga", "gattn", o_tok2)
            meet(pe, pos, 3)
            branch_pe(pe, pos, 0, "ga_lo")
            meet(pe, pos, 3)
            cv_pe(pe, pos)
            meet(pe, pos, 3)
            branch_pe(pe, pos, 1, "cv_lo")
            meet(pe, pos, 3)
            rms_pe(pe, "rm", KD, CTX)
            meet(pe, pos, 3)
            mkv_pe(pe, pos)
            meet(pe, pos, 3)
            qm_pe(pe, pos)
            meet(pe, pos, 3)
            mem_att.pe(pe, pos)
            meet(pe, pos, 3)
            gate_pe(pe, pos, "gm", "gmem", o_mem)
            meet(pe, pos, 3)
            branch_pe(pe, pos, 2, "gm_lo")
            meet(pe, pos, 3)
            out2_pe(pe, pos)


def _blocks(w, nk, m):
    n = w.shape[1] // m
    return w.reshape(nk, P, n, m).transpose(2, 1, 0, 3).reshape(n, P, nk * m)


def _pad(a, width=1024):
    return np.concatenate([a, np.zeros((*a.shape[:-1], width - a.shape[-1]), np.float32)], axis=-1)


def _features(v):
    return np.ascontiguousarray(v.reshape(-1, P).T)


def _weight_units(a):
    w_in, w_in2 = a["w_in"][0], a["w_in_2"][0]
    parts = [_blocks(w_in[:, 0:512], 8, P), _blocks(w_in[:, 512:1024], 8, P), _blocks(w_in[:, 1024:1536], 8, P)]
    ua, ub = _blocks(w_in[:, 1536:2048], 8, P), _blocks(w_in[:, 2048:2560], 8, P)
    parts.append(np.stack([ua, ub], axis=1).reshape(8, P, 1024))
    parts.append(_blocks(a["w_out"][0], 8, P))
    w1, w2 = _blocks(a["w_mlp1"][0], 8, P), a["w_mlp2"][0]
    for g in range(FF_GROUPS):
        parts += [w1[8 * g:8 * g + 8], _blocks(w2[1024 * g:1024 * (g + 1)], 8, P)]
    at = np.cumsum([0, 384, 256, 32, 512, 512, 512, 512, 512, 512, 512, 3072])
    col = lambda i: w_in2[:, at[i]:at[i + 1]]
    parts += [_blocks(col(0), 8, P), _blocks(col(1), 8, P)]
    pe_cols = np.concatenate([np.zeros((1024, NOPE), np.float32), col(2)], axis=1)
    parts.append(_pad(_blocks(pe_cols, 8, QK)))
    uq = _blocks(a["w_uq_2"][0], NQL, QK)
    parts += [_pad(np.concatenate(list(uq[i:i + 3]), axis=-1))[None] for i in (0, 3, 6)]
    ukv = a["w_ukv_2"][0].reshape(256, HEADS, 128)
    uk = np.concatenate([ukv[:, :, 0:64], np.zeros((256, HEADS, ROPE), np.float32)], axis=2).reshape(256, HEADS * QK)
    uk = _blocks(uk, NKVL, QK)
    parts += [_pad(np.concatenate(list(uk[i:i + 4]), axis=-1))[None] for i in (0, 4)]
    parts.append(_blocks(np.ascontiguousarray(ukv[:, :, 64:128]).reshape(256, 512), NKVL, 512))
    parts.append(_blocks(col(7), 8, P))
    r = _blocks(col(10), 8, P)

    def branch(b, w):
        br = _blocks(w[0], 4, P)
        out = []
        for p in range(4):
            out += [r[8 * b + 2 * p], r[8 * b + 2 * p + 1], np.concatenate([br[2 * p], br[2 * p + 1]], axis=-1)]
        return np.stack(out)

    parts.append(branch(0, a["w_br_attn_2"]))
    cvs = [_blocks(col(i), 8, P) for i in (4, 5, 3, 8)]
    parts.append(np.stack(cvs, axis=1).reshape(16, P, 1024))
    parts.append(branch(1, a["w_br_conv_2"]))
    mkv = a["w_mkv_2"][0].reshape(1024, MH, 2, P)
    parts += [_blocks(np.ascontiguousarray(mkv[:, :, i]).reshape(1024, MH * P), 8, P) for i in (0, 1)]
    parts += [_blocks(col(6), 8, P), _blocks(col(9), 8, P)]
    parts.append(branch(2, a["w_br_mem_2"]))
    parts.append(_blocks(a["w_out_2"][0], 8, P))
    return np.concatenate(parts)


def _small(a):
    rows = lambda v: np.concatenate([v.reshape(-1), np.zeros(P - v.size, np.float32)])[:, None]
    invf = (np.float32(10000.0) ** (-np.arange(0, ROPE, 2, dtype=np.float32) / np.float32(ROPE))).astype(np.float32)
    inv_col, sign_col = np.zeros((P, 1), np.float32), np.zeros((P, 1), np.float32)
    inv_col[NOPE:QK, 0] = np.concatenate([invf, invf])
    sign_col[NOPE:QK, 0] = [-1.0] * 16 + [1.0] * 16
    c2 = np.stack([a["c"].reshape(KD, P), a["c_ctx"].reshape(KD, P)], axis=-1)
    cols = {
        "c": c2.transpose(1, 0, 2).reshape(P, 16), "b_ada": _features(a["b_ada"][0]),
        "norm1": _features(a["norm1_g"][0]), "norm2": _features(a["norm2_g"][0]), "final": _features(a["final_g"]),
        "norm_2": _features(a["norm_g_2"][0]), "memn": _features(a["mem_norm_g_2"][0]),
        "ln_g": _features(a["conv_ln_g"][0]), "ln_b": _features(a["conv_ln_b"][0]), "dwb": _features(a["dw_bias"][0]),
        "dww": a["dw_kernel"][0].reshape(TAPS, 4, P).transpose(2, 1, 0).reshape(P, 4 * TAPS),
        "b_gate": _features(a["b_gate_2"][0]), "qn": _features(a["q_norm_g_2"][0]), "kvn": _features(a["kv_norm_g_2"][0]),
        "qh": rows(a["q_head_g_2"]), "kh": rows(a["k_head_g_2"]),
        "cw": a["conv_w_2"][0].reshape(3, 4, P).transpose(2, 1, 0).reshape(P, 12), "cb": _features(a["conv_b_2"][0]),
        "mq": rows(a["mem_q_g_2"]), "mk": rows(a["mem_k_g_2"]), "invf": inv_col, "sign": sign_col,
    }
    return np.ascontiguousarray(np.concatenate([cols[n] for n in SMALL], axis=1))


def _tokens(x):
    return np.ascontiguousarray(x.T.reshape(KD, P, -1).transpose(1, 0, 2))


def _grid_tables():
    n = HD // 4
    inv = (np.float32(10000.0) ** (-np.arange(n, dtype=np.float32) / np.float32(n))).astype(np.float32)
    t = np.arange(T)
    pos = np.stack([t // W_GRID, t % W_GRID]).astype(np.float32)
    ang = (pos[:, None, :] * inv[None, :, None]).astype(np.float32).astype(np.float64)
    c, s = np.cos(ang), np.sin(ang)
    c = np.concatenate([c, c], axis=1).reshape(64, T)
    s = np.concatenate([-s, s], axis=1).reshape(64, T)
    return np.concatenate([c, c]).astype(np.float32), np.concatenate([s, s]).astype(np.float32)


def _window_mask():
    tiles = {v: t for t, v in reversed(list(enumerate(VARIANT)))}
    m = np.full((P, 5, 10, W_GRID), -1.0e30, np.float32)
    c = np.arange(W_GRID)
    c0 = np.clip(c - NA_C // 2, 0, W_GRID - NA_C)
    ok = (c[None, :] >= c0[:, None]) & (c[None, :] < c0[:, None] + NA_C)
    for v, t in tiles.items():
        for a in range(2):
            r = 2 * t + a
            r0 = int(np.clip(r - NA_R // 2, 0, ROWS - NA_R))
            for b in range(10):
                if r0 <= 2 * t + SHIFT[v] + b < r0 + NA_R:
                    m[a * 64:a * 64 + 64, v, b] = np.where(ok, 0.0, -1.0e30)
    return m.reshape(P, 5 * KEYS)


def kernel(**inputs):
    import numpy as _np
    import concourse.bacc as _bacc
    from concourse.bass_utils import run_bass_kernel_spmd as _run

    a = {k: _np.asarray(v) for k, v in inputs.items()}
    rope_c, rope_s = _grid_tables()
    rpb_pad = _np.pad(a["rpb"][0], ((0, 0), (2, 2), (48, 48)))
    rpb_pad = _np.tile(rpb_pad, (1, 1, W_GRID))
    arrays = {
        "x_t": _tokens(a["x"][0]), "ctx_t": _tokens(a["ctx"][0]), "mem_t": _tokens(a["mem_2"][0]),
        "w_ada": _np.ascontiguousarray(a["w_ada"][0].reshape(KD, P, 12, HALF).transpose(2, 1, 0, 3)),
        "units": _weight_units(a), "small": _small(a), "rope_c": rope_c, "rope_s": rope_s,
        "rpb_pad": rpb_pad, "mask": _window_mask(), "positions": a["positions_2"].reshape(T),
    }
    assert arrays["units"].shape == (N_UNITS, P, 1024)
    nc = _bacc.Bacc("TRN2", target_bir_lowering=False, num_devices=1)
    args = [nc.dram_tensor(n, v.shape, mybir.dt.from_np(v.dtype), kind="ExternalInput").ap() for n, v in arrays.items()]
    out = nc.dram_tensor("out_t", (P, KD, T), F32, kind="ExternalOutput").ap()
    spill = nc.dram_tensor("x_spill", (P, KD, T), F32).ap()
    build(nc, *args, out, spill)
    r = _run(nc, [arrays], core_ids=[0])
    got = r.results[0]["out_t"]
    return got.transpose(1, 0, 2).reshape(D, T).T.reshape(1, T, D)
```

```python
from contextlib import ExitStack

import numpy as np

import concourse.bass as bass
from concourse import mybir

F32 = mybir.dt.float32
F32R = mybir.dt.float32r
I32 = mybir.dt.int32
ALU = mybir.AluOpType
ACT = mybir.ActivationFunctionType
AX = mybir.AxisListType.X

P = 128
T = 1024
TT = T // P
HALF = 512
D = 1024
KD = D // P
CTX = 256
EPS = 1e-6
W_GRID = 64
ROWS = T // W_GRID
HEADS = 8
HD = 64
NA_R, NA_C = 8, 16
TAPS = 31
PAD = TAPS // 2
FF_GROUPS = 4
KEYS = 10 * W_GRID
NKT = (KEYS + CTX) // P
VARIANT = [0, 1, 2, 2, 2, 2, 3, 4]
SHIFT = [0, -2, -4, -6, -8]
QK = 96
NOPE = 64
ROPE = 32
NQL, NKVL = 3, 2
MH = 4
EARLY_TAPS = 15
TABLE = 2 * W_GRID - 1
TWO_PI = 2.0 * np.pi

SMALL = {}
_at = 0
for _name, _n in [("c", 16), ("b_ada", 48), ("norm1", 8), ("norm2", 8), ("final", 8), ("norm_2", 8),
                  ("memn", 8), ("ln_g", 4), ("ln_b", 4), ("dwb", 4), ("dww", 4 * TAPS), ("b_gate", 24),
                  ("qn", 3), ("kvn", 2), ("qh", 1), ("kh", 1), ("cw", 12), ("cb", 4), ("mq", 1), ("mk", 1),
                  ("invf", 1), ("sign", 1), ("khr", 1)]:
    SMALL[_name] = _at
    _at += _n
N_SMALL = _at

STAGE_UNITS = [("q", 4), ("k", 4), ("v", 4), ("u", 8), ("out1", 8), ("mlp", 16 * FF_GROUPS), ("lat", 6),
               ("uq", 4), ("uk", 3), ("uv", 1), ("gattn", 4), ("br0", 12), ("cv", 16), ("br1", 12),
               ("mkv", 8), ("qm", 4), ("gmem", 4), ("br2", 12), ("out2", 8)]
N_UNITS = sum(n for _, n in STAGE_UNITS)
UNIT0 = {}
_at = 0
for _name, _n in STAGE_UNITS:
    UNIT0[_name] = _at
    _at += _n
ATTN_SPLIT = UNIT0["out1"] + 2


KINDS = {
    "rms": [("rc", 8), ("r1", 8), ("lnv", 4), ("rm", 8)],
    "norm": [("nc", 8), ("n1", 8), ("lnn", 4), ("n2", 8), ("n3", 8), ("nq", 3), ("nk", 2), ("nm", 8)],
    "head": [("hq", 8), ("hk", 8), ("mk", 4), ("qm", 4)],
    "att": [("na", 64), ("mla", 64), ("ma", 32)],
    "gate": [("ga", 4), ("gm", 4)],
    "branch": [("br0", 8), ("br1", 8), ("br2", 8)],
}
SHARED = {tag: (kind, stages[:i]) for kind, stages in KINDS.items() for i, (tag, _) in enumerate(stages)}
COUNTS = {f"{tag}_{what}": 1 for tag, _ in KINDS["rms"] for what in ("root", "rs")} | {f"br{b}_part": 4 for b in range(3)} \
    | {"hq_part": 4, "hk_part": 5}


def build(nc, x_t, ctx_t, mem_t, w_ada, units, small, rope_c, rope_s, rpb_pad, mask, positions, out, x_spill,
          rs_spill):
    def sbuf_map():
        at = (nc.sbuf_base + 63) // 64 * 64
        return at, at + 43 * 1024 + 512

    base, arena = sbuf_map()

    def fixed(name, shape, offset, dt=F32):
        return nc.alloc_sbuf_tensor_at(name, [P, *shape], dt, offset=base + offset)

    def place(name, shape, kib, dt=F32):
        return nc.alloc_sbuf_tensor_at(name, [P, *shape], dt, offset=arena + int(kib * 1024))

    KIB = 1024
    w_raw = fixed("w_raw", [2, 1024], 0)
    w_hi = fixed("w_hi", [2, 1024], 8 * KIB, F32R)
    w_lo = fixed("w_lo", [2, 1024], 16 * KIB, F32R)
    tmp = fixed("tmp", [4, T], 24 * KIB)
    ident = fixed("ident", [P], 40 * KIB)
    ones = fixed("ones", [P], 40 * KIB + 512)
    par = fixed("par", [N_SMALL], 41 * KIB)
    der = fixed("der", [256], 41 * KIB + (4 * N_SMALL + 31) // 32 * 32)
    assert 4 * N_SMALL + 32 + 1024 <= 2560

    def sp_(name, n=1, k=0):
        return par[:, SMALL[name] + k:SMALL[name] + k + n]

    mod_x, mod_c = der[:, 0:48], der[:, 48:64]
    a1, a1c, a2 = der[:, 64:72], der[:, 72:80], der[:, 80:88]
    silu_c = der[:, 88:104]
    qh_s, mq_s = der[:, 104:105], der[:, 105:106]
    one_col = der[:, 106:107]
    eps_col = der[:, 107:108]
    both_g = der[:, 128:136]
    row_max, neg_max, row_sum, inv_sum = (der[:, 112 + 4 * i:116 + 4 * i] for i in range(4))

    ada_buf = place("ada_buf", [2, KD, HALF], 0)
    ada_row = place("ada_row", [2, HALF], 32)
    ctx_sb = place("ctx_sb", [KD, CTX], 36)
    hc_hi = place("hc_hi", [KD, CTX], 44, F32R)
    hc_lo = place("hc_lo", [KD, CTX], 52, F32R)
    x_sb = place("x_sb", [KD, T], 64)
    h_hi = place("h_hi", [KD, T], 96, F32R)
    h_lo = place("h_lo", [KD, T], 128, F32R)
    q_t = place("q_t", [4, T], 0)
    q_rot = place("q_rot", [4, T], 16)
    k_ctx = place("k_ctx", [4, CTX], 32)
    v_ctx = place("v_ctx", [2, HALF], 36)
    cos1 = place("cos1", [T], 40)
    sin1 = place("sin1", [T], 60)
    k_rot = place("k_rot", [4, T], 64)
    v_tok = place("v_tok", [TT, HALF], 80)
    glu = place("glu", [4, T + 2 * PAD], 40)
    conv = fixed("conv", [4, T], 24 * KIB)
    na_prob = place("na_prob", [2, KEYS + CTX], 96)
    na_prob_t = place("na_prob_t", [2, NKT, P], 104)
    tmp_b = place("tmp_b", [4, T], 96)
    o_tok = place("o_tok", [TT, HALF], 112)
    bias_t = place("bias_t", [5, KEYS + CTX], 128)
    mask_t = place("mask_t", [5, KEYS], 145.5)
    toep = [place("toep0", [18, W_GRID], 57), place("toep1", [18, W_GRID], 158)]
    mix_hi = place("mix_hi", [KD, T], 0, F32R)
    mix_lo = place("mix_lo", [KD, T], 64, F32R)
    x1 = place("x1", [KD, T], 128)
    h2_hi = place("h2_hi", [KD, T], 96, F32R)
    h2_lo = place("h2_lo", [KD, T], 32, F32R)
    ff_hi = place("ff_hi", [KD, T], 0, F32R)
    ff_lo = place("ff_lo", [KD, T], 64, F32R)
    q_h = place("q_h", [HEADS, T], 0)
    k_h = place("k_h", [HEADS, T], 64)
    v2 = place("v2", [TT, HALF], 128)
    q_lat = place("q_lat", [NQL, T], 0)
    lat_sq = place("lat_sq", [2, T], 12)
    rs1 = place("rs1", [T], 20)
    ql_hi = place("ql_hi", [NQL, T], 64, F32R)
    ql_lo = place("ql_lo", [NQL, T], 76, F32R)
    k_turned = place("k_turned", [T], 92)
    kv_lat = place("kv_lat", [NKVL, T], 128)
    k_pe = place("k_pe", [T], 136)
    cos2 = place("cos2", [T], 140)
    kvl_hi = place("kvl_hi", [NKVL, T], 144, F32R)
    kvl_lo = place("kvl_lo", [NKVL, T], 152, F32R)
    sin2 = place("sin2", [T], 160)
    pos_i = nc.alloc_sbuf_tensor_at("pos_i", [P, T], I32, offset=arena + 160 * 1024)
    o_tok2 = place("o_tok2", [TT, HALF], 144)
    o_hi = place("o_hi", [4, T], 0, F32R)
    o_lo = place("o_lo", [4, T], 16, F32R)
    y = place("y", [KD, T], 64)
    z_pad = place("z_pad", [T + 2], 128)
    mem_sb = place("mem_sb", [KD, CTX], 133)
    hm_hi = place("hm_hi", [KD, CTX], 141, F32R)
    hm_lo = place("hm_lo", [KD, CTX], 149, F32R)
    m_k = place("m_k", [MH, CTX], 157)
    m_v = place("m_v", [2, HALF], 133)
    q_mem = place("q_mem", [MH, T], 0)
    o_mem = place("o_mem", [TT, HALF], 137)
    y_hi = place("y_hi", [KD, T], 96, F32R)
    y_lo = place("y_lo", [KD, T], 32, F32R)
    x3 = place("x3", [KD, T], 128)
    rs1_again = place("rs1_again", [T], 160)

    prob = nc.alloc_sbuf_tensor_at("prob", [P, 2, T], F32, offset=base + 24 * KIB)
    prob_t = nc.alloc_sbuf_tensor_at("prob_t", [P, 2, TT, P], F32, offset=base + 32 * KIB)

    region = nc.alloc_psum_tensor("region", [P, 2, T], F32)
    aux = nc.alloc_psum_tensor("aux", [P, T], F32)
    pv = nc.alloc_psum_tensor("pv", [P, 2, HALF], F32)

    sems = {}

    def sem(name):
        tag, _, what = name.partition("_")
        if tag in SHARED:
            name = f"{SHARED[tag][0]}_{what}"
        if name not in sems:
            sems[name] = nc.alloc_semaphore(name)
        return sems[name]

    def reach(e, name, value):
        tag, _, what = name.partition("_")
        if tag in SHARED:
            kind, before = SHARED[tag]
            value = value + sum(COUNTS.get(f"{t}_{what}", n) for t, n in before)
        e.wait_ge(sem(name), value)

    raw_loaded = [sem("raw_loaded_0"), sem("raw_loaded_1")]
    free = [sem("region_free_0"), sem("region_free_1")]
    unit_split, unit_done = sem("unit_split"), sem("unit_done")

    class Pos:

        def __init__(self):
            self.use = 0
            self.count = {}

        def next_use(self):
            self.use += 1
            return self.use - 1

        def add(self, name, n=1):
            self.count[name] = self.count.get(name, 0) + n
            return self.count[name]

    def wait_region(e, use):
        if use >= 2:
            e.wait_ge(free[use % 2], use // 2)

    def copy(e, dst, src, **kw):
        return e.activation(dst, src, ACT.Copy, **kw)

    def mm3(pe, dst, wh, wl, xh, xl, first, last):
        pe.matmul(dst, wh, xh, start=first, stop=False)
        pe.matmul(dst, wh, xl, start=False, stop=False)
        return pe.matmul(dst, wl, xh, start=False, stop=last)

    def project(pe, use, unit, xh, xl, nk, width=T, m=P, off=0, step=P, wait_k=None):
        r, s = use % 2, unit % 2
        pe.wait_ge(unit_split, unit + 1)
        wait_region(pe, use)
        for lo in range(0, width, HALF):
            n = min(HALF, width - lo)
            for k in range(nk):
                if wait_k is not None and lo == 0:
                    wait_k(k)
                w = slice(off + k * step, off + k * step + m)
                last = mm3(pe, region[0:m, r, lo:lo + n], w_hi[:, s, w], w_lo[:, s, w],
                           xh[:, k, lo:lo + n], xl[:, k, lo:lo + n], k == 0, k == nk - 1)
        return last

    LAG = 3
    LAGGED = [(n, k) for t in range(KD + LAG) for n, k in ((0, t), (1, t - LAG)) if 0 <= k < KD]
    LATE_LAST = [(0, k) for k in range(KD - 1)] + [(1, k) for k in range(LAG)] + [(0, KD - 1)] \
        + [(1, k) for k in range(LAG, KD)]

    def project_pair(pe, arrive, xh, xl, wait_k, order=LAGGED):
        for n, k in order:
            if k == 0:
                arrive(n)
            if n == 0:
                wait_k(k)
            w = slice(k * P, k * P + P)
            for lo in (0, HALF):
                last = mm3(pe, region[:, n, lo:lo + HALF], w_hi[:, n, w], w_lo[:, n, w],
                           xh[:, k, lo:lo + HALF], xl[:, k, lo:lo + HALF], k == 0, k == KD - 1)
            if k == KD - 1:
                last.then_inc(unit_done, 1)

    def start_pair(pe, pos, unit0, xh, xl, wait_k):
        assert pos.use % 2 == 0 and unit0 % 2 == 0

        def arrive(n):
            pe.wait_ge(unit_split, unit0 + n + 1)
            wait_region(pe, pos.use + n)

        project_pair(pe, arrive, xh, xl, wait_k)
        pos.use += 2

    def project_tokens(pe, use, units, xh, xl, nk, tiles, cols, rhs):
        r = use % 2
        wait_region(pe, use)
        for i, t in enumerate(tiles):
            for k in range(nk):
                xs = slice(t * P, t * P + P)
                dst = region[:, r, i * cols:(i + 1) * cols]
                pe.matmul(dst, xh[:, k, xs], rhs(w_hi, k), start=(k == 0), stop=False)
                pe.matmul(dst, xl[:, k, xs], rhs(w_hi, k), start=False, stop=False)
                last = pe.matmul(dst, xh[:, k, xs], rhs(w_lo, k), start=False, stop=(k == nk - 1))
        return last

    def column_sums(pe, tag, src, nk, width, rows=P, ready=None):
        for k in range(nk):
            reach(pe, f"{tag}_sq", k + 1)
            for lo in range(0, width, HALF):
                n = min(HALF, width - lo)
                last = pe.matmul(aux[0:rows, lo:lo + n], ones[0:rows, 0:rows], src(k)[:, lo:lo + n],
                                 start=(k == 0), stop=(k == nk - 1))
            last.then_inc(sem(f"{tag}_sqmm"), 1)

    class Chain:
        def __init__(self, e, name):
            self.e, self.s, self.n = e, sem(name), 0

        def __call__(self, ins):
            self.n += 1
            ins.then_inc(self.s, 1)
            self.e.wait_ge(self.s, self.n)

    def meet(e, pos, engines=2, wait=True):
        n = pos.add(f"meet{engines}")
        e.drain().then_inc(sem(f"stage_end_{engines}"), 1)
        if wait:
            reach(e, f"stage_end_{engines}", engines * n)

    def rms_act(e, ch, tag, src, nk, width, n, scale_from_ready=None, tmp=tmp):
        for k in range(nk):
            if k >= 2:
                reach(e, f"{tag}_sqmm", k - 1)
            if scale_from_ready:
                scale_from_ready(k)
            e.activation(tmp[:, k % 2, 0:width], src(k), ACT.Square).then_inc(sem(f"{tag}_sq"), 1)
        reach(e, f"{tag}_sqmm", nk)
        root_act(e, tag, tmp[:, 3, 0:width], aux[:, 0:width], n, eps_col)

    def root_act(e, tag, dst, src, n, eps):
        e.activation(dst, src, ACT.Sqrt, scale=1.0 / n, bias=eps).then_inc(sem(f"{tag}_root"), 1)

    def inverse_dve(e, tag, k, root):
        reach(e, f"{tag}_root", k)
        e.reciprocal(root, root).then_inc(sem(f"{tag}_rs"), 1)
        reach(e, f"{tag}_rs", k)

    def rms_pe(e, tag, nk, width, tmp=tmp):
        column_sums(e, tag, lambda k: tmp[:, k % 2], nk, width)

    def rms_dve(e, ch, tag, width, tmp=tmp):
        inverse_dve(e, tag, 1, tmp[:, 3, 0:width])

    def norm_act(e, ch, tag, nk, width, hi, scale, bias, func=ACT.Identity, tmp=tmp):
        for k in range(nk):
            t = tmp[:, k % 2, 0:width]
            reach(e, f"{tag}_nm", k + 1)
            e.activation(t, t, func, scale=scale(k), bias=bias(k) if bias else 0.0).then_inc(sem(f"{tag}_af"), 1)
            reach(e, f"{tag}_af", k + 1)
            copy(e, hi[:, k, 0:width], t).then_inc(sem(f"{tag}_hi"), 1)

    def norm_dve(e, ch, tag, nk, width, src, hi, lo, tmp=tmp, rs=3):
        def low(k):
            reach(e, f"{tag}_hi", k + 1)
            e.tensor_tensor(lo[:, k, 0:width], tmp[:, k % 2, 0:width], hi[:, k, 0:width].bitcast(F32),
                            ALU.subtract).then_inc(sem(f"{tag}_lo"), 1)

        for k in range(nk):
            if k >= 2:
                reach(e, f"{tag}_lo", k - 1)
            e.tensor_tensor(tmp[:, k % 2, 0:width], src(k), tmp[:, rs, 0:width], ALU.mult).then_inc(sem(f"{tag}_nm"), 1)
            if k:
                low(k - 1)
        low(nk - 1)

    def split_act(e, tag, k, dst, src):
        copy(e, dst, src).then_inc(sem(f"{tag}_hi"), 1)

    N_ADA = 12

    def ada_sp(e, pos):
        for g in range(N_ADA):
            if g >= 2:
                reach(e, "ada_mm", g - 1)
            e.dma_start(ada_buf[:, g % 2], w_ada[g]).then_inc(sem(f"ada_ld{g % 2}"), 16)

    def ada_pe(e, pos):
        def turn(g):
            reach(e, "ada_row", g + 1)
            for j in range(4):
                m = 4 * g + j
                last = e.transpose(aux[:, 2 * m:2 * m + 2], ada_row[0:2, g % 2, j * P:(j + 1) * P], ident[0:2, 0:2])
            last.then_inc(sem("ada_tr"), 1)

        reach(e, "silu_c", 1)
        for g in range(N_ADA):
            use = pos.next_use()
            wait_region(e, use)
            reach(e, f"ada_ld{g % 2}", 16 * (g // 2 + 1))
            for k in range(KD):
                last = e.matmul(region[0:2, use % 2, 0:HALF], silu_c[:, 2 * k:2 * k + 2], ada_buf[:, g % 2, k],
                                start=(k == 0), stop=(k == KD - 1))
            last.then_inc(sem("ada_mm"), 1)
            if g:
                turn(g - 1)
        turn(N_ADA - 1)

    def ada_act(e, pos, ch):
        reach(e, "small_ld", 16)
        e.activation(silu_c, sp_("c", 16), ACT.Silu).then_inc(sem("silu_c"), 1)
        for g in range(N_ADA):
            use = pos.next_use()
            reach(e, "ada_mm", g + 1)
            if g >= 2:
                reach(e, "ada_tr", g - 1)
            copy(e, ada_row[0:2, g % 2], region[0:2, use % 2, 0:HALF]).then_inc(free[use % 2], 1)
            e.wait_ge(free[use % 2], use // 2 + 1)
            e.sem_inc(sem("ada_row"), 1)

    def ada_dve(e, pos, ch):
        for _ in range(N_ADA):
            pos.next_use()
        reach(e, "small_ld", 16)
        ch(e.memset(eps_col, EPS))
        ch(e.tensor_scalar(qh_s, sp_("qh"), QK ** -0.5, None, ALU.mult))
        ch(e.tensor_tensor(both_g, sp_("final", 8), sp_("norm_2", 8), ALU.mult))
        ch(e.tensor_scalar(mq_s, sp_("mq"), P ** -0.5, None, ALU.mult))
        reach(e, "ada_tr", N_ADA)
        both = aux[:, 0:96].rearrange("p (m two) -> p m two", two=2)
        ch(e.tensor_tensor(mod_x, both[:, :, 0], sp_("b_ada", 48), ALU.add))
        ch(e.tensor_tensor(mod_c, both[:, 0:16, 1], sp_("b_ada", 16), ALU.add))
        ch(e.scalar_tensor_tensor(out=a1, in0=mod_x[:, 8:16], scalar=1.0, in1=sp_("norm1", 8), op0=ALU.add, op1=ALU.mult))
        ch(e.scalar_tensor_tensor(out=a1c, in0=mod_c[:, 8:16], scalar=1.0, in1=sp_("norm1", 8), op0=ALU.add, op1=ALU.mult))
        ch(e.scalar_tensor_tensor(out=a2, in0=mod_x[:, 32:40], scalar=1.0, in1=sp_("norm2", 8), op0=ALU.add, op1=ALU.mult))

    SWAP = [(i + 16) % 32 for i in range(32)]

    def proj1_pe(e, pos):
        start_pair(e, pos, UNIT0["q"], h_hi, h_lo, lambda k: reach(e, "n1_lo", k + 1))
        for j in range(2, 4):
            use = pos.next_use()
            project(e, use, UNIT0["q"] + j, h_hi, h_lo, KD).then_inc(unit_done, 1)
        for j in range(4):
            use = pos.next_use()
            project(e, use, UNIT0["k"] + j, h_hi, h_lo, KD).then_inc(sem("k_part"), 1)
            use = pos.next_use()
            project(e, use, UNIT0["k"] + j, hc_hi, hc_lo, KD, width=CTX,
                    wait_k=(lambda k: reach(e, "nc_lo", k + 1)) if j == 0 else None).then_inc(unit_done, 1)
        for p in range(2):
            e.wait_ge(unit_split, UNIT0["v"] + 2 * p + 2)
            pair = lambda w, k: w[:, 0:2, k * P:(k + 1) * P]
            for g in range(2):
                use = pos.next_use()
                project_tokens(e, use, None, h_hi, h_lo, KD, range(4 * g, 4 * g + 4), 256, pair).then_inc(sem("v_part"), 1)
            use = pos.next_use()
            project_tokens(e, use, None, hc_hi, hc_lo, KD, range(2), 256, pair).then_inc(unit_done, 2)
        for j in range(8):
            use = pos.next_use()
            project(e, use, UNIT0["u"] + j, h_hi, h_lo, KD).then_inc(unit_done, 1)

    def proj1_act(e, pos, ch):
        for j in range(4):
            use = pos.next_use()
            e.wait_ge(unit_done, UNIT0["q"] + j + 1)
            e.activation(q_t[:, j], region[:, use % 2], ACT.Copy, scale=HD ** -0.5).then_inc(free[use % 2], 1)
        for j in range(4):
            use = pos.next_use()
            reach(e, "k_part", j + 1)
            if j >= 2:
                reach(e, "k_rot", j - 1)
            copy(e, tmp[:, 2 + j % 2], region[:, use % 2]).then_inc(free[use % 2], 1)
            use = pos.next_use()
            e.wait_ge(unit_done, UNIT0["k"] + j + 1)
            copy(e, k_ctx[:, j], region[:, use % 2, 0:CTX]).then_inc(free[use % 2], 1)
        for p in range(2):
            cols = slice(256 * p, 256 * p + 256)
            for g in range(2):
                use = pos.next_use()
                reach(e, "v_part", 2 * p + g + 1)
                copy(e, v_tok[:, 4 * g:4 * g + 4, cols],
                     region[:, use % 2].rearrange("p (t c) -> p t c", c=256)).then_inc(free[use % 2], 1)
            use = pos.next_use()
            e.wait_ge(unit_done, UNIT0["v"] + 2 * p + 2)
            copy(e, v_ctx[:, :, cols],
                 region[:, use % 2, 0:512].rearrange("p (t c) -> p t c", c=256)).then_inc(free[use % 2], 1)
        reach(e, "k_rot", 4)
        for j in range(4):
            use = pos.next_use()
            e.wait_ge(unit_done, UNIT0["u"] + 2 * j + 1)
            e.activation(glu[:, j, PAD:PAD + T], region[:, use % 2], ACT.Sigmoid).then_inc(free[use % 2], 1)
            pos.next_use()

    def proj1_dve(e, pos, ch):
        def rotate(dst, src, done=None):
            ch(e.stream_shuffle(tmp[:, 0], src, SWAP))
            ch(e.tensor_tensor(tmp[:, 0], tmp[:, 0], sin1[:], ALU.mult))
            ch(e.tensor_tensor(dst, src, cos1[:], ALU.mult))
            last = e.tensor_tensor(dst, dst, tmp[:, 0], ALU.add)
            if done:
                last.then_inc(done, 1)
            else:
                ch(last)

        reach(e, "rope1_ld", 32)
        for j in range(4):
            use = pos.next_use()
            e.wait_ge(free[use % 2], use // 2 + 1)
            rotate(q_rot[:, j], q_t[:, j])
        for j in range(4):
            use = pos.next_use()
            pos.next_use()
            e.wait_ge(free[use % 2], use // 2 + 1)
            rotate(k_rot[:, j], tmp[:, 2 + j % 2], sem("k_rot"))
            reach(e, "k_rot", j + 1)
        last_v = 0
        for _ in range(6):
            last_v = pos.next_use()
        e.wait_ge(unit_done, UNIT0["u"] + 1)
        for j in range(4):
            ch(e.memset(glu[:, j, 0:PAD], 0.0))
            ch(e.memset(glu[:, j, PAD + T:], 0.0))
        for j in range(4):
            use = pos.next_use()
            e.wait_ge(free[use % 2], use // 2 + 1)
            use = pos.next_use()
            e.wait_ge(unit_done, UNIT0["u"] + 2 * j + 2)
            g = glu[:, j, PAD:PAD + T]
            e.tensor_tensor(g, region[:, use % 2], g, ALU.mult).then_inc(free[use % 2], 1)
            e.wait_ge(free[use % 2], use // 2 + 1)
            if j < 3:
                for n in range(EARLY_TAPS * j, EARLY_TAPS * (j + 1)):
                    conv_tap(e, ch, n)

    class Attention:

        def __init__(self, tag, heads, nkeys, bufs, score, v_of, store, bias=None, extra=None):
            self.tag, self.n, self.nkeys, self.nkt = tag, heads * TT, nkeys, nkeys // P
            self.score, self.v_of, self.store, self.bias, self.extra = score, v_of, store, bias, extra
            self.split = min(self.nkt, 4)
            self.prob, self.prob_t = bufs

        def s(self, what):
            return sem(f"{self.tag}_{what}")

        def pe(self, e, pos):
            uses = {}

            def scores(i):
                use = uses[i] = pos.next_use()
                wait_region(e, use)
                self.score(e, i, region[:, use % 2]).then_inc(self.s("scored"), 1)

            def turn(i):
                reach(e, self.tag + "_prob", i + 1)
                if i:
                    reach(e, self.tag + "_pt_a", i)
                    if self.nkt > self.split:
                        reach(e, self.tag + "_pt_b", i)
                for b in range(self.nkt):
                    last = e.transpose(aux[:, b * P:(b + 1) * P], self.prob[:, i % 2, b * P:(b + 1) * P], ident[:])
                last.then_inc(self.s("turned"), 1)

            def values(i):
                reach(e, self.tag + "_pt_a", i + 1)
                if self.nkt > self.split:
                    reach(e, self.tag + "_pt_b", i + 1)
                if i >= 2:
                    reach(e, self.tag + "_stored", i - 1)
                for b in range(self.nkt):
                    last = e.matmul(pv[:, i % 2, 0:P], self.prob_t[:, i % 2, b], self.v_of(i, b),
                                    start=(b == 0), stop=(b == self.nkt - 1))
                last.then_inc(self.s("summed"), 1)

            for i in range(self.n + 2):
                if i < self.n:
                    scores(i)
                if 1 <= i <= self.n:
                    turn(i - 1)
                if i >= 2:
                    values(i - 2)

        def act(self, e, pos, ch):
            def exps(i):
                use = pos.next_use()
                src = self.prob[:, i % 2, 0:self.nkeys] if self.bias else region[:, use % 2, 0:self.nkeys]
                reach(e, self.tag + "_maxed", i + 1)
                if i >= 2:
                    reach(e, self.tag + "_turned", i - 1)
                if i >= 4:
                    reach(e, self.tag + "_stored", i - 3)
                e.activation(self.prob[:, i % 2, 0:self.nkeys], src, ACT.Exp, bias=neg_max[:, i % 4:i % 4 + 1],
                             accum_out=row_sum[:, i % 4:i % 4 + 1]).then_inc(self.s("prob"), 1)
                if not self.bias:
                    reach(e, self.tag + "_prob", i + 1)
                    e.sem_inc(free[use % 2], 1)

            def move(i):
                reach(e, self.tag + "_turned", i + 1)
                if i >= 2:
                    reach(e, self.tag + "_summed", i - 1)
                copy(e, self.prob_t[:, i % 2, 0:self.split], aux[:, 0:self.split * P].rearrange("p (b k) -> p b k", k=P))\
                    .then_inc(self.s("pt_a"), 1)

            for i in range(self.n + 1):
                if i < self.n:
                    exps(i)
                if i:
                    move(i - 1)

        def dve(self, e, pos, ch):
            def maxes(i):
                use = pos.next_use()
                reach(e, self.tag + "_scored", i + 1)
                if i >= 4:
                    reach(e, self.tag + "_prob", i - 3)
                if self.bias:
                    if i >= 2:
                        reach(e, self.tag + "_turned", i - 1)
                    reach(e, self.tag + "_bias", self.bias_count(i))
                    e.tensor_tensor_reduce(self.prob[:, i % 2, 0:self.nkeys], region[:, use % 2, 0:self.nkeys], self.bias(i),
                                           1.0, -3.0e38, ALU.add, ALU.max, row_max[:, i % 4:i % 4 + 1])\
                        .then_inc(free[use % 2], 1)
                    e.wait_ge(free[use % 2], use // 2 + 1)
                    e.tensor_scalar(neg_max[:, i % 4:i % 4 + 1], row_max[:, i % 4:i % 4 + 1], -1.0, None,
                                    ALU.mult).then_inc(self.s("maxed"), 1)
                else:
                    e.tensor_reduce(neg_max[:, i % 4:i % 4 + 1], region[:, use % 2, 0:self.nkeys], AX, ALU.max,
                                    negate=True).then_inc(self.s("maxed"), 1)

            def move(i):
                if self.nkt > self.split:
                    reach(e, self.tag + "_turned", i + 1)
                    if i >= 2:
                        reach(e, self.tag + "_summed", i - 1)
                    e.tensor_copy(self.prob_t[:, i % 2, self.split:self.nkt],
                                  aux[:, self.split * P:self.nkt * P].rearrange("p (b k) -> p b k", k=P))\
                        .then_inc(self.s("pt_b"), 1)

            def store(i):
                reach(e, self.tag + "_summed", i + 1)
                ch(e.reciprocal(inv_sum[:, i % 4:i % 4 + 1], row_sum[:, i % 4:i % 4 + 1]))
                dst, cols = self.store(i)
                e.tensor_scalar(dst, pv[:, i % 2, cols], inv_sum[:, i % 4:i % 4 + 1], None, ALU.mult)\
                    .then_inc(self.s("stored"), 1)

            for i in range(self.n + 2):
                if i < self.n:
                    maxes(i)
                if 1 <= i <= self.n:
                    move(i - 1)
                if i >= 2:
                    store(i - 2)
                if self.extra:
                    self.extra(e, ch, i)
            reach(e, self.tag + "_stored", self.n)

    def first_key_row(t):
        return 2 * t + SHIFT[VARIANT[t]]

    def na_score(e, i, dst):
        h, t = divmod(i, TT)
        rows = slice(64 * (h % 2), 64 * (h % 2) + 64)
        j, qs, k0 = h // 2, slice(t * P, t * P + P), first_key_row(t) * W_GRID
        e.matmul(dst[:, 0:512], q_rot[rows, j, qs], k_rot[rows, j, k0:k0 + 512], start=True, stop=True)
        e.matmul(dst[:, 512:KEYS], q_rot[rows, j, qs], k_rot[rows, j, k0 + 512:k0 + KEYS], start=True, stop=True)
        return e.matmul(dst[:, KEYS:KEYS + CTX], q_t[rows, j, qs], k_ctx[rows, j], start=True, stop=True)

    def na_v(i, b):
        h, t = divmod(i, TT)
        cols = slice(P * (h // 2), P * (h // 2) + P)
        if b < KEYS // P:
            return v_tok[:, first_key_row(t) // 2 + b, cols]
        return v_ctx[:, b - KEYS // P, cols]

    def head_store(buf):
        def store(i):
            h, t = divmod(i, TT)
            return buf[:, t, h * 64:h * 64 + 64], slice(64 * (h % 2), 64 * (h % 2) + 64)
        return store

    def conv_tap(e, ch, n):
        j, k = divmod(n, TAPS)
        src, w = glu[:, j, k:k + T], sp_("dww", 1, j * TAPS + k)
        if k == 0:
            ch(e.tensor_scalar(conv[:, j], src, w, sp_("dwb", 1, j), ALU.mult, ALU.add))
        else:
            ch(e.scalar_tensor_tensor(out=conv[:, j], in0=src, scalar=w, in1=conv[:, j], op0=ALU.mult, op1=ALU.add))

    def conv_extra(e, ch, i):
        left = 4 * TAPS - 3 * EARLY_TAPS
        tiles = HEADS * TT - 2
        for n in range(left * i // tiles, min(left * (i + 1) // tiles, left)):
            conv_tap(e, ch, 3 * EARLY_TAPS + n)

    na = Attention("na", HEADS, KEYS + CTX, (na_prob, na_prob_t), na_score, na_v, head_store(o_tok),
                   bias=lambda i: bias_t[:, VARIANT[i % TT]], extra=conv_extra)
    na.bias_count = lambda i: 5 * (i // TT) + VARIANT[i % TT] + 1

    def bias_pool(e, pos):
        e.wait_ge(unit_done, UNIT0["u"] + 8)

        def load_toep(h):
            for a in range(2):
                start = (h * 19 + 1 - a) * TABLE * W_GRID + W_GRID - 1
                src = bass.AP(rpb_pad.tensor, start, [[TABLE - 1, W_GRID], [TABLE * W_GRID, 18], [1, W_GRID]])
                e.dma_start(toep[h % 2][a * 64:a * 64 + 64], src).then_inc(sem(f"toep_ld{h % 2}"), 16)

        load_toep(0)
        e.dma_start(mask_t[:].rearrange("p v k -> p (v k)"), mask).then_inc(sem("mask_ld"), 16)
        load_toep(1)
        for v in range(5):
            e.memset(bias_t[:, v, KEYS:], 0.0).then_inc(sem("bias_tail"), 1)
        reach(e, "bias_tail", 5)
        reach(e, "mask_ld", 16)
        for h in range(HEADS):
            reach(e, f"toep_ld{h % 2}", 32 * (h // 2 + 1))
            for v in range(5):
                if h:
                    last_tile = max(t for t in range(TT) if VARIANT[t] == v)
                    reach(e, "na_maxed", TT * (h - 1) + last_tile + 1)
                r0 = SHIFT[v] + 8
                e.tensor_tensor(bias_t[:, v, 0:KEYS].rearrange("p (r c) -> p r c", c=W_GRID),
                                toep[h % 2][:, r0:r0 + 10],
                                mask_t[:, v].rearrange("p (r c) -> p r c", c=W_GRID), ALU.add)\
                    .then_inc(sem("na_bias"), 1)
            if h + 2 < HEADS:
                reach(e, "na_bias", 5 * (h + 1))
                load_toep(h + 2)

    def turn_back_pe(e, pos, tag, src):
        for j in range(4):
            use = pos.next_use()
            wait_region(e, use)
            for t in range(TT):
                last = e.transpose(region[:, use % 2, t * P:(t + 1) * P], src[:, t, j * P:(j + 1) * P], ident[:])
            last.then_inc(sem(f"{tag}_tb"), 1)

    def turn_back_act(e, pos, tag, hi):
        for j in range(4):
            use = pos.next_use()
            reach(e, f"{tag}_tb", j + 1)
            copy(e, hi[:, j], region[:, use % 2]).then_inc(sem(f"{tag}_tbhi"), 1)

    def turn_back_dve(e, pos, tag, hi, lo):
        for j in range(4):
            use = pos.next_use()
            reach(e, f"{tag}_tbhi", j + 1)
            e.tensor_tensor(lo[:, j], region[:, use % 2], hi[:, j].bitcast(F32), ALU.subtract).then_inc(free[use % 2], 1)

    def ln_pe(e, pos):
        for j in range(4):
            for lo in range(0, T, HALF):
                last = e.matmul(aux[:, lo:lo + HALF], ones[:], conv[:, j, lo:lo + HALF], start=(j == 0), stop=(j == 3))
        last.then_inc(sem("ln_sum"), 1)
        reach(e, "ln_dev", 4)
        rms_pe(e, "lnv", 4, T, tmp_b)

    def ln_dve(e, pos, ch):
        reach(e, "ln_sum", 1)
        for j in range(4):
            e.scalar_tensor_tensor(out=conv[:, j], in0=aux[:], scalar=-1.0 / 512, in1=conv[:, j],
                                   op0=ALU.mult, op1=ALU.add).then_inc(sem("ln_dev"), 1)
        rms_dve(e, ch, "lnv", T, tmp_b)
        norm_dve(e, ch, "lnn", 4, T, lambda k: conv[:, k], mix_hi[:, 4:8], mix_lo[:, 4:8], tmp_b)

    def ln_act(e, pos, ch):
        rms_act(e, ch, "lnv", lambda k: conv[:, k], 4, T, 512,
                scale_from_ready=lambda k: reach(e, "ln_dev", k + 1), tmp=tmp_b)
        norm_act(e, ch, "lnn", 4, T, mix_hi[:, 4:8], lambda k: sp_("ln_g", 1, k), lambda k: sp_("ln_b", 1, k), ACT.Silu, tmp_b)

    def out1_pe(e, pos):
        start_pair(e, pos, UNIT0["out1"], mix_hi, mix_lo, lambda k: reach(e, "lnn_lo", k - 3) if k >= 4 else None)
        for j in range(2, 8):
            use = pos.next_use()
            project(e, use, UNIT0["out1"] + j, mix_hi, mix_lo, KD).then_inc(unit_done, 1)

    def out1_dve(e, pos, ch):
        reach(e, "x_again", 16)
        for j in range(8):
            use = pos.next_use()
            e.wait_ge(unit_done, UNIT0["out1"] + j + 1)
            e.scalar_tensor_tensor(out=x1[:, j], in0=region[:, use % 2], scalar=mod_x[:, 16 + j:17 + j],
                                   in1=x1[:, j], op0=ALU.mult, op1=ALU.add).then_inc(free[use % 2], 1)
            e.wait_ge(free[use % 2], use // 2 + 1)
            if j:
                reach(e, "r2_sq", j + 1)
                if j >= 2:
                    reach(e, "r2_acc", j - 1)
                e.tensor_tensor(tmp[:, 2], tmp[:, 2], tmp[:, j % 2], ALU.add).then_inc(sem("r2_acc"), 1)

    def out1_act(e, pos, ch):
        for j in range(8):
            use = pos.next_use()
            e.wait_ge(free[use % 2], use // 2 + 1)
            if j >= 3:
                reach(e, "r2_acc", j - 2)
            e.activation(tmp[:, j % 2] if j else tmp[:, 2], x1[:, j], ACT.Square).then_inc(sem("r2_sq"), 1)

    def sum_pe(e, src, dst):
        for lo in range(0, T, HALF):
            last = e.matmul(dst(lo), ones[:], src[:, lo:lo + HALF], start=True, stop=True)
        return last

    def r2_pe(e, pos):
        reach(e, "r2_acc", KD - 1)
        sum_pe(e, tmp[:, 2], lambda lo: aux[:, lo:lo + HALF]).then_inc(sem("r2_sqmm"), 1)

    def mlp_pe(e, pos):
        u0, c0 = UNIT0["mlp"], pos.use
        assert c0 % 2 == 0 and u0 % 2 == 0
        with e.Fori(0, FF_GROUPS) as g:
            def arrive(n):
                e.wait_ge(unit_split, g * 16 + (u0 + n + 1))
                e.wait_ge(free[n % 2], g * 8 + (c0 + n) // 2)

            def unit(n, xh, xl):
                r = s = n % 2
                arrive(n)
                for lo in (0, HALF):
                    for k in range(KD):
                        w = slice(k * P, k * P + P)
                        last = mm3(e, region[:, r, lo:lo + HALF], w_hi[:, s, w], w_lo[:, s, w],
                                   xh[:, k, lo:lo + HALF], xl[:, k, lo:lo + HALF], k == 0, k == KD - 1)
                last.then_inc(unit_done, 1)
            project_pair(e, arrive, h2_hi, h2_lo, lambda k: reach(e, "n2_lo", k + 1))
            for f in range(2, KD):
                unit(f, h2_hi, h2_lo)
            project_pair(e, lambda n: arrive(KD + n), ff_hi, ff_lo, lambda k: reach(e, "ff_lo", g * 8 + (k + 1)), LATE_LAST)
            for d in range(2, KD):
                unit(KD + d, ff_hi, ff_lo)
        pos.use += 16 * FF_GROUPS

    def mlp_act(e, pos, ch):
        u0, c0 = UNIT0["mlp"], pos.use
        with e.Fori(0, FF_GROUPS) as g:
            def hi(f):
                reach(e, "ff_sq", g * 8 + (f + 1))
                copy(e, ff_hi[:, f], tmp[:, 2 + f % 2]).then_inc(sem("ff_hi"), 1)

            for f in range(KD):
                e.wait_ge(unit_done, g * 16 + (u0 + f + 1))
                if f >= 2:
                    reach(e, "ff_sq", g * 8 + (f - 1))
                else:
                    reach(e, "nf_acc", g * 14 + 1)
                e.activation(tmp[:, f % 2], region[:, f % 2], ACT.Relu).then_inc(free[f % 2], 1)
                if f:
                    hi(f - 1)
            hi(KD - 1)
            for d in range(KD):
                e.wait_ge(free[d % 2], g * 8 + (c0 + KD + d) // 2 + 1)
                if d:
                    reach(e, "nf_acc", g * 14 + (2 * d - 1))
                else:
                    reach(e, "ff_lo", g * 8 + 8)
                e.activation(tmp[:, 0 if d else 2], x1[:, d], ACT.Square).then_inc(sem("nf_sq"), 1)
                e.activation(tmp[:, 1 if d else 3], x1[:, d], ACT.Square, scale=sp_("final", 1, d)).then_inc(sem("nf_sq"), 1)
        pos.use += 16 * FF_GROUPS

    def mlp_dve(e, pos, ch):
        u0, c0 = UNIT0["mlp"], pos.use
        e.sem_inc(sem("nf_acc"), 1)
        with e.Fori(0, FF_GROUPS) as g:
            def low(f):
                reach(e, "ff_hi", g * 8 + (f + 1))
                e.tensor_tensor(ff_lo[:, f], tmp[:, 2 + f % 2], ff_hi[:, f].bitcast(F32), ALU.subtract)\
                    .then_inc(sem("ff_lo"), 1)

            for f in range(KD):
                e.wait_ge(free[f % 2], g * 8 + (c0 + f) // 2 + 1)
                if f >= 2:
                    reach(e, "ff_lo", g * 8 + (f - 1))
                e.tensor_tensor(tmp[:, 2 + f % 2], tmp[:, f % 2], tmp[:, f % 2], ALU.mult).then_inc(sem("ff_sq"), 1)
                if f:
                    low(f - 1)
            low(KD - 1)
            for d in range(KD):
                e.wait_ge(unit_done, g * 16 + (u0 + KD + d + 1))
                e.scalar_tensor_tensor(out=x1[:, d], in0=region[:, d % 2], scalar=mod_x[:, 40 + d:41 + d],
                                       in1=x1[:, d], op0=ALU.mult, op1=ALU.add).then_inc(free[d % 2], 1)
                e.wait_ge(free[d % 2], g * 8 + (c0 + KD + d) // 2 + 1)
                if d:
                    for i in range(2):
                        reach(e, "nf_sq", g * 16 + (2 * d + 1 + i))
                        if d >= 2:
                            reach(e, "nf_acc", g * 14 + (2 * d - 2 + i))
                        e.tensor_tensor(tmp[:, 2 + i], tmp[:, 2 + i], tmp[:, i], ALU.add).then_inc(sem("nf_acc"), 1)
            reach(e, "nf_acc", g * 14 + 15)
        pos.use += 16 * FF_GROUPS

    def nf_pe(e, pos):
        reach(e, "nf_acc", 14 * FF_GROUPS + 1)
        sum_pe(e, tmp[:, 2], lambda lo: aux[:, lo:lo + HALF]).then_inc(sem("nf_sqmm"), 1)
        sum_pe(e, tmp[:, 3], lambda lo: pv[:, lo // HALF]).then_inc(sem("nf_sqmm"), 1)

    def nf_dve(e, pos, ch):
        reach(e, "nf_sqmm", 1)
        e.tensor_scalar(tmp[:, 0], aux[:], 1.0 / D, EPS, ALU.mult, ALU.add).then_inc(sem("nf_a"), 1)
        reach(e, "nf_a", 1)
        reach(e, "nf_sqmm", 2)
        e.scalar_tensor_tensor(out=tmp[:, 3], in0=tmp[:, 0], scalar=EPS * D, in1=pv[:].rearrange("p a b -> p (a b)"),
                               op0=ALU.mult, op1=ALU.add).then_inc(sem("nf_b"), 1)
        inverse_dve(e, "nf", 1, tmp[:, 3])
        reach(e, "rs1_root", 1)

    def nf_act(e, pos, ch):
        reach(e, "nf_acc", 14 * FF_GROUPS + 1)
        e.dma_start(x_spill, x1[:]).then_inc(sem("spill"), 16)
        reach(e, "nf_b", 1)
        e.activation(tmp[:, 3], tmp[:, 3], ACT.Sqrt, scale=1.0 / D).then_inc(sem("nf_root"), 1)
        e.activation(rs1[:], tmp[:, 0], ACT.Sqrt).then_inc(sem("rs1_root"), 1)

    RR = slice(NOPE, P)
    LATS = NQL + NKVL

    def lat_pe(e, pos):
        def sums(i):
            reach(e, "lat_sq", i + 1)
            for lo in range(0, T, HALF):
                dst = aux[:, lo:lo + HALF] if i < NQL else pv[:, lo // HALF]
                last = e.matmul(dst, ones[:], lat_sq[:, i % 2, lo:lo + HALF], start=(i in (0, NQL)), stop=(i in (NQL - 1, LATS - 1)))
            last.then_inc(sem("lat_mm"), 1)

        start_pair(e, pos, UNIT0["lat"], h2_hi, h2_lo, lambda k: reach(e, "n3_lo", k + 1))
        for j in range(2, 1 + LATS):
            use = pos.next_use()
            project(e, use, UNIT0["lat"] + j, h2_hi, h2_lo, KD).then_inc(unit_done, 1)
            if j >= 2:
                sums(j - 2)
        sums(LATS - 1)

    def lat_act(e, pos, ch):
        def table(which, dst):
            reach(e, "angle", which + 1)
            e.activation(dst[RR], tmp[RR, 2], ACT.Sin).then_inc(sem("table"), 1)

        use = pos.next_use()
        e.wait_ge(unit_done, UNIT0["lat"] + 1)
        reach(e, "spill", 16)
        copy(e, k_pe[RR], region[RR, use % 2]).then_inc(free[use % 2], 1)
        table(0, sin2)
        for i in range(LATS):
            use = pos.next_use()
            e.wait_ge(unit_done, UNIT0["lat"] + i + 2)
            dst = q_lat[:, i] if i < NQL else kv_lat[:, i - NQL]
            copy(e, dst, region[:, use % 2]).then_inc(free[use % 2], 1)
            e.wait_ge(free[use % 2], use // 2 + 1)
            if i >= 2:
                reach(e, "lat_mm", i - 1)
            e.activation(lat_sq[:, i % 2], dst, ACT.Square).then_inc(sem("lat_sq"), 1)
            if i == 0:
                table(1, cos2)
            if i == NQL:
                reach(e, "lat_mm", NQL)
                root_act(e, "rq", tmp[:, 3], aux[:], P * NQL, eps_col)
        norm_act(e, ch, "nq", NQL, T, ql_hi, lambda k: sp_("qn", 1, k), None)
        reach(e, "lat_mm", LATS)
        root_act(e, "rk", tmp[:, 2], pv[:].rearrange("p a b -> p (a b)"), P * NKVL, eps_col)
        norm_act(e, ch, "nk", NKVL, T, kvl_hi, lambda k: sp_("kvn", 1, k), None)

    def lat_dve(e, pos, ch):
        r = RR
        ch(e.reciprocal(rs1[:], rs1[:]))
        e.sem_inc(sem("rs1_ready"), 1)
        reach(e, "pos_ld", 16)
        ch(e.tensor_copy(tmp[r, 0], pos_i[r]))
        ch(e.tensor_scalar(tmp[r, 0], tmp[r, 0], par[r, SMALL["invf"]:SMALL["invf"] + 1], None, ALU.mult))
        c1 = 6.28125
        c2 = float(np.float32(np.round((TWO_PI - c1) * 2 ** 21) / 2 ** 21))
        c3 = float(TWO_PI - c1 - c2)
        magic = 1.5 * 2 ** 23
        for which, (quarter, shift) in enumerate([(0.0, 0.0), (0.25, np.pi / 2)]):
            ch(e.tensor_scalar(tmp[r, 1], tmp[r, 0], 1.0 / TWO_PI, quarter, ALU.mult, ALU.add))
            ch(e.tensor_scalar(tmp[r, 1], tmp[r, 1], magic, magic, ALU.add, ALU.subtract))
            if which:
                reach(e, "table", 1)
            ch(e.scalar_tensor_tensor(out=tmp[r, 2], in0=tmp[r, 1], scalar=-c1, in1=tmp[r, 0], op0=ALU.mult, op1=ALU.add))
            ch(e.scalar_tensor_tensor(out=tmp[r, 2], in0=tmp[r, 1], scalar=-c2, in1=tmp[r, 2], op0=ALU.mult, op1=ALU.add))
            ch(e.scalar_tensor_tensor(out=tmp[r, 2], in0=tmp[r, 1], scalar=-c3, in1=tmp[r, 2], op0=ALU.mult, op1=ALU.add))
            ch(e.tensor_scalar(tmp[r, 2], tmp[r, 2], shift, 3.1415925, ALU.add, ALU.min))
            e.tensor_scalar(tmp[r, 2], tmp[r, 2], -3.1415925, None, ALU.max).then_inc(sem("angle"), 1)
        reach(e, "angle", 2)
        reach(e, "table", 1)
        ch(e.tensor_scalar(sin2[r], sin2[r], par[r, SMALL["sign"]:SMALL["sign"] + 1], None, ALU.mult))
        reach(e, "table", 2)
        ch(e.tensor_scalar(k_turned[r], k_pe[r], sp_("khr")[r], None, ALU.mult))
        ch(e.stream_shuffle(tmp[r, 0], k_turned[r], SWAP))
        ch(e.tensor_tensor(tmp[r, 0], tmp[r, 0], sin2[r], ALU.mult))
        ch(e.tensor_tensor(k_turned[r], k_turned[r], cos2[r], ALU.mult))
        ch(e.tensor_tensor(k_turned[r], k_turned[r], tmp[r, 0], ALU.add))
        ch(e.memset(cos2[0:NOPE], 1.0))
        ch(e.tensor_copy(cos2[QK:P], sin2[QK:P]))
        inverse_dve(e, "rq", 1, tmp[:, 3])
        norm_dve(e, ch, "nq", NQL, T, lambda k: q_lat[:, k], ql_hi, ql_lo)
        inverse_dve(e, "rk", 1, tmp[:, 2])
        norm_dve(e, ch, "nk", NKVL, T, lambda k: kv_lat[:, k], kvl_hi, kvl_lo, rs=2)

    class Heads:

        def __init__(self, tag, units, x, nk, per_unit, heads, m, rows, from_psum, width, rs, ready=None):
            self.tag, self.units, self.x, self.nk, self.per_unit, self.m = tag, UNIT0[units], x, nk, per_unit, m
            self.heads, self.rows, self.from_psum, self.width, self.rs = heads, rows, from_psum, width, rs
            self.ready = ready

        def last_of_unit(self, h):
            return h % self.per_unit == self.per_unit - 1 or h == self.heads - 1

        def pe(self, e, pos):
            tag, rows, width, m = self.tag, self.rows, self.width, self.m

            def sums(h):
                reach(e, f"{tag}_sq", h + 1)
                if h or tag != "hq":
                    reach(e, f"{tag}_root", h)
                for lo in range(0, width, HALF):
                    n = min(HALF, width - lo)
                    last = e.matmul(aux[:, lo:lo + n], ones[0:rows], tmp[0:rows, 2 + h % 2, lo:lo + n],
                                    start=True, stop=True)
                last.then_inc(sem(f"{tag}_ss"), 1)

            for h in range(self.heads):
                use = pos.next_use()
                last = project(e, use, self.units + h // self.per_unit, *self.x, self.nk, width=width, m=m,
                               off=(h % self.per_unit) * self.nk * m, step=m,
                               wait_k=(lambda k: self.ready(e, k)) if self.ready and h == 0 else None)
                last.then_inc(unit_done if self.last_of_unit(h) else sem(f"{tag}_part"), 1)
                if h:
                    sums(h - 1)
            sums(self.heads - 1)

        def act(self, e, pos, ch):
            tag, rows, width = self.tag, self.rows, self.width
            parts = 0

            def scale(h):
                reach(e, f"{tag}_ss", h + 1)
                if h >= 2:
                    reach(e, f"{tag}_sc", h - 1)
                root_act(e, tag, self.rs[:, h % 2, 0:width], aux[:, 0:width], rows, eps_col)

            for h in range(self.heads):
                use = pos.next_use()
                if self.last_of_unit(h):
                    e.wait_ge(unit_done, self.units + h // self.per_unit + 1)
                else:
                    parts += 1
                    reach(e, f"{tag}_part", parts)
                if h >= 2:
                    reach(e, f"{tag}_sc", h - 1)
                    reach(e, f"{tag}_ss", h - 1)
                n = self.from_psum
                s = min(n, rows)
                copy(e, tmp[0:n, h % 2, 0:width], region[0:n, use % 2, 0:width]).then_inc(free[use % 2], 1)
                e.wait_ge(free[use % 2], use // 2 + 1)
                e.activation(tmp[0:s, 2 + h % 2, 0:width], tmp[0:s, h % 2, 0:width], ACT.Square).then_inc(sem(f"{tag}_sq"), 1)
                if h + 1 < self.heads:
                    scale(h)
            scale(self.heads - 1)

        def dve(self, e, pos, ch, dst, gain, table=None):
            tag, width = self.tag, self.width
            for h in range(self.heads):
                pos.next_use()
                inverse_dve(e, tag, h + 1, self.rs[:, h % 2, 0:width])
                e.scalar_tensor_tensor(out=dst[:, h, 0:width], in0=tmp[:, h % 2, 0:width], scalar=gain,
                                       in1=self.rs[:, h % 2, 0:width], op0=ALU.mult, op1=ALU.mult)\
                    .then_inc(sem(f"{tag}_sc"), 1)
                reach(e, f"{tag}_sc", h + 1)
                if table is not None:
                    ch(e.tensor_tensor(dst[:, h], dst[:, h], table, ALU.mult))

    rs_h = place("rs_h", [2, T], 128)
    q_heads = Heads("hq", "uq", (ql_hi, ql_lo), NQL, 2, HEADS, P, QK, P, T, rs_h,
                    ready=lambda e, k: reach(e, "nq_lo", k + 1))
    k_heads = Heads("hk", "uk", (kvl_hi, kvl_lo), NKVL, 3, HEADS, QK, QK, NOPE, T, rs_h,
                    ready=lambda e, k: reach(e, "nk_lo", k + 1))

    def hk_act(e, pos, ch):
        for i in range(2):
            e.activation(tmp[NOPE:QK, 2 + i], k_pe[NOPE:QK], ACT.Square).then_inc(sem("kpe_sq"), 1)
        reach(e, "kpe_sq", 2)
        k_heads.act(e, pos, ch)

    def hk_dve(e, pos, ch):
        for i in range(2):
            ch(e.tensor_copy(tmp[RR, i], k_turned[RR]))
        k_heads.dve(e, pos, ch, k_h, sp_("kh"))

    def uv_pe(e, pos):
        e.wait_ge(unit_split, UNIT0["uv"] + 1)
        s = UNIT0["uv"] % 2
        for g in range(4):
            use = pos.next_use()
            last = project_tokens(e, use, None, kvl_hi, kvl_lo, NKVL, range(2 * g, 2 * g + 2), HALF,
                                  lambda w, k: w[:, s, k * HALF:(k + 1) * HALF])
            last.then_inc(unit_done if g == 3 else sem("uv_part"), 1)

    def uv_act(e, pos, ch):
        for g in range(4):
            use = pos.next_use()
            if g < 3:
                reach(e, "uv_part", g + 1)
            else:
                e.wait_ge(unit_done, UNIT0["uv"] + 1)
            copy(e, v2[:, 2 * g:2 * g + 2], region[:, use % 2].rearrange("p (t c) -> p t c", c=HALF))\
                .then_inc(free[use % 2], 1)

    def mla_score(e, i, dst):
        h, t = divmod(i, TT)
        for lo in (0, HALF):
            last = e.matmul(dst[:, lo:lo + HALF], q_h[:, h, t * P:(t + 1) * P], k_h[:, h, lo:lo + HALF],
                            start=True, stop=True)
        return last

    mla = Attention("mla", HEADS, T, (prob, prob_t), mla_score,
                    lambda i, b: v2[:, b, P * (i // TT // 2):P * (i // TT // 2) + P], head_store(o_tok2))

    def gate_pe(e, pos, tag, units, src):
        for j in range(4):
            if j:
                reach(e, f"{tag}_gated", j)
            for t in range(TT):
                last = e.transpose(aux[:, t * P:(t + 1) * P], src[:, t, j * P:(j + 1) * P], ident[:])
            last.then_inc(sem(f"{tag}_tb"), 1)
            use = pos.next_use()
            project(e, use, UNIT0[units] + j, h2_hi, h2_lo, KD).then_inc(unit_done, 1)

    def gate_act(e, pos, ch, tag, units):
        for j in range(4):
            use = pos.next_use()
            e.wait_ge(unit_done, UNIT0[units] + j + 1)
            if j >= 2:
                reach(e, f"{tag}_gated", j - 1)
            e.activation(tmp[:, j % 2], region[:, use % 2], ACT.Silu).then_inc(free[use % 2], 1)
            reach(e, f"{tag}_gated", j + 1)
            copy(e, o_hi[:, j], tmp[:, 2 + j % 2]).then_inc(sem(f"{tag}_hi"), 1)

    def gate_dve(e, pos, ch, tag):
        for j in range(4):
            use = pos.next_use()
            e.wait_ge(free[use % 2], use // 2 + 1)
            reach(e, f"{tag}_tb", j + 1)
            e.tensor_tensor(tmp[:, 2 + j % 2], aux[:], tmp[:, j % 2], ALU.mult).then_inc(sem(f"{tag}_gated"), 1)
            reach(e, f"{tag}_hi", j + 1)
            e.tensor_tensor(o_lo[:, j], tmp[:, 2 + j % 2], o_hi[:, j].bitcast(F32), ALU.subtract).then_inc(sem(f"{tag}_lo"), 1)
        reach(e, f"{tag}_lo", 4)

    def branch_pe(e, pos, b, lo_tag):
        u0 = UNIT0[f"br{b}"]
        for p in range(4):
            for dd in range(2):
                use = pos.next_use()
                project(e, use, u0 + 3 * p + dd, h2_hi, h2_lo, KD).then_inc(unit_done, 1)
            for dd in range(2):
                use = pos.next_use()
                last = project(e, use, u0 + 3 * p + 2, o_hi, o_lo, 4, off=dd * HALF,
                               wait_k=(lambda k: reach(e, lo_tag, k + 1)) if p == dd == 0 else None)
                last.then_inc(unit_done if dd else sem(f"br{b}_part"), 1)

    def branch_act(e, pos, ch, b):
        u0 = UNIT0[f"br{b}"]
        for p in range(4):
            for dd in range(2):
                use = pos.next_use()
                e.wait_ge(unit_done, u0 + 3 * p + dd + 1)
                if p:
                    reach(e, f"br{b}_used", 2 * (p - 1) + dd + 1)
                e.activation(tmp[:, dd], region[:, use % 2], ACT.Sigmoid, bias=sp_("b_gate", 1, 8 * b + 2 * p + dd))\
                    .then_inc(free[use % 2], 1)
            pos.next_use(), pos.next_use()

    def branch_dve(e, pos, ch, b):
        u0 = UNIT0[f"br{b}"]
        for p in range(4):
            gates = [pos.next_use(), pos.next_use()]
            for dd in range(2):
                use = pos.next_use()
                e.wait_ge(free[gates[dd] % 2], gates[dd] // 2 + 1)
                if dd:
                    e.wait_ge(unit_done, u0 + 3 * p + 3)
                else:
                    reach(e, f"br{b}_part", p + 1)
                d = 2 * p + dd
                dst = tmp[:, 2 + dd] if b else y[:, d]
                if b and p:
                    reach(e, f"br{b}_used", 2 * (p - 1) + dd + 1)
                e.tensor_tensor(dst, region[:, use % 2], tmp[:, dd], ALU.mult).then_inc(free[use % 2], 1)
                e.wait_ge(free[use % 2], use // 2 + 1)
                if b:
                    e.tensor_tensor(y[:, d], y[:, d], dst, ALU.add).then_inc(sem(f"br{b}_used"), 1)
                else:
                    e.sem_inc(sem(f"br{b}_used"), 1)
        if b:
            reach(e, f"br{b}_used", 8)

    def cv_pe(e, pos):
        for j in range(16):
            use = pos.next_use()
            project(e, use, UNIT0["cv"] + j, h2_hi, h2_lo, KD).then_inc(unit_done, 1)

    def cv_act(e, pos, ch):
        for j in range(4):
            u = UNIT0["cv"] + 4 * j
            use = pos.next_use()
            e.wait_ge(unit_done, u + 1)
            if j:
                reach(e, "cv_z", j)
            copy(e, tmp[:, 0], region[:, use % 2]).then_inc(free[use % 2], 1)
            pos.next_use(), pos.next_use()
            use = pos.next_use()
            e.wait_ge(unit_done, u + 4)
            if j:
                reach(e, "cv_o", j)
            e.activation(tmp[:, 2], region[:, use % 2], ACT.Silu).then_inc(free[use % 2], 1)
            reach(e, "cv_o", j + 1)
            copy(e, o_hi[:, j], tmp[:, 3]).then_inc(sem("cv_hi"), 1)

    def cv_dve(e, pos, ch):
        ch(e.memset(z_pad[:, 0:1], 0.0))
        ch(e.memset(z_pad[:, T + 1:T + 2], 0.0))
        for j in range(4):
            u = UNIT0["cv"] + 4 * j
            w = lambda k: sp_("cw", 1, 3 * j + k)
            use = pos.next_use()
            e.wait_ge(free[use % 2], use // 2 + 1)
            use = pos.next_use()
            e.wait_ge(unit_done, u + 2)
            e.tensor_tensor(z_pad[:, 1:T + 1], region[:, use % 2], tmp[:, 0], ALU.mult).then_inc(free[use % 2], 1)
            e.wait_ge(free[use % 2], use // 2 + 1)
            e.sem_inc(sem("cv_z"), 1)
            ch(e.tensor_scalar(tmp[:, 1], z_pad[:, 0:T], w(0), sp_("cb", 1, j), ALU.mult, ALU.add))
            for k in (1, 2):
                ch(e.scalar_tensor_tensor(out=tmp[:, 1], in0=z_pad[:, k:k + T], scalar=w(k), in1=tmp[:, 1],
                                          op0=ALU.mult, op1=ALU.add))
            use = pos.next_use()
            e.wait_ge(unit_done, u + 3)
            e.tensor_tensor(tmp[:, 1], region[:, use % 2], tmp[:, 1], ALU.mult).then_inc(free[use % 2], 1)
            e.wait_ge(free[use % 2], use // 2 + 1)
            use = pos.next_use()
            e.wait_ge(free[use % 2], use // 2 + 1)
            if j:
                reach(e, "cv_lo", j)
            e.tensor_tensor(tmp[:, 3], tmp[:, 1], tmp[:, 2], ALU.mult).then_inc(sem("cv_o"), 1)
            reach(e, "cv_hi", j + 1)
            e.tensor_tensor(o_lo[:, j], tmp[:, 3], o_hi[:, j].bitcast(F32), ALU.subtract).then_inc(sem("cv_lo"), 1)
        reach(e, "cv_lo", 4)

    rs_m = place("rs_m", [2, T], 137)
    mk_heads = Heads("mk", "mkv", (hm_hi, hm_lo), KD, 1, MH, P, P, P, CTX, place("rs_mk", [2, CTX], 161),
                     ready=lambda e, k: reach(e, "nm_lo", k + 1))
    qm_heads = Heads("qm", "qm", (h2_hi, h2_lo), KD, 1, MH, P, P, P, T, rs_m)

    def mv_pe(e, pos):
        for p in range(2):
            use = pos.next_use()
            u = UNIT0["mkv"] + 4 + 2 * p
            assert u % 2 == 0
            e.wait_ge(unit_split, u + 2)
            project_tokens(e, use, None, hm_hi, hm_lo, KD, range(2), 256,
                           lambda w, k: w[:, 0:2, k * P:(k + 1) * P]).then_inc(unit_done, 2)

    def mv_act(e, pos):
        for p in range(2):
            use = pos.next_use()
            e.wait_ge(unit_done, UNIT0["mkv"] + 6 + 2 * p)
            copy(e, m_v[:, :, 256 * p:256 * p + 256],
                 region[:, use % 2, 0:512].rearrange("p (t c) -> p t c", c=256)).then_inc(free[use % 2], 1)

    def mem_score(e, i, dst):
        h, t = divmod(i, TT)
        return e.matmul(dst[:, 0:CTX], q_mem[:, h, t * P:(t + 1) * P], m_k[:, h], start=True, stop=True)

    mem_att = Attention("ma", MH, CTX, (prob, prob_t), mem_score, lambda i, b: m_v[:, b, P * (i // TT):P * (i // TT) + P],
                        lambda i: (o_mem[:, i % TT, P * (i // TT):P * (i // TT) + P], slice(0, P)))

    def out2_pe(e, pos):
        start_pair(e, pos, UNIT0["out2"], y_hi, y_lo, lambda k: reach(e, "y_lo", k + 1))
        for j in range(2, 8):
            use = pos.next_use()
            project(e, use, UNIT0["out2"] + j, y_hi, y_lo, KD).then_inc(unit_done, 1)

    def x3_dve(e, pos, ch):
        reach(e, "x3_ld", 32)
        for j in range(KD):
            ch(e.scalar_tensor_tensor(out=x3[:, j], in0=x3[:, j], scalar=sp_("final", 1, j), in1=rs1_again[:],
                                      op0=ALU.mult, op1=ALU.mult))

    def out2_act(e, pos, ch):
        for k in range(KD):
            copy(e, y_hi[:, k], y[:, k]).then_inc(sem("y_hi"), 1)

    def out2_dve(e, pos, ch):
        for k in range(KD):
            reach(e, "y_hi", k + 1)
            e.tensor_tensor(y_lo[:, k], y[:, k], y_hi[:, k].bitcast(F32), ALU.subtract).then_inc(sem("y_lo"), 1)
        for j in range(8):
            use = pos.next_use()
            e.wait_ge(unit_done, UNIT0["out2"] + j + 1)
            e.tensor_tensor(x3[:, j], region[:, use % 2], x3[:, j], ALU.add).then_inc(sem("out_ready"), 1)
            reach(e, "out_ready", j + 1)
            e.sem_inc(free[use % 2], 1)

    with nc.Block() as block:
        @block.sync
        def _(sp):
            def load(u, s):
                sp.dma_start(w_raw[:, s], units[u]).then_inc(raw_loaded[s], 16)

            sp.dma_start(par[:], small).then_inc(sem("small_ld"), 16)
            load(0, 0)
            load(1, 1)
            ada_sp(sp, None)
            with sp.Fori(1, N_UNITS // 2) as i:
                for s in range(2):
                    sp.wait_ge(unit_split, i * 2 + (s - 1))
                    sp.dma_start(w_raw[:, s], units[i * 2 + s]).then_inc(raw_loaded[s], 16)
            for j in range(KD):
                reach(sp, "out_ready", j + 1)
                sp.dma_start(out[:, j], x3[:, j]).then_inc(sem("out_st"), 16)
            reach(sp, "out_st", 16 * KD)

        @block.gpsimd
        def _(pool):
            def split(i, s):
                pool.wait_ge(raw_loaded[s], i * 16 + 16)
                pool.tensor_tensor(w_hi[:, s], w_raw[:, s], one_col.broadcast_to([P, 1024]), ALU.mult)\
                    .then_inc(sem("hi_split"), 1)
                reach(pool, "hi_split", i * 2 + (s + 1))
                pool.tensor_tensor(w_lo[:, s], w_raw[:, s], w_hi[:, s].bitcast(F32), ALU.subtract)\
                    .then_inc(unit_split, 1)

            def split_range(a, b):
                with pool.Fori(a // 2, b // 2) as i:
                    for s in range(2):
                        pool.wait_ge(unit_done, i * 2 + (s - 1))
                        split(i, s)

            pool.memset(one_col, 1.0).then_inc(sem("consts"), 1)
            pool.memset(ones[:], 1.0).then_inc(sem("consts"), 1)
            pool.memset(ident[:], 0.0).then_inc(sem("consts"), 1)
            reach(pool, "consts", 3)
            pool.affine_select(out=ident[:], in_=ident[:], compare_op=ALU.not_equal, fill=1.0, base=0,
                               pattern=[[-1, P]], channel_multiplier=1).then_inc(sem("consts"), 1)
            split(0, 0)
            split(0, 1)
            split_range(2, ATTN_SPLIT)
            bias_pool(pool, None)
            split_range(ATTN_SPLIT, N_UNITS)

        @block.scalar
        def _(act):
            pos = Pos()
            ch = Chain(act, "scalar_step")
            act.dma_start(ctx_sb[:], ctx_t).then_inc(sem("ctx_ld"), 16)
            act.dma_start(x_sb[:], x_t).then_inc(sem("x_ld"), 16)
            ada_act(act, pos, ch)
            reach(act, "ctx_ld", 16)
            meet(act, pos)
            rms_act(act, ch, "rc", lambda k: ctx_sb[:, k], KD, CTX, D)
            norm_act(act, ch, "nc", KD, CTX, hc_hi, lambda k: a1c[:, k:k + 1], lambda k: mod_c[:, k:k + 1])
            reach(act, "x_ld", 16)
            meet(act, pos)
            act.dma_start(sin1[:], rope_s).then_inc(sem("rope1_ld"), 16)
            act.dma_start(cos1[:], rope_c).then_inc(sem("rope1_ld"), 16)
            rms_act(act, ch, "r1", lambda k: x_sb[:, k], KD, T, D)
            norm_act(act, ch, "n1", KD, T, h_hi, lambda k: a1[:, k:k + 1], lambda k: mod_x[:, k:k + 1])
            meet(act, pos)
            proj1_act(act, pos, ch)
            meet(act, pos, 3)
            na.act(act, pos, ch)
            meet(act, pos, 3)
            act.dma_start(x1[:], x_t).then_inc(sem("x_again"), 16)
            act.dma_start(pos_i[RR], positions.partition_broadcast(P - NOPE)).then_inc(sem("pos_ld"), 16)
            turn_back_act(act, pos, "nt", mix_hi)
            ln_act(act, pos, ch)
            meet(act, pos, 3)
            out1_act(act, pos, ch)
            reach(act, "r2_sqmm", 1)
            root_act(act, "r2", tmp[:, 3], aux[:], D, eps_col)
            norm_act(act, ch, "n2", KD, T, h2_hi, lambda k: a2[:, k:k + 1], lambda k: mod_x[:, 24 + k:25 + k])
            mlp_act(act, pos, ch)
            nf_act(act, pos, ch)
            norm_act(act, ch, "n3", KD, T, h2_hi, lambda k: both_g[:, k:k + 1], None)
            lat_act(act, pos, ch)
            reach(act, "rs1_ready", 1)
            act.dma_start(rs_spill, rs1[0:1]).then_inc(sem("rs1_spill"), 16)
            reach(act, "rs1_spill", 16)
            meet(act, pos)
            q_heads.act(act, pos, ch)
            meet(act, pos)
            hk_act(act, pos, ch)
            meet(act, pos)
            uv_act(act, pos, ch)
            meet(act, pos, 3)
            mla.act(act, pos, ch)
            meet(act, pos, 3)
            gate_act(act, pos, ch, "ga", "gattn")
            meet(act, pos, 3)
            branch_act(act, pos, ch, 0)
            act.dma_start(mem_sb[:], mem_t).then_inc(sem("mem_ld"), 16)
            meet(act, pos, 3)
            cv_act(act, pos, ch)
            meet(act, pos, 3)
            branch_act(act, pos, ch, 1)
            reach(act, "mem_ld", 16)
            meet(act, pos, 3)
            rms_act(act, ch, "rm", lambda k: mem_sb[:, k], KD, CTX, D)
            norm_act(act, ch, "nm", KD, CTX, hm_hi, lambda k: sp_("memn", 1, k), None)
            meet(act, pos, 3)
            mk_heads.act(act, pos, ch)
            mv_act(act, pos)
            meet(act, pos, 3)
            qm_heads.act(act, pos, ch)
            meet(act, pos, 3)
            mem_att.act(act, pos, ch)
            meet(act, pos, 3)
            gate_act(act, pos, ch, "gm", "gmem")
            meet(act, pos, 3)
            act.dma_start(x3[:], x_spill).then_inc(sem("x3_ld"), 16)
            act.dma_start(rs1_again[:], rs_spill.rearrange("a t -> (a t)").partition_broadcast(P)).then_inc(sem("x3_ld"), 16)
            branch_act(act, pos, ch, 2)
            meet(act, pos, 3)
            out2_act(act, pos, ch)

        @block.vector
        def _(dve):
            pos = Pos()
            ch = Chain(dve, "vector_step")
            ada_dve(dve, pos, ch)
            meet(dve, pos)
            rms_dve(dve, ch, "rc", CTX)
            norm_dve(dve, ch, "nc", KD, CTX, lambda k: ctx_sb[:, k], hc_hi, hc_lo)
            meet(dve, pos)
            rms_dve(dve, ch, "r1", T)
            norm_dve(dve, ch, "n1", KD, T, lambda k: x_sb[:, k], h_hi, h_lo)
            meet(dve, pos)
            proj1_dve(dve, pos, ch)
            meet(dve, pos, 3)
            na.dve(dve, pos, ch)
            meet(dve, pos, 3)
            turn_back_dve(dve, pos, "nt", mix_hi, mix_lo)
            ln_dve(dve, pos, ch)
            meet(dve, pos, 3)
            out1_dve(dve, pos, ch)
            rms_dve(dve, ch, "r2", T)
            norm_dve(dve, ch, "n2", KD, T, lambda k: x1[:, k], h2_hi, h2_lo)
            mlp_dve(dve, pos, ch)
            nf_dve(dve, pos, ch)
            norm_dve(dve, ch, "n3", KD, T, lambda k: x1[:, k], h2_hi, h2_lo)
            for _ in range(6):
                pos.next_use()
            lat_dve(dve, pos, ch)
            meet(dve, pos)
            q_heads.dve(dve, pos, ch, q_h, qh_s, cos2[:])
            meet(dve, pos)
            hk_dve(dve, pos, ch)
            meet(dve, pos)
            for _ in range(4):
                pos.next_use()
            meet(dve, pos, 3)
            mla.dve(dve, pos, ch)
            meet(dve, pos, 3)
            gate_dve(dve, pos, ch, "ga")
            meet(dve, pos, 3)
            branch_dve(dve, pos, ch, 0)
            meet(dve, pos, 3)
            cv_dve(dve, pos, ch)
            meet(dve, pos, 3)
            branch_dve(dve, pos, ch, 1)
            meet(dve, pos, 3)
            rms_dve(dve, ch, "rm", CTX)
            norm_dve(dve, ch, "nm", KD, CTX, lambda k: mem_sb[:, k], hm_hi, hm_lo)
            meet(dve, pos, 3)
            mk_heads.dve(dve, pos, ch, m_k, sp_("mk"))
            pos.next_use(), pos.next_use()
            meet(dve, pos, 3)
            qm_heads.dve(dve, pos, ch, q_mem, mq_s)
            meet(dve, pos, 3)
            mem_att.dve(dve, pos, ch)
            meet(dve, pos, 3)
            gate_dve(dve, pos, ch, "gm")
            meet(dve, pos, 3)
            x3_dve(dve, pos, ch)
            branch_dve(dve, pos, ch, 2)
            meet(dve, pos, 3)
            out2_dve(dve, pos, ch)

        @block.tensor
        def _(pe):
            pos = Pos()
            reach(pe, "consts", 4)
            ada_pe(pe, pos)
            rms_pe(pe, "rc", KD, CTX)
            rms_pe(pe, "r1", KD, T)
            proj1_pe(pe, pos)
            meet(pe, pos, 3)
            na.pe(pe, pos)
            meet(pe, pos, 3)
            turn_back_pe(pe, pos, "nt", o_tok)
            ln_pe(pe, pos)
            meet(pe, pos, 3, wait=False)
            out1_pe(pe, pos)
            r2_pe(pe, pos)
            mlp_pe(pe, pos)
            nf_pe(pe, pos)
            lat_pe(pe, pos)
            q_heads.pe(pe, pos)
            k_heads.pe(pe, pos)
            uv_pe(pe, pos)
            meet(pe, pos, 3)
            mla.pe(pe, pos)
            meet(pe, pos, 3)
            gate_pe(pe, pos, "ga", "gattn", o_tok2)
            meet(pe, pos, 3)
            branch_pe(pe, pos, 0, "ga_lo")
            meet(pe, pos, 3)
            cv_pe(pe, pos)
            meet(pe, pos, 3)
            branch_pe(pe, pos, 1, "cv_lo")
            meet(pe, pos, 3)
            rms_pe(pe, "rm", KD, CTX)
            meet(pe, pos, 3)
            mk_heads.pe(pe, pos)
            mv_pe(pe, pos)
            meet(pe, pos, 3)
            qm_heads.pe(pe, pos)
            meet(pe, pos, 3)
            mem_att.pe(pe, pos)
            meet(pe, pos, 3)
            gate_pe(pe, pos, "gm", "gmem", o_mem)
            meet(pe, pos, 3)
            branch_pe(pe, pos, 2, "gm_lo")
            meet(pe, pos, 3)
            out2_pe(pe, pos)


def _blocks(w, nk, m):
    n = w.shape[1] // m
    return w.reshape(nk, P, n, m).transpose(2, 1, 0, 3).reshape(n, P, nk * m)


def _pad(a, width=1024):
    return np.concatenate([a, np.zeros((*a.shape[:-1], width - a.shape[-1]), np.float32)], axis=-1)


def _features(v):
    return np.ascontiguousarray(v.reshape(-1, P).T)


def _weight_units(a):
    w_in, w_in2 = a["w_in"][0], a["w_in_2"][0]
    parts = [_blocks(w_in[:, 0:512], 8, P), _blocks(w_in[:, 512:1024], 8, P), _blocks(w_in[:, 1024:1536], 8, P)]
    ua, ub = _blocks(w_in[:, 1536:2048], 8, P), _blocks(w_in[:, 2048:2560], 8, P)
    parts.append(np.stack([ub, ua], axis=1).reshape(8, P, 1024))
    parts.append(_blocks(a["w_out"][0], 8, P))
    w1, w2 = _blocks(a["w_mlp1"][0], 8, P), a["w_mlp2"][0]
    for g in range(FF_GROUPS):
        parts += [w1[8 * g:8 * g + 8], _blocks(w2[1024 * g:1024 * (g + 1)], 8, P)]
    at = np.cumsum([0, 384, 256, 32, 512, 512, 512, 512, 512, 512, 512, 3072])
    col = lambda i: w_in2[:, at[i]:at[i + 1]]
    pe_cols = np.concatenate([np.zeros((1024, NOPE), np.float32), col(2), col(2)], axis=1)
    parts += [_blocks(pe_cols, 8, P), _blocks(col(0), 8, P), _blocks(col(1), 8, P)]
    uq = a["w_uq_2"][0].reshape(384, HEADS, QK)
    uq = np.concatenate([uq, uq[:, :, 80:96], uq[:, :, 64:80]], axis=2).reshape(384, HEADS * P)
    uq = _blocks(uq, NQL, P)
    parts += [_pad(np.concatenate(list(uq[i:i + 2]), axis=-1))[None] for i in (0, 2, 4, 6)]
    ukv = a["w_ukv_2"][0].reshape(256, HEADS, 128)
    uk = np.concatenate([ukv[:, :, 0:64], np.zeros((256, HEADS, ROPE), np.float32)], axis=2).reshape(256, HEADS * QK)
    uk = _blocks(uk, NKVL, QK)
    parts += [_pad(np.concatenate(list(uk[i:i + 3]), axis=-1))[None] for i in (0, 3, 6)]
    parts.append(_blocks(np.ascontiguousarray(ukv[:, :, 64:128]).reshape(256, 512), NKVL, 512))
    parts.append(_blocks(col(7), 8, P))
    r = _blocks(col(10), 8, P)

    def branch(b, w):
        br = _blocks(w[0], 4, P)
        out = []
        for p in range(4):
            out += [r[8 * b + 2 * p], r[8 * b + 2 * p + 1], np.concatenate([br[2 * p], br[2 * p + 1]], axis=-1)]
        return np.stack(out)

    parts.append(branch(0, a["w_br_attn_2"]))
    cvs = [_blocks(col(i), 8, P) for i in (4, 5, 3, 8)]
    parts.append(np.stack(cvs, axis=1).reshape(16, P, 1024))
    parts.append(branch(1, a["w_br_conv_2"]))
    mkv = a["w_mkv_2"][0].reshape(1024, MH, 2, P)
    parts += [_blocks(np.ascontiguousarray(mkv[:, :, i]).reshape(1024, MH * P), 8, P) for i in (0, 1)]
    parts += [_blocks(col(6), 8, P), _blocks(col(9), 8, P)]
    parts.append(branch(2, a["w_br_mem_2"]))
    parts.append(_blocks(a["w_out_2"][0], 8, P))
    return np.concatenate(parts)


def _small(a):
    rows = lambda v: np.concatenate([v.reshape(-1), np.zeros(P - v.size, np.float32)])[:, None]
    invf = (np.float32(10000.0) ** (-np.arange(0, ROPE, 2, dtype=np.float32) / np.float32(ROPE))).astype(np.float32)
    inv_col, sign_col = np.zeros((P, 1), np.float32), np.zeros((P, 1), np.float32)
    inv_col[NOPE:, 0] = np.concatenate([invf] * 4)
    sign_col[NOPE:, 0] = ([-1.0] * 16 + [1.0] * 16) * 2
    qh, kh = a["q_head_g_2"].reshape(-1), a["k_head_g_2"].reshape(-1)
    c2 = np.stack([a["c"].reshape(KD, P), a["c_ctx"].reshape(KD, P)], axis=-1)
    cols = {
        "c": c2.transpose(1, 0, 2).reshape(P, 16), "b_ada": _features(a["b_ada"][0]),
        "norm1": _features(a["norm1_g"][0]), "norm2": _features(a["norm2_g"][0]), "final": _features(a["final_g"]),
        "norm_2": _features(a["norm_g_2"][0]), "memn": _features(a["mem_norm_g_2"][0]),
        "ln_g": _features(a["conv_ln_g"][0]), "ln_b": _features(a["conv_ln_b"][0]), "dwb": _features(a["dw_bias"][0]),
        "dww": a["dw_kernel"][0].reshape(TAPS, 4, P).transpose(2, 1, 0).reshape(P, 4 * TAPS),
        "b_gate": _features(a["b_gate_2"][0]), "qn": _features(a["q_norm_g_2"][0]), "kvn": _features(a["kv_norm_g_2"][0]),
        "qh": rows(np.concatenate([qh, qh[80:96], qh[64:80]])),
        "kh": rows(np.concatenate([kh[0:NOPE], np.ones(P - NOPE, np.float32)])),
        "khr": rows(np.concatenate([np.zeros(NOPE, np.float32), kh[NOPE:], kh[NOPE:]])),
        "cw": a["conv_w_2"][0].reshape(3, 4, P).transpose(2, 1, 0).reshape(P, 12), "cb": _features(a["conv_b_2"][0]),
        "mq": rows(a["mem_q_g_2"]), "mk": rows(a["mem_k_g_2"]), "invf": inv_col, "sign": sign_col,
    }
    return np.ascontiguousarray(np.concatenate([cols[n] for n in SMALL], axis=1))


def _tokens(x):
    return np.ascontiguousarray(x.T.reshape(KD, P, -1).transpose(1, 0, 2))


def _grid_tables():
    n = HD // 4
    inv = (np.float32(10000.0) ** (-np.arange(n, dtype=np.float32) / np.float32(n))).astype(np.float32)
    t = np.arange(T)
    pos = np.stack([t // W_GRID, t % W_GRID]).astype(np.float32)
    ang = (pos[:, None, :] * inv[None, :, None]).astype(np.float32).astype(np.float64)
    c, s = np.cos(ang), np.sin(ang)
    c = np.concatenate([c, c], axis=1).reshape(64, T)
    s = np.concatenate([-s, s], axis=1).reshape(64, T)
    return np.concatenate([c, c]).astype(np.float32), np.concatenate([s, s]).astype(np.float32)


def _window_mask():
    tiles = {v: t for t, v in reversed(list(enumerate(VARIANT)))}
    m = np.full((P, 5, 10, W_GRID), -1.0e30, np.float32)
    c = np.arange(W_GRID)
    c0 = np.clip(c - NA_C // 2, 0, W_GRID - NA_C)
    ok = (c[None, :] >= c0[:, None]) & (c[None, :] < c0[:, None] + NA_C)
    for v, t in tiles.items():
        for a in range(2):
            r = 2 * t + a
            r0 = int(np.clip(r - NA_R // 2, 0, ROWS - NA_R))
            for b in range(10):
                if r0 <= 2 * t + SHIFT[v] + b < r0 + NA_R:
                    m[a * 64:a * 64 + 64, v, b] = np.where(ok, 0.0, -1.0e30)
    return m.reshape(P, 5 * KEYS)


def kernel(**inputs):
    import numpy as _np
    import concourse.bacc as _bacc
    from concourse.bass_utils import run_bass_kernel_spmd as _run

    a = {k: _np.asarray(v) for k, v in inputs.items()}
    rope_c, rope_s = _grid_tables()
    rpb_pad = _np.pad(a["rpb"][0], ((0, 0), (2, 2), (48, 48)))
    rpb_pad = _np.tile(rpb_pad, (1, 1, W_GRID))
    arrays = {
        "x_t": _tokens(a["x"][0]), "ctx_t": _tokens(a["ctx"][0]), "mem_t": _tokens(a["mem_2"][0]),
        "w_ada": _np.ascontiguousarray(a["w_ada"][0].reshape(KD, P, 12, HALF).transpose(2, 1, 0, 3)),
        "units": _weight_units(a), "small": _small(a), "rope_c": rope_c, "rope_s": rope_s,
        "rpb_pad": rpb_pad, "mask": _window_mask(), "positions": a["positions_2"].reshape(T),
    }
    assert arrays["units"].shape == (N_UNITS, P, 1024)
    nc = _bacc.Bacc("TRN2", target_bir_lowering=False, num_devices=1)
    args = [nc.dram_tensor(n, v.shape, mybir.dt.from_np(v.dtype), kind="ExternalInput").ap() for n, v in arrays.items()]
    out = nc.dram_tensor("out_t", (P, KD, T), F32, kind="ExternalOutput").ap()
    spill = nc.dram_tensor("x_spill", (P, KD, T), F32).ap()
    rs_spill = nc.dram_tensor("rs_spill", (1, T), F32).ap()
    build(nc, *args, out, spill, rs_spill)
    r = _run(nc, [arrays], core_ids=[0])
    got = r.results[0]["out_t"]
    return got.transpose(1, 0, 2).reshape(D, T).T.reshape(1, T, D)
```

```python
from contextlib import ExitStack

import numpy as np

import concourse.bass as bass
from concourse import mybir

F32 = mybir.dt.float32
F32R = mybir.dt.float32r
I32 = mybir.dt.int32
ALU = mybir.AluOpType
ACT = mybir.ActivationFunctionType
AX = mybir.AxisListType.X

P = 128
T = 1024
TT = T // P
HALF = 512
D = 1024
KD = D // P
CTX = 256
EPS = 1e-6
W_GRID = 64
ROWS = T // W_GRID
HEADS = 8
HD = 64
NA_R, NA_C = 8, 16
TAPS = 31
PAD = TAPS // 2
FF_GROUPS = 4
KEYS = 10 * W_GRID
NKT = (KEYS + CTX) // P
VARIANT = [0, 1, 2, 2, 2, 2, 3, 4]
SHIFT = [0, -2, -4, -6, -8]
QK = 96
NOPE = 64
ROPE = 32
NQL, NKVL = 3, 2
MH = 4
EARLY_TAPS = 15
TABLE = 2 * W_GRID - 1
TWO_PI = 2.0 * np.pi

SMALL = {}
_at = 0
for _name, _n in [("c", 16), ("b_ada", 48), ("norm1", 8), ("norm2", 8), ("final", 8), ("norm_2", 8),
                  ("memn", 8), ("ln_g", 4), ("ln_b", 4), ("dwb", 4), ("dww", 4 * TAPS), ("b_gate", 24),
                  ("qn", 3), ("kvn", 2), ("qh", 1), ("kh", 1), ("cw", 12), ("cb", 4), ("mq", 1), ("mk", 1),
                  ("invf", 1), ("sign", 1), ("khr", 1)]:
    SMALL[_name] = _at
    _at += _n
N_SMALL = _at
N_DERIVED = 144

STAGE_UNITS = [("q", 4), ("k", 4), ("v", 4), ("u", 8), ("out1", 8), ("mlp", 16 * FF_GROUPS), ("lat", 6),
               ("uq", 4), ("uk", 3), ("uv", 1), ("gattn", 4), ("br0", 12), ("cv", 16), ("br1", 12),
               ("mkq", 8), ("mv", 4), ("gmem", 4), ("br2", 12), ("out2", 8)]
N_UNITS = sum(n for _, n in STAGE_UNITS)
UNIT0 = {}
_at = 0
for _name, _n in STAGE_UNITS:
    UNIT0[_name] = _at
    _at += _n
ATTN_SPLIT = UNIT0["out1"] + 2


KINDS = {
    "rms": [("r1", 8), ("rc", 8), ("lnv", 4), ("rm", 8)],
    "norm": [("n1", 8), ("nc", 8), ("lnn", 4), ("n2", 8), ("n3", 8), ("nq", 3), ("nk", 2), ("nm", 8)],
    "att": [("na", 64), ("mla", 64), ("ma", 32)],
    "gate": [("ga", 4), ("gm", 4)],
    "branch": [("br0", 8), ("br1", 8), ("br2", 8)],
}
SHARED = {tag: (kind, stages[:i]) for kind, stages in KINDS.items() for i, (tag, _) in enumerate(stages)}
COUNTS = {f"{tag}_{what}": 1 for tag, _ in KINDS["rms"] for what in ("root", "rs")} | {f"br{b}_part": 4 for b in range(3)}


def build(nc, x_t, ctx_t, mem_t, w_ada, w_ada_late, units, small, rope_c, rope_s, rpb_pad, mask, positions, out, x_spill,
          rs_spill):
    def sbuf_map():
        at = (nc.sbuf_base + 63) // 64 * 64
        return at, at + 43 * 1024 + 512

    base, arena = sbuf_map()

    def fixed(name, shape, offset, dt=F32):
        return nc.alloc_sbuf_tensor_at(name, [P, *shape], dt, offset=base + offset)

    def place(name, shape, kib, dt=F32):
        return nc.alloc_sbuf_tensor_at(name, [P, *shape], dt, offset=arena + int(kib * 1024))

    KIB = 1024
    w_raw = fixed("w_raw", [2, 1024], 0)
    w_hi = fixed("w_hi", [2, 1024], 8 * KIB, F32R)
    w_lo = fixed("w_lo", [2, 1024], 16 * KIB, F32R)
    tmp = fixed("tmp", [4, T], 24 * KIB)
    ident = fixed("ident", [P], 40 * KIB)
    ones = fixed("ones", [P], 40 * KIB + 512)
    par = fixed("par", [N_SMALL], 41 * KIB)
    der = fixed("der", [N_DERIVED], 41 * KIB + (4 * N_SMALL + 31) // 32 * 32)
    assert 4 * N_SMALL + 32 + 4 * N_DERIVED <= 2 * KIB

    def sp_(name, n=1, k=0):
        return par[:, SMALL[name] + k:SMALL[name] + k + n]

    mod_x, mod_c = der[:, 0:48], der[:, 48:64]
    a1, a1c, a2 = der[:, 64:72], der[:, 72:80], der[:, 80:88]
    silu_c = der[:, 88:104]
    qh_s, mq_s = der[:, 104:105], der[:, 105:106]
    one_col = der[:, 106:107]
    eps_col = der[:, 107:108]
    both_g = der[:, 128:136]
    row_max, neg_max, row_sum, inv_sum = (der[:, 112 + 4 * i:116 + 4 * i] for i in range(4))

    ada_buf = place("ada_buf", [2, KD, HALF], 0)
    ada_row = place("ada_row", [2, HALF], 32)
    ctx_sb = place("ctx_sb", [KD, CTX], 36)
    hc_hi = place("hc_hi", [KD, CTX], 44, F32R)
    hc_lo = place("hc_lo", [KD, CTX], 52, F32R)
    x_sb = place("x_sb", [KD, T], 64)
    h_hi = place("h_hi", [KD, T], 96, F32R)
    h_lo = place("h_lo", [KD, T], 128, F32R)
    q_t = place("q_t", [4, T], 0)
    q_rot = place("q_rot", [4, T], 16)
    k_ctx = place("k_ctx", [4, CTX], 32)
    v_ctx = place("v_ctx", [2, HALF], 36)
    cos1 = place("cos1", [T], 160)
    sin1 = place("sin1", [T], 60)
    k_rot = place("k_rot", [4, T], 64)
    v_tok = place("v_tok", [TT, HALF], 80)
    glu = place("glu", [4, T + 2 * PAD], 40)
    conv = fixed("conv", [4, T], 24 * KIB)
    na_prob = place("na_prob", [2, KEYS + CTX], 96)
    na_prob_t = place("na_prob_t", [2, NKT, P], 104)
    tmp_b = place("tmp_b", [4, T], 96)
    o_tok = place("o_tok", [TT, HALF], 112)
    bias_t = place("bias_t", [5, KEYS + CTX], 128)
    mask_t = place("mask_t", [5, KEYS], 145.5)
    v_ctx_raw = fixed("v_ctx_raw", [2, CTX], 28 * KIB)
    late_row = place("late_row", [P], 62)
    toep = [place("toep0", [18, W_GRID], 57), place("toep1", [18, W_GRID], 158)]
    mix_hi = place("mix_hi", [KD, T], 0, F32R)
    mix_lo = place("mix_lo", [KD, T], 64, F32R)
    x1 = place("x1", [KD, T], 128)
    h2_hi = place("h2_hi", [KD, T], 96, F32R)
    h2_lo = place("h2_lo", [KD, T], 32, F32R)
    ff_hi = place("ff_hi", [KD, T], 0, F32R)
    ff_lo = place("ff_lo", [KD, T], 64, F32R)
    q_h = place("q_h", [HEADS, T], 0)
    k_h = place("k_h", [HEADS, T], 64)
    v2 = place("v2", [TT, HALF], 128)
    q_lat = place("q_lat", [NQL, T], 0)
    lat_sq = place("lat_sq", [2, T], 12)
    rs1 = place("rs1", [T // 4], 20)
    ql_hi = place("ql_hi", [NQL, T], 64, F32R)
    ql_lo = place("ql_lo", [NQL, T], 76, F32R)
    k_turned = place("k_turned", [T], 92)
    kv_lat = place("kv_lat", [NKVL, T], 128)
    k_pe = place("k_pe", [T], 136)
    cos2 = place("cos2", [T], 140)
    kvl_hi = place("kvl_hi", [NKVL, T], 144, F32R)
    kvl_lo = place("kvl_lo", [NKVL, T], 152, F32R)
    sin2 = place("sin2", [T], 160)
    pos_i = nc.alloc_sbuf_tensor_at("pos_i", [P, T], I32, offset=arena + 160 * 1024)
    o_tok2 = place("o_tok2", [TT, HALF], 144)
    o_hi = place("o_hi", [4, T], 0, F32R)
    o_lo = place("o_lo", [4, T], 16, F32R)
    y = place("y", [KD, T], 64)
    z_pad = place("z_pad", [T + 2], 128)
    mem_sb = place("mem_sb", [KD, CTX], 133)
    hm_hi = place("hm_hi", [KD, CTX], 141, F32R)
    hm_lo = place("hm_lo", [KD, CTX], 149, F32R)
    m_k = place("m_k", [MH, CTX], 157)
    m_v = place("m_v", [2, HALF], 133)
    q_mem = place("q_mem", [MH, T], 0)
    o_mem = place("o_mem", [TT, HALF], 137)
    y_hi = place("y_hi", [KD, T], 96, F32R)
    y_lo = place("y_lo", [KD, T], 32, F32R)
    x3 = place("x3", [KD, T], 128)
    rs1_again = place("rs1_again", [T], 160)

    prob = nc.alloc_sbuf_tensor_at("prob", [P, 2, T], F32, offset=base + 24 * KIB)
    prob_t = nc.alloc_sbuf_tensor_at("prob_t", [P, 2, TT, P], F32, offset=base + 32 * KIB)

    region = nc.alloc_psum_tensor("region", [P, 2, T], F32)
    aux = nc.alloc_psum_tensor("aux", [P, T], F32)
    pv = nc.alloc_psum_tensor("pv", [P, 2, HALF], F32)

    pv_flat = pv[:].rearrange("p a b -> p (a b)")

    sems = {}

    def sem(name):
        tag, _, what = name.partition("_")
        if tag in SHARED:
            name = f"{SHARED[tag][0]}_{what}"
        if name not in sems:
            sems[name] = nc.alloc_semaphore(name)
        return sems[name]

    def reach(e, name, value):
        tag, _, what = name.partition("_")
        if tag in SHARED:
            kind, before = SHARED[tag]
            value = value + sum(COUNTS.get(f"{t}_{what}", n) for t, n in before)
        e.wait_ge(sem(name), value)

    raw_loaded = [sem("raw_loaded_0"), sem("raw_loaded_1")]
    free = [sem("region_free_0"), sem("region_free_1")]
    unit_split, unit_done = sem("unit_split"), sem("unit_done")

    class Pos:

        def __init__(self):
            self.use = 0
            self.count = {}

        def next_use(self):
            self.use += 1
            return self.use - 1

        def add(self, name, n=1):
            self.count[name] = self.count.get(name, 0) + n
            return self.count[name]

    def wait_region(e, use):
        if use >= 2:
            e.wait_ge(free[use % 2], use // 2)

    def copy(e, dst, src, **kw):
        return e.activation(dst, src, ACT.Copy, **kw)

    def mm3(pe, dst, wh, wl, xh, xl, first, last):
        pe.matmul(dst, wh, xh, start=first, stop=False)
        pe.matmul(dst, wh, xl, start=False, stop=False)
        return pe.matmul(dst, wl, xh, start=False, stop=last)

    def project(pe, use, unit, xh, xl, nk, width=T, m=P, off=0, step=P, wait_k=None):
        r, s = use % 2, unit % 2
        pe.wait_ge(unit_split, unit + 1)
        wait_region(pe, use)
        for lo in range(0, width, HALF):
            n = min(HALF, width - lo)
            for k in range(nk):
                if wait_k is not None and lo == 0:
                    wait_k(k)
                w = slice(off + k * step, off + k * step + m)
                last = mm3(pe, region[0:m, r, lo:lo + n], w_hi[:, s, w], w_lo[:, s, w],
                           xh[:, k, lo:lo + n], xl[:, k, lo:lo + n], k == 0, k == nk - 1)
        return last

    LAG = 3
    LAGGED = [(n, k) for t in range(KD + LAG) for n, k in ((0, t), (1, t - LAG)) if 0 <= k < KD]
    LATE_LAST = [(0, k) for k in range(KD - 1)] + [(1, k) for k in range(LAG)] + [(0, KD - 1)] \
        + [(1, k) for k in range(LAG, KD)]

    def project_pair(pe, arrive, xh, xl, wait_k, order=LAGGED):
        for n, k in order:
            if k == 0:
                arrive(n)
            if n == 0:
                wait_k(k)
            w = slice(k * P, k * P + P)
            for lo in (0, HALF):
                last = mm3(pe, region[:, n, lo:lo + HALF], w_hi[:, n, w], w_lo[:, n, w],
                           xh[:, k, lo:lo + HALF], xl[:, k, lo:lo + HALF], k == 0, k == KD - 1)
            if k == KD - 1:
                last.then_inc(unit_done, 1)

    def start_pair(pe, pos, unit0, xh, xl, wait_k):
        assert pos.use % 2 == 0 and unit0 % 2 == 0

        def arrive(n):
            pe.wait_ge(unit_split, unit0 + n + 1)
            wait_region(pe, pos.use + n)

        project_pair(pe, arrive, xh, xl, wait_k)
        pos.use += 2

    def project_tokens(pe, use, units, xh, xl, nk, tiles, cols, rhs):
        r = use % 2
        wait_region(pe, use)
        for i, t in enumerate(tiles):
            for k in range(nk):
                xs = slice(t * P, t * P + P)
                dst = region[:, r, i * cols:(i + 1) * cols]
                pe.matmul(dst, xh[:, k, xs], rhs(w_hi, k), start=(k == 0), stop=False)
                pe.matmul(dst, xl[:, k, xs], rhs(w_hi, k), start=False, stop=False)
                last = pe.matmul(dst, xh[:, k, xs], rhs(w_lo, k), start=False, stop=(k == nk - 1))
        return last

    QTR = T // 4
    assert QTR == CTX

    def packed_sums(pe, dst, src, rows=P):
        for q in range(4):
            last = pe.matmul(dst[32 * q:32 * q + 32], ones[0:rows, 0:32], src[:, q * QTR:(q + 1) * QTR], start=True, stop=True)
        return last

    def spread(pe, dst, packed):
        for q in range(4):
            pick = ident[:, 32 * q:32 * q + 1].broadcast_to([P, P])
            last = pe.matmul(dst[:, q * QTR:(q + 1) * QTR], pick, packed, start=True, stop=True)
        return last

    def column_sums(pe, tag, src, nk, width, rows=P, ready=None):
        for k in range(nk):
            reach(pe, f"{tag}_sq", k + 1)
            for lo in range(0, width, HALF):
                n = min(HALF, width - lo)
                last = pe.matmul(aux[0:rows, lo:lo + n], ones[0:rows, 0:rows], src(k)[:, lo:lo + n],
                                 start=(k == 0), stop=(k == nk - 1))
            last.then_inc(sem(f"{tag}_sqmm"), 1)

    class Chain:
        def __init__(self, e, name):
            self.e, self.s, self.n = e, sem(name), 0

        def __call__(self, ins):
            self.n += 1
            ins.then_inc(self.s, 1)
            self.e.wait_ge(self.s, self.n)

    def meet(e, pos, engines=2):
        e.drain().then_inc(sem("stage_end"), 1)
        reach(e, "stage_end", 2 * pos.add("stages"))
        if engines == 3:
            reach(e, "tensor_stage_end", pos.add("tensor_stages"))

    def rms_act(e, ch, tag, src, nk, width, n, scale_from_ready=None, tmp=tmp, rs=3):
        for k in range(nk):
            if k >= 2:
                reach(e, f"{tag}_sqmm", k - 1)
            if scale_from_ready:
                scale_from_ready(k)
            e.activation(tmp[:, k % 2, 0:width], src(k), ACT.Square).then_inc(sem(f"{tag}_sq"), 1)
        reach(e, f"{tag}_sqmm", nk)
        root_act(e, tag, tmp[:, rs, 0:width], aux[:, 0:width], n, eps_col)

    def root_act(e, tag, dst, src, n, eps):
        e.activation(dst, src, ACT.Sqrt, scale=1.0 / n, bias=eps).then_inc(sem(f"{tag}_root"), 1)

    def inverse_dve(e, tag, k, root):
        reach(e, f"{tag}_root", k)
        e.reciprocal(root, root).then_inc(sem(f"{tag}_rs"), 1)
        reach(e, f"{tag}_rs", k)

    def rms_pe(e, tag, nk, width, tmp=tmp):
        column_sums(e, tag, lambda k: tmp[:, k % 2], nk, width)

    def rms_dve(e, ch, tag, width, tmp=tmp, rs=3):
        inverse_dve(e, tag, 1, tmp[:, rs, 0:width])

    def norm_act(e, ch, tag, nk, width, hi, scale, bias, func=ACT.Identity, tmp=tmp):
        for k in range(nk):
            t = tmp[:, k % 2, 0:width]
            reach(e, f"{tag}_nm", k + 1)
            e.activation(t, t, func, scale=scale(k), bias=bias(k) if bias else 0.0).then_inc(sem(f"{tag}_af"), 1)
            reach(e, f"{tag}_af", k + 1)
            copy(e, hi[:, k, 0:width], t).then_inc(sem(f"{tag}_hi"), 1)

    def norm_dve(e, ch, tag, nk, width, src, hi, lo, tmp=tmp, rs=None):
        def low(k):
            reach(e, f"{tag}_hi", k + 1)
            e.tensor_tensor(lo[:, k, 0:width], tmp[:, k % 2, 0:width], hi[:, k, 0:width].bitcast(F32),
                            ALU.subtract).then_inc(sem(f"{tag}_lo"), 1)

        for k in range(nk):
            if k >= 2:
                reach(e, f"{tag}_lo", k - 1)
            e.tensor_tensor(tmp[:, k % 2, 0:width], src(k), (tmp[:, 3] if rs is None else rs)[:, 0:width], ALU.mult)\
                .then_inc(sem(f"{tag}_nm"), 1)
            if k:
                low(k - 1)
        low(nk - 1)
        reach(e, f"{tag}_lo", nk)

    def split_act(e, tag, k, dst, src):
        copy(e, dst, src).then_inc(sem(f"{tag}_hi"), 1)

    N_ADA = 4

    def ada_sp(e, pos):
        for g in range(N_ADA):
            if g >= 2:
                reach(e, "ada_mm", g - 1)
            e.dma_start(ada_buf[:, g % 2], w_ada[g]).then_inc(sem(f"ada_ld{g % 2}"), 16)

    def ada_pe(e, pos):
        def turn(g):
            reach(e, "ada_row", g + 1)
            for j in range(4):
                m = 4 * g + j
                last = e.transpose(pv[:, 0, 2 * m:2 * m + 2], ada_row[0:2, g % 2, j * P:(j + 1) * P], ident[0:2, 0:2])
            last.then_inc(sem("ada_tr"), 1)

        for g in range(N_ADA):
            use = pos.next_use()
            wait_region(e, use)
            reach(e, f"ada_ld{g % 2}", 16 * (g // 2 + 1))
            for k in range(KD):
                last = e.matmul(region[0:2, use % 2, 0:HALF], silu_c[:, 2 * k:2 * k + 2], ada_buf[:, g % 2, k],
                                start=(k == 0), stop=(k == KD - 1))
            last.then_inc(sem("ada_mm"), 1)
            if g:
                turn(g - 1)
        turn(N_ADA - 1)

    def ada_act(e, pos, ch):
        for g in range(N_ADA):
            use = pos.next_use()
            reach(e, "ada_mm", g + 1)
            if g >= 2:
                reach(e, "ada_tr", g - 1)
            copy(e, ada_row[0:2, g % 2], region[0:2, use % 2, 0:HALF]).then_inc(free[use % 2], 1)
            e.wait_ge(free[use % 2], use // 2 + 1)
            e.sem_inc(sem("ada_row"), 1)

    def ada_dve(e, pos, ch):
        for _ in range(N_ADA):
            pos.next_use()
        reach(e, "ada_tr", N_ADA)
        both = pv[:, 0, 0:32].rearrange("p (m two) -> p m two", two=2)
        ch(e.tensor_tensor(mod_x[:, 0:16], both[:, :, 0], sp_("b_ada", 16), ALU.add))
        ch(e.tensor_tensor(mod_c, both[:, :, 1], sp_("b_ada", 16), ALU.add))
        ch(e.scalar_tensor_tensor(out=a1, in0=mod_x[:, 8:16], scalar=1.0, in1=sp_("norm1", 8), op0=ALU.add, op1=ALU.mult))
        ch(e.scalar_tensor_tensor(out=a1c, in0=mod_c[:, 8:16], scalar=1.0, in1=sp_("norm1", 8), op0=ALU.add, op1=ALU.mult))

    def constants_dve(e, ch):
        ch(e.memset(eps_col, EPS))
        e.sem_inc(sem("eps"), 1)
        reach(e, "small_ld", 16)
        ch(e.tensor_scalar(qh_s, sp_("qh"), QK ** -0.5, None, ALU.mult))
        ch(e.tensor_tensor(both_g, sp_("final", 8), sp_("norm_2", 8), ALU.mult))
        ch(e.tensor_scalar(mq_s, sp_("mq"), P ** -0.5, None, ALU.mult))

    N_LATE = 32

    def late_turn(e):
        return e.transpose(pv[:, 1, 256:258], late_row[0:2], ident[0:2, 0:2])

    def late_pe(e, i):
        if i % 2 == 0:
            return
        n = i // 2
        if n:
            late_turn(e)
        reach(e, f"late_ld{n % 2}", 16 * (n // 2 + 1))
        for k in range(KD):
            last = e.matmul(pv[0:2, 1, P:2 * P], silu_c[:, 2 * k:2 * k + 2], w_raw[:, n % 2, k * P:(k + 1) * P],
                            start=(k == 0), stop=(k == KD - 1))
        last.then_inc(sem("late_used"), 1)

    def late_add(e, ch, n):
        ch(e.tensor_tensor(mod_x[:, 16 + n:17 + n], pv[:, 1, 256:257], sp_("b_ada", 1, 16 + n), ALU.add))

    def late_dve(e, ch, i):
        if i % 2:
            if i > 1:
                late_add(e, ch, i // 2 - 1)
            ch(e.tensor_copy(late_row[0:2], pv[0:2, 1, P:2 * P]))

    def late_end_pe(e, pos):
        reach(e, "na_stored", HEADS * TT)
        late_turn(e).then_inc(sem("late_tr"), 1)

    def late_end_dve(e, pos, ch):
        reach(e, "late_tr", 1)
        late_add(e, ch, N_LATE - 1)
        ch(e.scalar_tensor_tensor(out=a2, in0=mod_x[:, 32:40], scalar=1.0, in1=sp_("norm2", 8), op0=ALU.add, op1=ALU.mult))

    SWAP = [(i + 16) % 32 for i in range(32)]

    def proj1_pe(e, pos):
        start_pair(e, pos, UNIT0["q"], h_hi, h_lo, lambda k: reach(e, "n1_lo", k + 1))
        reach(e, "r1_root", 1)
        rms_pe(e, "rc", KD, CTX)
        for j in range(2, 4):
            use = pos.next_use()
            project(e, use, UNIT0["q"] + j, h_hi, h_lo, KD).then_inc(unit_done, 1)
        for j in range(4):
            use = pos.next_use()
            project(e, use, UNIT0["k"] + j, h_hi, h_lo, KD).then_inc(sem("k_part"), 1)
            use = pos.next_use()
            project(e, use, UNIT0["k"] + j, hc_hi, hc_lo, KD, width=CTX,
                    wait_k=(lambda k: reach(e, "nc_lo", k + 1)) if j == 0 else None).then_inc(unit_done, 1)

        def turn_v(j):
            reach(e, "v_copied", 2 * j + 2)
            if j:
                reach(e, "v_turned", 2 * j)
            for t in range(TT):
                e.transpose(aux[:, t * P:(t + 1) * P], tmp[:, 2 + j % 2, t * P:(t + 1) * P], ident[:])
            for t in range(2):
                last = e.transpose(pv[:, 0, t * P:(t + 1) * P], v_ctx_raw[:, j % 2, t * P:(t + 1) * P], ident[:])
            last.then_inc(sem("v_tr"), 1)

        for j in range(4):
            use = pos.next_use()
            project(e, use, UNIT0["v"] + j, h_hi, h_lo, KD).then_inc(sem("v_part"), 1)
            use = pos.next_use()
            project(e, use, UNIT0["v"] + j, hc_hi, hc_lo, KD, width=CTX).then_inc(unit_done, 1)
            if j:
                turn_v(j - 1)
        for j in range(8):
            use = pos.next_use()
            project(e, use, UNIT0["u"] + j, h_hi, h_lo, KD).then_inc(unit_done, 1)
            if j == 0:
                turn_v(3)

    def proj1_act_q(e, pos, js):
        for j in js:
            use = pos.next_use()
            e.wait_ge(unit_done, UNIT0["q"] + j + 1)
            e.activation(q_t[:, j], region[:, use % 2], ACT.Copy, scale=HD ** -0.5).then_inc(free[use % 2], 1)

    def proj1_act(e, pos, ch):
        proj1_act_q(e, pos, range(2, 4))
        for j in range(4):
            use = pos.next_use()
            reach(e, "k_part", j + 1)
            if j >= 2:
                reach(e, "k_rot", j - 1)
            copy(e, tmp[:, 2 + j % 2], region[:, use % 2]).then_inc(free[use % 2], 1)
            use = pos.next_use()
            e.wait_ge(unit_done, UNIT0["k"] + j + 1)
            copy(e, k_ctx[:, j], region[:, use % 2, 0:CTX]).then_inc(free[use % 2], 1)
        for j in range(4):
            use = pos.next_use()
            reach(e, "v_part", j + 1)
            if j < 2:
                reach(e, "k_rot", 3 + j)
            else:
                reach(e, "v_tr", j - 1)
            copy(e, tmp[:, 2 + j % 2], region[:, use % 2]).then_inc(free[use % 2], 1)
            e.wait_ge(free[use % 2], use // 2 + 1)
            e.sem_inc(sem("v_copied"), 1)
            use = pos.next_use()
            e.wait_ge(unit_done, UNIT0["v"] + j + 1)
            copy(e, v_ctx_raw[:, j % 2], region[:, use % 2, 0:CTX]).then_inc(free[use % 2], 1)
            e.wait_ge(free[use % 2], use // 2 + 1)
            e.sem_inc(sem("v_copied"), 1)
        for j in range(4):
            use = pos.next_use()
            e.wait_ge(unit_done, UNIT0["u"] + 2 * j + 1)
            e.activation(glu[:, j, PAD:PAD + T], region[:, use % 2], ACT.Sigmoid).then_inc(free[use % 2], 1)
            pos.next_use()

    def proj1_dve(e, pos, ch):
        def rotate(dst, src, done=None):
            ch(e.stream_shuffle(tmp[:, 0], src, SWAP))
            ch(e.tensor_tensor(tmp[:, 0], tmp[:, 0], sin1[:], ALU.mult))
            ch(e.tensor_tensor(dst, src, cos1[:], ALU.mult))
            last = e.tensor_tensor(dst, dst, tmp[:, 0], ALU.add)
            if done:
                last.then_inc(done, 1)
            else:
                ch(last)

        reach(e, "rope1_ld", 32)
        for j in range(4):
            use = pos.next_use()
            e.wait_ge(free[use % 2], use // 2 + 1)
            rotate(q_rot[:, j], q_t[:, j])
        for j in range(4):
            use = pos.next_use()
            pos.next_use()
            e.wait_ge(free[use % 2], use // 2 + 1)
            rotate(k_rot[:, j], tmp[:, 2 + j % 2], sem("k_rot"))
            reach(e, "k_rot", j + 1)
        for j in range(4):
            pos.next_use(), pos.next_use()
            cols = slice(j * P, (j + 1) * P)
            reach(e, "v_tr", j + 1)
            e.tensor_copy(v_tok[:, :, cols], aux[:].rearrange("p (t c) -> p t c", c=P)).then_inc(sem("v_turned"), 1)
            e.tensor_copy(v_ctx[:, :, cols], pv[:, 0, 0:2 * P].rearrange("p (t c) -> p t c", c=P)).then_inc(sem("v_turned"), 1)
        e.wait_ge(unit_done, UNIT0["u"] + 1)
        for j in range(4):
            ch(e.memset(glu[:, j, 0:PAD], 0.0))
            ch(e.memset(glu[:, j, PAD + T:], 0.0))
        for j in range(4):
            use = pos.next_use()
            e.wait_ge(free[use % 2], use // 2 + 1)
            use = pos.next_use()
            e.wait_ge(unit_done, UNIT0["u"] + 2 * j + 2)
            g = glu[:, j, PAD:PAD + T]
            e.tensor_tensor(g, region[:, use % 2], g, ALU.mult).then_inc(free[use % 2], 1)
            e.wait_ge(free[use % 2], use // 2 + 1)
            if j < 3:
                for n in range(EARLY_TAPS * j, EARLY_TAPS * (j + 1)):
                    conv_tap(e, ch, n)

    class Attention:

        def __init__(self, tag, heads, nkeys, bufs, score, v_of, store, bias=None, extra=None, beside_pe=None, beside_dve=None,
                     ahead_act=None, ahead_dve=None):
            self.ahead_act, self.ahead_dve = ahead_act, ahead_dve
            self.beside_pe, self.beside_dve = beside_pe, beside_dve
            self.tag, self.n, self.nkeys, self.nkt = tag, heads * TT, nkeys, nkeys // P
            self.score, self.v_of, self.store, self.bias, self.extra = score, v_of, store, bias, extra
            self.split = min(self.nkt, 4)
            self.prob, self.prob_t = bufs

        def s(self, what):
            return sem(f"{self.tag}_{what}")

        def pe(self, e, pos):
            uses = {}

            def scores(i):
                use = uses[i] = pos.next_use()
                wait_region(e, use)
                self.score(e, i, region[:, use % 2]).then_inc(self.s("scored"), 1)

            def turn(i):
                reach(e, self.tag + "_prob", i + 1)
                if i:
                    reach(e, self.tag + "_pt_a", i)
                    if self.nkt > self.split:
                        reach(e, self.tag + "_pt_b", i)
                for b in range(self.nkt):
                    last = e.transpose(aux[:, b * P:(b + 1) * P], self.prob[:, i % 2, b * P:(b + 1) * P], ident[:])
                last.then_inc(self.s("turned"), 1)

            def values(i):
                reach(e, self.tag + "_pt_a", i + 1)
                if self.nkt > self.split:
                    reach(e, self.tag + "_pt_b", i + 1)
                if i >= 2:
                    reach(e, self.tag + "_stored", i - 1)
                if self.beside_pe:
                    self.beside_pe(e, i)
                for b in range(self.nkt):
                    last = e.matmul(pv[:, i % 2, 0:P], self.prob_t[:, i % 2, b], self.v_of(i, b),
                                    start=(b == 0), stop=(b == self.nkt - 1))
                last.then_inc(self.s("summed"), 1)

            for i in range(self.n + 3):
                if i < self.n:
                    scores(i)
                if 2 <= i < self.n + 2:
                    turn(i - 2)
                if i >= 3:
                    values(i - 3)

        def act(self, e, pos, ch):
            def exps(i):
                use = pos.next_use()
                src = self.prob[:, i % 2, 0:self.nkeys] if self.bias else region[:, use % 2, 0:self.nkeys]
                reach(e, self.tag + "_maxed", i + 1)
                if i >= 2:
                    reach(e, self.tag + "_turned", i - 1)
                if i >= 4:
                    reach(e, self.tag + "_stored", i - 3)
                e.activation(self.prob[:, i % 2, 0:self.nkeys], src, ACT.Exp, bias=neg_max[:, i % 4:i % 4 + 1],
                             accum_out=row_sum[:, i % 4:i % 4 + 1]).then_inc(self.s("prob"), 1)
                if not self.bias:
                    reach(e, self.tag + "_prob", i + 1)
                    e.sem_inc(free[use % 2], 1)

            def move(i):
                reach(e, self.tag + "_turned", i + 1)
                if i >= 2:
                    reach(e, self.tag + "_summed", i - 1)
                copy(e, self.prob_t[:, i % 2, 0:self.split], aux[:, 0:self.split * P].rearrange("p (b k) -> p b k", k=P))\
                    .then_inc(self.s("pt_a"), 1)

            for i in range(self.n + 2):
                if self.ahead_act and i < self.n:
                    self.ahead_act(e, i)
                if i >= 2:
                    move(i - 2)
                if i < self.n:
                    exps(i)

        def dve(self, e, pos, ch):
            def maxes(i):
                use = pos.next_use()
                reach(e, self.tag + "_scored", i + 1)
                if i >= 4:
                    reach(e, self.tag + "_prob", i - 3)
                if self.bias:
                    if i >= 2:
                        reach(e, self.tag + "_turned", i - 1)
                    reach(e, self.tag + "_bias", self.bias_count(i))
                    e.tensor_tensor_reduce(self.prob[:, i % 2, 0:self.nkeys], region[:, use % 2, 0:self.nkeys], self.bias(i),
                                           1.0, -3.0e38, ALU.add, ALU.max, row_max[:, i % 4:i % 4 + 1])\
                        .then_inc(free[use % 2], 1)
                    e.wait_ge(free[use % 2], use // 2 + 1)
                    e.tensor_scalar(neg_max[:, i % 4:i % 4 + 1], row_max[:, i % 4:i % 4 + 1], -1.0, None,
                                    ALU.mult).then_inc(self.s("maxed"), 1)
                else:
                    e.tensor_reduce(neg_max[:, i % 4:i % 4 + 1], region[:, use % 2, 0:self.nkeys], AX, ALU.max,
                                    negate=True).then_inc(self.s("maxed"), 1)

            def move(i):
                if self.nkt > self.split:
                    reach(e, self.tag + "_turned", i + 1)
                    if i >= 2:
                        reach(e, self.tag + "_summed", i - 1)
                    e.tensor_copy(self.prob_t[:, i % 2, self.split:self.nkt],
                                  aux[:, self.split * P:self.nkt * P].rearrange("p (b k) -> p b k", k=P))\
                        .then_inc(self.s("pt_b"), 1)

            def store(i):
                reach(e, self.tag + "_summed", i + 1)
                if self.beside_dve:
                    self.beside_dve(e, ch, i)
                ch(e.reciprocal(inv_sum[:, i % 4:i % 4 + 1], row_sum[:, i % 4:i % 4 + 1]))
                dst, cols = self.store(i)
                e.tensor_scalar(dst, pv[:, i % 2, cols], inv_sum[:, i % 4:i % 4 + 1], None, ALU.mult)\
                    .then_inc(self.s("stored"), 1)

            for i in range(self.n + 3):
                if self.ahead_dve and i < self.n:
                    self.ahead_dve(e, i)
                if i < self.n:
                    maxes(i)
                if 2 <= i < self.n + 2:
                    move(i - 2)
                if i >= 3:
                    store(i - 3)
                if self.extra:
                    self.extra(e, ch, i)
            reach(e, self.tag + "_stored", self.n)

    def first_key_row(t):
        return 2 * t + SHIFT[VARIANT[t]]

    def na_score(e, i, dst):
        h, t = divmod(i, TT)
        rows = slice(64 * (h % 2), 64 * (h % 2) + 64)
        j, qs, k0 = h // 2, slice(t * P, t * P + P), first_key_row(t) * W_GRID
        e.matmul(dst[:, 0:512], q_rot[rows, j, qs], k_rot[rows, j, k0:k0 + 512], start=True, stop=True)
        e.matmul(dst[:, 512:KEYS], q_rot[rows, j, qs], k_rot[rows, j, k0 + 512:k0 + KEYS], start=True, stop=True)
        return e.matmul(dst[:, KEYS:KEYS + CTX], q_t[rows, j, qs], k_ctx[rows, j], start=True, stop=True)

    def na_v(i, b):
        h, t = divmod(i, TT)
        cols = slice(P * (h // 2), P * (h // 2) + P)
        if b < KEYS // P:
            return v_tok[:, first_key_row(t) // 2 + b, cols]
        return v_ctx[:, b - KEYS // P, cols]

    def head_store(buf):
        def store(i):
            h, t = divmod(i, TT)
            return buf[:, t, h * 64:h * 64 + 64], slice(64 * (h % 2), 64 * (h % 2) + 64)
        return store

    def conv_tap(e, ch, n):
        j, k = divmod(n, TAPS)
        src, w = glu[:, j, k:k + T], sp_("dww", 1, j * TAPS + k)
        if k == 0:
            ch(e.tensor_scalar(conv[:, j], src, w, sp_("dwb", 1, j), ALU.mult, ALU.add))
        else:
            ch(e.scalar_tensor_tensor(out=conv[:, j], in0=src, scalar=w, in1=conv[:, j], op0=ALU.mult, op1=ALU.add))

    def conv_extra(e, ch, i):
        left = 4 * TAPS - 3 * EARLY_TAPS
        tiles = HEADS * TT - 2
        for n in range(left * i // tiles, min(left * (i + 1) // tiles, left)):
            conv_tap(e, ch, 3 * EARLY_TAPS + n)

    na = Attention("na", HEADS, KEYS + CTX, (na_prob, na_prob_t), na_score, na_v, head_store(o_tok),
                   bias=lambda i: bias_t[:, VARIANT[i % TT]], extra=conv_extra,
                   beside_pe=late_pe, beside_dve=late_dve)
    na.bias_count = lambda i: 5 * (i // TT) + VARIANT[i % TT] + 1

    def load_toep(e, h):
        for a in range(2):
            start = (h * 19 + 1 - a) * TABLE * W_GRID + W_GRID - 1
            src = bass.AP(rpb_pad.tensor, start, [[TABLE - 1, W_GRID], [TABLE * W_GRID, 18], [1, W_GRID]])
            e.dma_start(toep[h % 2][a * 64:a * 64 + 64], src).then_inc(sem(f"toep_ld{h % 2}"), 16)

    def bias_early_pool(e):
        e.wait_ge(unit_done, UNIT0["v"] + 4)
        reach(e, "k_rot", 4)
        load_toep(e, 0)

    def bias_add(e, h, v):
        r0 = SHIFT[v] + 8
        e.tensor_tensor(bias_t[:, v, 0:KEYS].rearrange("p (r c) -> p r c", c=W_GRID),
                        toep[h % 2][:, r0:r0 + 10],
                        mask_t[:, v].rearrange("p (r c) -> p r c", c=W_GRID), ALU.add)\
            .then_inc(sem("na_bias"), 1)

    def bias_first_pool(e):
        e.wait_ge(unit_done, UNIT0["u"] + 8)
        e.dma_start(mask_t[:, 0], mask[:, 0:KEYS]).then_inc(sem("mask_ld0"), 16)
        e.dma_start(mask_t[:, 1:].rearrange("p v k -> p (v k)"), mask[:, KEYS:]).then_inc(sem("mask_ld1"), 16)
        load_toep(e, 1)
        for v in range(5):
            e.memset(bias_t[:, v, KEYS:], 0.0).then_inc(sem("bias_tail"), 1)
        reach(e, "bias_tail", 5)
        reach(e, "toep_ld0", 32)
        reach(e, "mask_ld0", 16)
        bias_add(e, 0, 0)

    def bias_pool(e):
        reach(e, "mask_ld1", 16)
        for h in range(HEADS):
            reach(e, f"toep_ld{h % 2}", 32 * (h // 2 + 1))
            for v in range(5):
                if h:
                    last_tile = max(t for t in range(TT) if VARIANT[t] == v)
                    reach(e, "na_maxed", TT * (h - 1) + last_tile + 1)
                if h or v:
                    bias_add(e, h, v)
            if h + 2 < HEADS:
                reach(e, "na_bias", 5 * (h + 1))
                load_toep(e, h + 2)

    def turn_back_pe(e, pos, tag, src):
        for j in range(4):
            use = pos.next_use()
            wait_region(e, use)
            for t in range(TT):
                last = e.transpose(region[:, use % 2, t * P:(t + 1) * P], src[:, t, j * P:(j + 1) * P], ident[:])
            last.then_inc(sem(f"{tag}_tb"), 1)

    def turn_back_act(e, pos, tag, hi):
        for j in range(4):
            use = pos.next_use()
            reach(e, f"{tag}_tb", j + 1)
            copy(e, hi[:, j], region[:, use % 2]).then_inc(sem(f"{tag}_tbhi"), 1)

    def turn_back_dve(e, pos, tag, hi, lo):
        for j in range(4):
            use = pos.next_use()
            reach(e, f"{tag}_tbhi", j + 1)
            e.tensor_tensor(lo[:, j], region[:, use % 2], hi[:, j].bitcast(F32), ALU.subtract).then_inc(free[use % 2], 1)

    def ln_pe(e, pos):
        for j in range(4):
            for lo in range(0, T, HALF):
                last = e.matmul(aux[:, lo:lo + HALF], ones[:], conv[:, j, lo:lo + HALF], start=(j == 0), stop=(j == 3))
        last.then_inc(sem("ln_sum"), 1)
        reach(e, "ln_dev", 4)
        rms_pe(e, "lnv", 4, T, tmp_b)

    def ln_dve(e, pos, ch):
        reach(e, "ln_sum", 1)
        for j in range(4):
            e.scalar_tensor_tensor(out=conv[:, j], in0=aux[:], scalar=-1.0 / 512, in1=conv[:, j],
                                   op0=ALU.mult, op1=ALU.add).then_inc(sem("ln_dev"), 1)
        rms_dve(e, ch, "lnv", T, tmp_b)
        norm_dve(e, ch, "lnn", 4, T, lambda k: conv[:, k], mix_hi[:, 4:8], mix_lo[:, 4:8], tmp_b)

    def ln_act(e, pos, ch):
        rms_act(e, ch, "lnv", lambda k: conv[:, k], 4, T, 512,
                scale_from_ready=lambda k: reach(e, "ln_dev", k + 1), tmp=tmp_b)
        norm_act(e, ch, "lnn", 4, T, mix_hi[:, 4:8], lambda k: sp_("ln_g", 1, k), lambda k: sp_("ln_b", 1, k), ACT.Silu, tmp_b)

    def out1_pe(e, pos):
        start_pair(e, pos, UNIT0["out1"], mix_hi, mix_lo, lambda k: reach(e, "lnn_lo", k - 3) if k >= 4 else None)
        for j in range(2, 8):
            use = pos.next_use()
            project(e, use, UNIT0["out1"] + j, mix_hi, mix_lo, KD).then_inc(unit_done, 1)

    def out1_dve(e, pos, ch):
        reach(e, "x_again", 16)
        for j in range(8):
            use = pos.next_use()
            e.wait_ge(unit_done, UNIT0["out1"] + j + 1)
            e.scalar_tensor_tensor(out=x1[:, j], in0=region[:, use % 2], scalar=mod_x[:, 16 + j:17 + j],
                                   in1=x1[:, j], op0=ALU.mult, op1=ALU.add).then_inc(free[use % 2], 1)
            e.wait_ge(free[use % 2], use // 2 + 1)
            if j:
                reach(e, "r2_sq", j + 1)
                if j >= 2:
                    reach(e, "r2_acc", j - 1)
                e.tensor_tensor(tmp[:, 2], tmp[:, 2], tmp[:, j % 2], ALU.add).then_inc(sem("r2_acc"), 1)

    def out1_act(e, pos, ch):
        for j in range(8):
            use = pos.next_use()
            e.wait_ge(free[use % 2], use // 2 + 1)
            if j >= 3:
                reach(e, "r2_acc", j - 2)
            e.activation(tmp[:, j % 2] if j else tmp[:, 2], x1[:, j], ACT.Square).then_inc(sem("r2_sq"), 1)

    def r2_pe(e, pos):
        reach(e, "r2_acc", KD - 1)
        packed_sums(e, aux[:, 0:QTR], tmp[:, 2]).then_inc(sem("r2_sqmm"), 1)
        reach(e, "r2_rs", 1)
        spread(e, pv_flat, tmp[:, 3, 0:QTR]).then_inc(sem("r2_spread"), 1)

    def mlp_pe(e, pos):
        u0, c0 = UNIT0["mlp"], pos.use
        assert c0 % 2 == 0 and u0 % 2 == 0
        with e.Fori(0, FF_GROUPS) as g:
            def arrive(n):
                e.wait_ge(unit_split, g * 16 + (u0 + n + 1))
                e.wait_ge(free[n % 2], g * 8 + (c0 + n) // 2)

            def unit(n, xh, xl):
                r = s = n % 2
                arrive(n)
                for lo in (0, HALF):
                    for k in range(KD):
                        w = slice(k * P, k * P + P)
                        last = mm3(e, region[:, r, lo:lo + HALF], w_hi[:, s, w], w_lo[:, s, w],
                                   xh[:, k, lo:lo + HALF], xl[:, k, lo:lo + HALF], k == 0, k == KD - 1)
                last.then_inc(unit_done, 1)
            project_pair(e, arrive, h2_hi, h2_lo, lambda k: reach(e, "n2_lo", k + 1))
            for f in range(2, KD):
                unit(f, h2_hi, h2_lo)
            project_pair(e, lambda n: arrive(KD + n), ff_hi, ff_lo, lambda k: reach(e, "ff_lo", g * 8 + (k + 1)), LATE_LAST)
            for d in range(2, KD):
                unit(KD + d, ff_hi, ff_lo)
        pos.use += 16 * FF_GROUPS

    def mlp_act(e, pos, ch):
        u0, c0 = UNIT0["mlp"], pos.use
        with e.Fori(0, FF_GROUPS) as g:
            def hi(f):
                reach(e, "ff_sq", g * 8 + (f + 1))
                copy(e, ff_hi[:, f], tmp[:, 2 + f % 2]).then_inc(sem("ff_hi"), 1)

            for f in range(KD):
                e.wait_ge(unit_done, g * 16 + (u0 + f + 1))
                if f >= 2:
                    reach(e, "ff_sq", g * 8 + (f - 1))
                else:
                    reach(e, "nf_acc", g * 14 + 1)
                e.activation(tmp[:, f % 2], region[:, f % 2], ACT.Relu).then_inc(free[f % 2], 1)
                if f:
                    hi(f - 1)
            hi(KD - 1)
            for d in range(KD):
                e.wait_ge(free[d % 2], g * 8 + (c0 + KD + d) // 2 + 1)
                if d:
                    reach(e, "nf_acc", g * 14 + (2 * d - 1))
                else:
                    reach(e, "ff_lo", g * 8 + 8)
                e.activation(tmp[:, 0 if d else 2], x1[:, d], ACT.Square).then_inc(sem("nf_sq"), 1)
                e.activation(tmp[:, 1 if d else 3], x1[:, d], ACT.Square, scale=sp_("final", 1, d)).then_inc(sem("nf_sq"), 1)
        pos.use += 16 * FF_GROUPS

    def mlp_dve(e, pos, ch):
        u0, c0 = UNIT0["mlp"], pos.use
        e.sem_inc(sem("nf_acc"), 1)
        with e.Fori(0, FF_GROUPS) as g:
            def low(f):
                reach(e, "ff_hi", g * 8 + (f + 1))
                e.tensor_tensor(ff_lo[:, f], tmp[:, 2 + f % 2], ff_hi[:, f].bitcast(F32), ALU.subtract)\
                    .then_inc(sem("ff_lo"), 1)

            for f in range(KD):
                e.wait_ge(free[f % 2], g * 8 + (c0 + f) // 2 + 1)
                if f >= 2:
                    reach(e, "ff_lo", g * 8 + (f - 1))
                e.tensor_tensor(tmp[:, 2 + f % 2], tmp[:, f % 2], tmp[:, f % 2], ALU.mult).then_inc(sem("ff_sq"), 1)
                if f:
                    low(f - 1)
            low(KD - 1)
            for d in range(KD):
                e.wait_ge(unit_done, g * 16 + (u0 + KD + d + 1))
                e.scalar_tensor_tensor(out=x1[:, d], in0=region[:, d % 2], scalar=mod_x[:, 40 + d:41 + d],
                                       in1=x1[:, d], op0=ALU.mult, op1=ALU.add).then_inc(free[d % 2], 1)
                e.wait_ge(free[d % 2], g * 8 + (c0 + KD + d) // 2 + 1)
                if d:
                    for i in range(2):
                        reach(e, "nf_sq", g * 16 + (2 * d + 1 + i))
                        if d >= 2:
                            reach(e, "nf_acc", g * 14 + (2 * d - 2 + i))
                        e.tensor_tensor(tmp[:, 2 + i], tmp[:, 2 + i], tmp[:, i], ALU.add).then_inc(sem("nf_acc"), 1)
            reach(e, "nf_acc", g * 14 + 15)
        pos.use += 16 * FF_GROUPS

    nf_a, nf_b = tmp[:, 3, 0:QTR], tmp[:, 3, QTR:2 * QTR]

    def nf_pe(e, pos):
        reach(e, "nf_acc", 14 * FF_GROUPS + 1)
        packed_sums(e, aux[:, 0:QTR], tmp[:, 2]).then_inc(sem("nf_sqmm"), 1)
        packed_sums(e, aux[:, HALF:HALF + QTR], tmp[:, 3]).then_inc(sem("nf_sqmm"), 1)
        reach(e, "nf_rs", 1)
        spread(e, pv_flat, nf_b).then_inc(sem("nf_spread"), 1)

    def nf_dve(e, pos, ch):
        reach(e, "nf_sqmm", 2)
        e.tensor_scalar(nf_a, aux[:, 0:QTR], 1.0 / D, EPS, ALU.mult, ALU.add).then_inc(sem("nf_a"), 1)
        reach(e, "nf_a", 1)
        e.scalar_tensor_tensor(out=nf_b, in0=nf_a, scalar=EPS * D, in1=aux[:, HALF:HALF + QTR],
                               op0=ALU.mult, op1=ALU.add).then_inc(sem("nf_b"), 1)
        inverse_dve(e, "nf", 1, nf_b)
        reach(e, "nf_spread", 1)

    def nf_act(e, pos, ch):
        reach(e, "nf_acc", 14 * FF_GROUPS + 1)
        e.dma_start(x_spill, x1[:]).then_inc(sem("spill"), 16)
        reach(e, "nf_b", 1)
        e.activation(nf_b, nf_b, ACT.Sqrt, scale=1.0 / D).then_inc(sem("nf_root"), 1)
        e.activation(rs1[:], nf_a, ACT.Sqrt).then_inc(sem("rs1_root"), 1)

    RR = slice(NOPE, P)
    LATS = NQL + NKVL

    def lat_pe(e, pos):
        def sums(i):
            reach(e, "lat_sq", i + 1)
            for lo in range(0, T, HALF):
                dst = aux[:, lo:lo + HALF] if i < NQL else pv[:, lo // HALF]
                last = e.matmul(dst, ones[:], lat_sq[:, i % 2, lo:lo + HALF], start=(i in (0, NQL)), stop=(i in (NQL - 1, LATS - 1)))
            last.then_inc(sem("lat_mm"), 1)

        start_pair(e, pos, UNIT0["lat"], h2_hi, h2_lo, lambda k: reach(e, "n3_lo", k + 1))
        for j in range(2, 1 + LATS):
            use = pos.next_use()
            project(e, use, UNIT0["lat"] + j, h2_hi, h2_lo, KD).then_inc(unit_done, 1)
            if j >= 2:
                sums(j - 2)
        sums(LATS - 1)

    def lat_act(e, pos, ch):
        def table(which, dst):
            reach(e, "angle", which + 1)
            e.activation(dst[RR], tmp[RR, 2], ACT.Sin).then_inc(sem("table"), 1)

        use = pos.next_use()
        e.wait_ge(unit_done, UNIT0["lat"] + 1)
        reach(e, "spill", 16)
        copy(e, k_pe[RR], region[RR, use % 2]).then_inc(free[use % 2], 1)
        table(0, sin2)
        for i in range(LATS):
            use = pos.next_use()
            e.wait_ge(unit_done, UNIT0["lat"] + i + 2)
            dst = q_lat[:, i] if i < NQL else kv_lat[:, i - NQL]
            copy(e, dst, region[:, use % 2]).then_inc(free[use % 2], 1)
            e.wait_ge(free[use % 2], use // 2 + 1)
            if i >= 2:
                reach(e, "lat_mm", i - 1)
            e.activation(lat_sq[:, i % 2], dst, ACT.Square).then_inc(sem("lat_sq"), 1)
            if i == 0:
                table(1, cos2)
            if i == NQL:
                reach(e, "lat_mm", NQL)
                root_act(e, "rq", tmp[:, 3], aux[:], P * NQL, eps_col)
        norm_act(e, ch, "nq", NQL, T, ql_hi, lambda k: sp_("qn", 1, k), None)
        reach(e, "lat_mm", LATS)
        root_act(e, "rk", tmp[:, 2], pv[:].rearrange("p a b -> p (a b)"), P * NKVL, eps_col)
        norm_act(e, ch, "nk", NKVL, T, kvl_hi, lambda k: sp_("kvn", 1, k), None)

    def lat_dve(e, pos, ch):
        r = RR
        reach(e, "rs1_root", 1)
        ch(e.reciprocal(rs1[:], rs1[:]))
        e.sem_inc(sem("rs1_ready"), 1)
        reach(e, "pos_ld", 16)
        ch(e.tensor_copy(tmp[r, 0], pos_i[r]))
        ch(e.tensor_scalar(tmp[r, 0], tmp[r, 0], par[r, SMALL["invf"]:SMALL["invf"] + 1], None, ALU.mult))
        c1 = 6.28125
        c2 = float(np.float32(np.round((TWO_PI - c1) * 2 ** 21) / 2 ** 21))
        c3 = float(TWO_PI - c1 - c2)
        magic = 1.5 * 2 ** 23
        for which, (quarter, shift) in enumerate([(0.0, 0.0), (0.25, np.pi / 2)]):
            ch(e.tensor_scalar(tmp[r, 1], tmp[r, 0], 1.0 / TWO_PI, quarter, ALU.mult, ALU.add))
            ch(e.tensor_scalar(tmp[r, 1], tmp[r, 1], magic, magic, ALU.add, ALU.subtract))
            if which:
                reach(e, "table", 1)
            ch(e.scalar_tensor_tensor(out=tmp[r, 2], in0=tmp[r, 1], scalar=-c1, in1=tmp[r, 0], op0=ALU.mult, op1=ALU.add))
            ch(e.scalar_tensor_tensor(out=tmp[r, 2], in0=tmp[r, 1], scalar=-c2, in1=tmp[r, 2], op0=ALU.mult, op1=ALU.add))
            ch(e.scalar_tensor_tensor(out=tmp[r, 2], in0=tmp[r, 1], scalar=-c3, in1=tmp[r, 2], op0=ALU.mult, op1=ALU.add))
            ch(e.tensor_scalar(tmp[r, 2], tmp[r, 2], shift, 3.1415925, ALU.add, ALU.min))
            e.tensor_scalar(tmp[r, 2], tmp[r, 2], -3.1415925, None, ALU.max).then_inc(sem("angle"), 1)
        reach(e, "angle", 2)
        reach(e, "table", 1)
        ch(e.tensor_scalar(sin2[r], sin2[r], par[r, SMALL["sign"]:SMALL["sign"] + 1], None, ALU.mult))
        reach(e, "table", 2)
        ch(e.tensor_scalar(k_turned[r], k_pe[r], sp_("khr")[r], None, ALU.mult))
        ch(e.stream_shuffle(tmp[r, 0], k_turned[r], SWAP))
        ch(e.tensor_tensor(tmp[r, 0], tmp[r, 0], sin2[r], ALU.mult))
        ch(e.tensor_tensor(k_turned[r], k_turned[r], cos2[r], ALU.mult))
        ch(e.tensor_tensor(k_turned[r], k_turned[r], tmp[r, 0], ALU.add))
        ch(e.memset(cos2[0:NOPE], 1.0))
        ch(e.tensor_copy(cos2[QK:P], sin2[QK:P]))
        inverse_dve(e, "rq", 1, tmp[:, 3])
        norm_dve(e, ch, "nq", NQL, T, lambda k: q_lat[:, k], ql_hi, ql_lo)
        inverse_dve(e, "rk", 1, tmp[:, 2])
        norm_dve(e, ch, "nk", NKVL, T, lambda k: kv_lat[:, k], kvl_hi, kvl_lo, rs=tmp[:, 2])

    class Head:

        def __init__(self, unit, off, last_of_unit, x, nk, m, rows, made, dst, finish, ready=None, before=None,
                     width=T):
            self.unit, self.off, self.last_of_unit, self.x, self.nk, self.m = unit, off, last_of_unit, x, nk, m
            self.rows, self.made, self.dst, self.finish, self.ready, self.before = rows, made, dst, finish, ready, before
            self.width = width
            self.packed = width == T

    class Heads:

        def __init__(self, tag, heads, scale):
            self.tag, self.heads, self.scale_at = tag, heads, scale

        def pe(self, e, pos, meanwhile=None):
            tag = self.tag

            def sums(h):
                reach(e, f"{tag}_sq", h + 1)
                if h >= 2:
                    reach(e, f"{tag}_root", h - 1)
                rows, bank, width = self.heads[h].rows, (h % 2) * HALF, self.heads[h].width
                src = tmp[0:rows, 2 + h % 2]
                if self.heads[h].packed:
                    last = packed_sums(e, aux[:, bank:bank + QTR], src, rows)
                else:
                    last = e.matmul(aux[:, bank:bank + width], ones[0:rows], src[:, 0:width], start=True, stop=True)
                last.then_inc(sem(f"{tag}_ss"), 1)

            def spread_scale(h):
                if self.heads[h].packed:
                    reach(e, f"{tag}_rs", h + 1)
                    if h:
                        reach(e, f"{tag}_sc", h)
                    spread(e, pv_flat, self.scale_at[:, h % 2]).then_inc(sem(f"{tag}_spread"), 1)

            for h, head in enumerate(self.heads):
                use = pos.next_use()
                last = project(e, use, head.unit, *head.x, head.nk, width=head.width, m=head.m, off=head.off, step=head.m,
                               wait_k=(lambda k: head.ready(e, k)) if head.ready else None)
                last.then_inc(unit_done if head.last_of_unit else sem(f"{tag}_part"), 1)
                if h:
                    sums(h - 1)
                if h >= 2:
                    spread_scale(h - 2)
            n = len(self.heads)
            sums(n - 1)
            spread_scale(n - 2)
            if meanwhile:
                meanwhile()
            spread_scale(n - 1)

        def act(self, e, pos, ch):
            tag = self.tag
            parts = 0

            def root(h):
                reach(e, f"{tag}_ss", h + 1)
                if h >= 2:
                    if self.heads[h - 2].packed:
                        reach(e, f"{tag}_spread", sum(x.packed for x in self.heads[:h - 1]))
                    else:
                        reach(e, f"{tag}_sc", h - 1)
                bank = (h % 2) * HALF
                root_act(e, tag, self.scale_at[:, h % 2], aux[:, bank:bank + QTR], self.heads[h].rows, eps_col)

            for h, head in enumerate(self.heads):
                use = pos.next_use()
                if head.last_of_unit:
                    e.wait_ge(unit_done, head.unit + 1)
                else:
                    parts += 1
                    reach(e, f"{tag}_part", parts)
                if h >= 2:
                    reach(e, f"{tag}_ss", h - 1)
                if head.before:
                    head.before(e, h)
                copy(e, head.dst[0:head.made], region[0:head.made, use % 2, 0:head.width]).then_inc(free[use % 2], 1)
                if h:
                    root(h - 1)
                e.wait_ge(free[use % 2], use // 2 + 1)
                s = min(head.made, head.rows)
                e.activation(tmp[0:s, 2 + h % 2, 0:head.width], head.dst[0:s], ACT.Square).then_inc(sem(f"{tag}_sq"), 1)
            root(len(self.heads) - 1)

        def dve(self, e, pos, ch):
            tag = self.tag

            def finish(h):
                packed = self.heads[h].packed
                if packed:
                    reach(e, f"{tag}_spread", sum(x.packed for x in self.heads[:h + 1]))
                rs = pv_flat if packed else self.scale_at[:, h % 2]
                self.heads[h].finish(e, ch, self.heads[h].dst, rs)
                e.sem_inc(sem(f"{tag}_sc"), 1)

            for h in range(len(self.heads)):
                pos.next_use()
                inverse_dve(e, tag, h + 1, self.scale_at[:, h % 2])
                if h:
                    finish(h - 1)
            finish(len(self.heads) - 1)

    def scaled(gain, rows=P):
        def finish(e, ch, dst, rs):
            ch(e.scalar_tensor_tensor(out=dst[0:rows], in0=dst[0:rows], scalar=gain[0:rows], in1=rs[0:rows],
                                      op0=ALU.mult, op1=ALU.mult))
        return finish

    def q_finish(e, ch, dst, rs):
        scaled(qh_s)(e, ch, dst, rs)
        ch(e.tensor_tensor(dst, dst, cos2[:], ALU.mult))

    def k_finish(e, ch, dst, rs):
        scaled(sp_("kh"), NOPE)(e, ch, dst, rs)
        ch(e.tensor_tensor(dst[RR], k_turned[RR], rs[RR], ALU.mult))

    def k_before(e, h):
        e.activation(tmp[NOPE:QK, 2 + h % 2], k_pe[NOPE:QK], ACT.Square).then_inc(sem("kpe_sq"), 1)

    head_scale = place("head_scale", [2, QTR], 160)
    qk_heads = Heads("hd", [
        Head(UNIT0["uq"] + h // 2, (h % 2) * NQL * P, h % 2 == 1, (ql_hi, ql_lo), NQL, P, QK, P, q_h[:, h], q_finish,
             ready=(lambda e, k: reach(e, "nq_lo", k + 1)) if h == 0 else None) for h in range(HEADS)
    ] + [
        Head(UNIT0["uk"] + h // 3, (h % 3) * NKVL * QK, h % 3 == 2 or h == HEADS - 1, (kvl_hi, kvl_lo), NKVL, QK, QK, NOPE,
             k_h[:, h], k_finish, ready=(lambda e, k: reach(e, "nk_lo", k + 1)) if h == 0 else None,
             before=k_before if h < 2 else None) for h in range(HEADS)
    ], head_scale)

    def uv_pe(e, pos):
        e.wait_ge(unit_split, UNIT0["uv"] + 1)
        s = UNIT0["uv"] % 2
        for g in range(4):
            use = pos.next_use()
            last = project_tokens(e, use, None, kvl_hi, kvl_lo, NKVL, range(2 * g, 2 * g + 2), HALF,
                                  lambda w, k: w[:, s, k * HALF:(k + 1) * HALF])
            last.then_inc(unit_done if g == 3 else sem("uv_part"), 1)

    def uv_act(e, pos, ch):
        reach(e, "hd_sc", 2 * HEADS - 1)
        for g in range(4):
            use = pos.next_use()
            if g < 3:
                reach(e, "uv_part", g + 1)
            else:
                e.wait_ge(unit_done, UNIT0["uv"] + 1)
            copy(e, v2[:, 2 * g:2 * g + 2], region[:, use % 2].rearrange("p (t c) -> p t c", c=HALF))\
                .then_inc(free[use % 2], 1)

    q_hi = fixed("q_hi", [2, T], 8 * KIB, F32R)
    k_hi = fixed("k_hi", [2, T], 16 * KIB, F32R)
    q_lo = place("q_lo", [HEADS, T], 0, F32R)
    k_lo = place("k_lo", [HEADS, T], 64, F32R)

    def mla_score(e, i, dst):
        h, t = divmod(i, TT)
        if t == 0:
            reach(e, "qk_lo", 2 * h + 2)
        s, qs = h % 2, slice(t * P, (t + 1) * P)
        for lo in (0, HALF):
            ks = slice(lo, lo + HALF)
            last = mm3(e, dst[:, ks], q_hi[:, s, qs], q_lo[:, h, qs], k_hi[:, s, ks], k_lo[:, h, ks], True, True)
        return last

    def mla_hi(e, h):
        if h >= 2:
            reach(e, "mla_scored", TT * (h - 1))
        copy(e, q_hi[:, h % 2], q_h[:, h]).then_inc(sem("qk_hi"), 1)
        copy(e, k_hi[:, h % 2], k_h[:, h]).then_inc(sem("qk_hi"), 1)

    def mla_low(e, h):
        for n, (full, high, low) in enumerate([(q_h, q_hi, q_lo), (k_h, k_hi, k_lo)]):
            reach(e, "qk_hi", 2 * h + n + 1)
            e.tensor_tensor(low[:, h], full[:, h], high[:, h % 2].bitcast(F32), ALU.subtract).then_inc(sem("qk_lo"), 1)

    def mla_act_ahead(e, i):
        if i == 0:
            mla_hi(e, 0)
        if i % TT == 1 and i // TT + 1 < HEADS:
            mla_hi(e, i // TT + 1)

    def mla_dve_ahead(e, i):
        if i == 0:
            mla_low(e, 0)
        if i % TT == 3 and i // TT + 1 < HEADS:
            mla_low(e, i // TT + 1)

    mla = Attention("mla", HEADS, T, (prob, prob_t), mla_score,
                    lambda i, b: v2[:, b, P * (i // TT // 2):P * (i // TT // 2) + P], head_store(o_tok2),
                    ahead_act=mla_act_ahead, ahead_dve=mla_dve_ahead)

    turned = [aux[:], pv_flat]

    def gate_pe(e, pos, tag, units, src):
        for j in range(4):
            if j >= 2:
                reach(e, f"{tag}_gated", j - 1)
            for t in range(TT):
                last = e.transpose(turned[j % 2][:, t * P:(t + 1) * P], src[:, t, j * P:(j + 1) * P], ident[:])
            last.then_inc(sem(f"{tag}_tb"), 1)
            use = pos.next_use()
            project(e, use, UNIT0[units] + j, h2_hi, h2_lo, KD).then_inc(unit_done, 1)

    def gate_act(e, pos, ch, tag, units):
        for j in range(4):
            use = pos.next_use()
            e.wait_ge(unit_done, UNIT0[units] + j + 1)
            if j >= 2:
                reach(e, f"{tag}_gated", j - 1)
            e.activation(tmp[:, j % 2], region[:, use % 2], ACT.Silu).then_inc(free[use % 2], 1)
            reach(e, f"{tag}_gated", j + 1)
            copy(e, o_hi[:, j], tmp[:, 2 + j % 2]).then_inc(sem(f"{tag}_hi"), 1)

    def gate_dve(e, pos, ch, tag):
        for j in range(4):
            use = pos.next_use()
            e.wait_ge(free[use % 2], use // 2 + 1)
            reach(e, f"{tag}_tb", j + 1)
            e.tensor_tensor(tmp[:, 2 + j % 2], turned[j % 2], tmp[:, j % 2], ALU.mult).then_inc(sem(f"{tag}_gated"), 1)
            reach(e, f"{tag}_hi", j + 1)
            e.tensor_tensor(o_lo[:, j], tmp[:, 2 + j % 2], o_hi[:, j].bitcast(F32), ALU.subtract).then_inc(sem(f"{tag}_lo"), 1)
        reach(e, f"{tag}_lo", 4)

    def branch_pe(e, pos, b, lo_tag, beside=None):
        u0 = UNIT0[f"br{b}"]
        for p in range(4):
            for dd in range(2):
                use = pos.next_use()
                project(e, use, u0 + 3 * p + dd, h2_hi, h2_lo, KD).then_inc(unit_done, 1)
                if beside and p == dd == 0:
                    beside()
            for dd in range(2):
                use = pos.next_use()
                last = project(e, use, u0 + 3 * p + 2, o_hi, o_lo, 4, off=dd * HALF,
                               wait_k=(lambda k: reach(e, lo_tag, k + 1)) if p == dd == 0 else None)
                last.then_inc(unit_done if dd else sem(f"br{b}_part"), 1)

    def branch_act(e, pos, ch, b):
        u0 = UNIT0[f"br{b}"]
        for p in range(4):
            for dd in range(2):
                use = pos.next_use()
                e.wait_ge(unit_done, u0 + 3 * p + dd + 1)
                if p:
                    reach(e, f"br{b}_used", 2 * (p - 1) + dd + 1)
                e.activation(tmp[:, dd], region[:, use % 2], ACT.Sigmoid, bias=sp_("b_gate", 1, 8 * b + 2 * p + dd))\
                    .then_inc(free[use % 2], 1)
            pos.next_use(), pos.next_use()

    def branch_dve(e, pos, ch, b):
        u0 = UNIT0[f"br{b}"]
        for p in range(4):
            gates = [pos.next_use(), pos.next_use()]
            for dd in range(2):
                use = pos.next_use()
                e.wait_ge(free[gates[dd] % 2], gates[dd] // 2 + 1)
                if dd:
                    e.wait_ge(unit_done, u0 + 3 * p + 3)
                else:
                    reach(e, f"br{b}_part", p + 1)
                d = 2 * p + dd
                dst = tmp[:, 2 + dd] if b else y[:, d]
                if b and p:
                    reach(e, f"br{b}_used", 2 * (p - 1) + dd + 1)
                e.tensor_tensor(dst, region[:, use % 2], tmp[:, dd], ALU.mult).then_inc(free[use % 2], 1)
                e.wait_ge(free[use % 2], use // 2 + 1)
                if b:
                    e.tensor_tensor(y[:, d], y[:, d], dst, ALU.add).then_inc(sem(f"br{b}_used"), 1)
                else:
                    e.sem_inc(sem(f"br{b}_used"), 1)
        if b:
            reach(e, f"br{b}_used", 8)

    def cv_pe(e, pos):
        for j in range(16):
            use = pos.next_use()
            project(e, use, UNIT0["cv"] + j, h2_hi, h2_lo, KD).then_inc(unit_done, 1)

    def cv_act(e, pos, ch):
        for j in range(4):
            u = UNIT0["cv"] + 4 * j
            use = pos.next_use()
            e.wait_ge(unit_done, u + 1)
            if j:
                reach(e, "cv_z", j)
            copy(e, tmp[:, 0], region[:, use % 2]).then_inc(free[use % 2], 1)
            pos.next_use(), pos.next_use()
            use = pos.next_use()
            e.wait_ge(unit_done, u + 4)
            if j:
                reach(e, "cv_o", j)
            e.activation(tmp[:, 2], region[:, use % 2], ACT.Silu).then_inc(free[use % 2], 1)
            reach(e, "cv_o", j + 1)
            copy(e, o_hi[:, j], tmp[:, 3]).then_inc(sem("cv_hi"), 1)

    def cv_dve(e, pos, ch):
        ch(e.memset(z_pad[:, 0:1], 0.0))
        ch(e.memset(z_pad[:, T + 1:T + 2], 0.0))
        for j in range(4):
            u = UNIT0["cv"] + 4 * j
            w = lambda k: sp_("cw", 1, 3 * j + k)
            use = pos.next_use()
            e.wait_ge(free[use % 2], use // 2 + 1)
            use = pos.next_use()
            e.wait_ge(unit_done, u + 2)
            e.tensor_tensor(z_pad[:, 1:T + 1], region[:, use % 2], tmp[:, 0], ALU.mult).then_inc(free[use % 2], 1)
            e.wait_ge(free[use % 2], use // 2 + 1)
            e.sem_inc(sem("cv_z"), 1)
            ch(e.tensor_scalar(tmp[:, 1], z_pad[:, 0:T], w(0), sp_("cb", 1, j), ALU.mult, ALU.add))
            for k in (1, 2):
                ch(e.scalar_tensor_tensor(out=tmp[:, 1], in0=z_pad[:, k:k + T], scalar=w(k), in1=tmp[:, 1],
                                          op0=ALU.mult, op1=ALU.add))
            use = pos.next_use()
            e.wait_ge(unit_done, u + 3)
            e.tensor_tensor(tmp[:, 1], region[:, use % 2], tmp[:, 1], ALU.mult).then_inc(free[use % 2], 1)
            e.wait_ge(free[use % 2], use // 2 + 1)
            use = pos.next_use()
            e.wait_ge(free[use % 2], use // 2 + 1)
            if j:
                reach(e, "cv_lo", j)
            e.tensor_tensor(tmp[:, 3], tmp[:, 1], tmp[:, 2], ALU.mult).then_inc(sem("cv_o"), 1)
            reach(e, "cv_hi", j + 1)
            e.tensor_tensor(o_lo[:, j], tmp[:, 3], o_hi[:, j].bitcast(F32), ALU.subtract).then_inc(sem("cv_lo"), 1)
        reach(e, "cv_lo", 4)

    mem_scale = place("mem_scale", [2, QTR], 161)
    tmp_m = place("tmp_m", [4, CTX], 157)
    mem_heads = Heads("mh", [head for h in range(MH) for head in (
        Head(UNIT0["mkq"] + 2 * h, 0, True, (hm_hi, hm_lo), KD, P, P, P, m_k[:, h], scaled(sp_("mk")),
             ready=(lambda e, k: reach(e, "nm_lo", k + 1)) if h == 0 else None, width=CTX),
        Head(UNIT0["mkq"] + 2 * h + 1, 0, True, (h2_hi, h2_lo), KD, P, P, P, q_mem[:, h], scaled(mq_s)))], mem_scale)

    def mv_pe(e, pos):
        for p in range(2):
            use = pos.next_use()
            wait_region(e, use)
            for half in range(2):
                u = UNIT0["mv"] + 2 * p + half
                e.wait_ge(unit_split, u + 1)
                for t in range(2):
                    dst = region[:, use % 2, t * HALF:t * HALF + 256]
                    for kk in range(4):
                        k = 4 * half + kk
                        xh, xl = hm_hi[:, k, t * P:(t + 1) * P], hm_lo[:, k, t * P:(t + 1) * P]
                        wh, wl = (w[:, u % 2, kk * 256:(kk + 1) * 256] for w in (w_hi, w_lo))
                        e.matmul(dst, xh, wh, start=(k == 0), stop=False)
                        e.matmul(dst, xl, wh, start=False, stop=False)
                        last = e.matmul(dst, xh, wl, start=False, stop=(k == KD - 1))
                last.then_inc(unit_done, 1)

    def mv_act(e, pos):
        for p in range(2):
            use = pos.next_use()
            e.wait_ge(unit_done, UNIT0["mv"] + 2 * p + 2)
            copy(e, m_v[:, :, 256 * p:256 * p + 256],
                 region[:, use % 2].rearrange("p (t c) -> p t c", c=HALF)[:, :, 0:256]).then_inc(free[use % 2], 1)

    def mem_score(e, i, dst):
        h, t = divmod(i, TT)
        return e.matmul(dst[:, 0:CTX], q_mem[:, h, t * P:(t + 1) * P], m_k[:, h], start=True, stop=True)

    mem_att = Attention("ma", MH, CTX, (prob, prob_t), mem_score, lambda i, b: m_v[:, b, P * (i // TT):P * (i // TT) + P],
                        lambda i: (o_mem[:, i % TT, P * (i // TT):P * (i // TT) + P], slice(0, P)))

    def out2_pe(e, pos):
        start_pair(e, pos, UNIT0["out2"], y_hi, y_lo, lambda k: reach(e, "y_lo", k + 1))
        for j in range(2, 8):
            use = pos.next_use()
            project(e, use, UNIT0["out2"] + j, y_hi, y_lo, KD).then_inc(unit_done, 1)

    def x3_dve(e, pos, ch):
        reach(e, "x3_ld", 32)
        for j in range(KD):
            ch(e.scalar_tensor_tensor(out=x3[:, j], in0=x3[:, j], scalar=sp_("final", 1, j), in1=rs1_again[:],
                                      op0=ALU.mult, op1=ALU.mult))

    def out2_act(e, pos, ch):
        for k in range(KD):
            copy(e, y_hi[:, k], y[:, k]).then_inc(sem("y_hi"), 1)

    def out2_dve(e, pos, ch):
        for k in range(KD):
            reach(e, "y_hi", k + 1)
            e.tensor_tensor(y_lo[:, k], y[:, k], y_hi[:, k].bitcast(F32), ALU.subtract).then_inc(sem("y_lo"), 1)
        for j in range(8):
            use = pos.next_use()
            e.wait_ge(unit_done, UNIT0["out2"] + j + 1)
            e.tensor_tensor(x3[:, j], region[:, use % 2], x3[:, j], ALU.add).then_inc(sem("out_ready"), 1)
            reach(e, "out_ready", j + 1)
            e.sem_inc(free[use % 2], 1)

    with nc.Block() as block:
        @block.sync
        def _(sp):
            def load(u, s):
                sp.dma_start(w_raw[:, s], units[u]).then_inc(raw_loaded[s], 16)

            sp.dma_start(par[:], small).then_inc(sem("small_ld"), 16)
            ada_sp(sp, None)
            load(0, 0)
            load(1, 1)

            def load_range(a, b):
                with sp.Fori(a // 2, b // 2) as i:
                    for s in range(2):
                        sp.wait_ge(unit_split, i * 2 + (s - 1))
                        sp.dma_start(w_raw[:, s], units[i * 2 + s]).then_inc(raw_loaded[s], 16)

            load_range(2, ATTN_SPLIT)
            for s in range(2):
                sp.wait_ge(unit_split, ATTN_SPLIT - 1 + s)
                sp.dma_start(w_raw[:, s], w_ada_late[s]).then_inc(sem(f"late_ld{s}"), 16)
            with sp.Fori(1, N_LATE // 2) as i:
                for s in range(2):
                    reach(sp, "late_used", i * 2 + (s - 1))
                    sp.dma_start(w_raw[:, s], w_ada_late[i * 2 + s]).then_inc(sem(f"late_ld{s}"), 16)
            reach(sp, "late_used", N_LATE)
            load_range(ATTN_SPLIT, N_UNITS)
            for j in range(KD):
                reach(sp, "out_ready", j + 1)
                sp.dma_start(out[:, j], x3[:, j]).then_inc(sem("out_st"), 16)
            reach(sp, "out_st", 16 * KD)

        @block.gpsimd
        def _(pool):
            def split(i, s):
                pool.wait_ge(raw_loaded[s], i * 16 + 16)
                pool.tensor_tensor(w_hi[:, s], w_raw[:, s], one_col.broadcast_to([P, 1024]), ALU.mult)\
                    .then_inc(sem("hi_split"), 1)
                reach(pool, "hi_split", i * 2 + (s + 1))
                pool.tensor_tensor(w_lo[:, s], w_raw[:, s], w_hi[:, s].bitcast(F32), ALU.subtract)\
                    .then_inc(unit_split, 1)

            def split_range(a, b):
                with pool.Fori(a // 2, b // 2) as i:
                    for s in range(2):
                        pool.wait_ge(unit_done, i * 2 + (s - 1))
                        split(i, s)

            pool.memset(one_col, 1.0).then_inc(sem("consts"), 1)
            pool.memset(ones[:], 1.0).then_inc(sem("consts"), 1)
            pool.memset(ident[:], 0.0).then_inc(sem("consts"), 1)
            reach(pool, "consts", 3)
            pool.affine_select(out=ident[:], in_=ident[:], compare_op=ALU.not_equal, fill=1.0, base=0,
                               pattern=[[-1, P]], channel_multiplier=1).then_inc(sem("consts"), 1)
            split(0, 0)
            split(0, 1)
            u1 = ATTN_SPLIT - 4
            split_range(2, u1)
            bias_early_pool(pool)
            split_range(u1, ATTN_SPLIT - 2)
            pool.wait_ge(unit_done, ATTN_SPLIT - 3)
            split((ATTN_SPLIT - 2) // 2, 0)
            bias_first_pool(pool)
            split((ATTN_SPLIT - 2) // 2, 1)
            bias_pool(pool)
            split_range(ATTN_SPLIT, UNIT0["gattn"])
            reach(pool, "mla_scored", HEADS * TT)
            split_range(UNIT0["gattn"], N_UNITS)

        @block.scalar
        def _(act):
            pos = Pos()
            ch = Chain(act, "scalar_step")
            act.dma_start(x_sb[:, 0:4], x_t[:, 0:4]).then_inc(sem("x_ld0"), 16)
            act.dma_start(x_sb[:, 4:8], x_t[:, 4:8]).then_inc(sem("x_ld1"), 16)
            act.dma_start(ctx_sb[:], ctx_t).then_inc(sem("ctx_ld"), 16)
            act.dma_start(sin1[:], rope_s).then_inc(sem("rope1_ld"), 16)
            act.dma_start(cos1[:], rope_c).then_inc(sem("rope1_ld"), 16)
            reach(act, "small_ld", 16)
            act.activation(silu_c, sp_("c", 16), ACT.Silu).then_inc(sem("silu_c"), 1)
            reach(act, "eps", 1)
            rms_act(act, ch, "r1", lambda k: x_sb[:, k], KD, T, D,
                    scale_from_ready=lambda k: reach(act, f"x_ld{k // 4}", 16))
            ada_act(act, pos, ch)
            reach(act, "ctx_ld", 16)
            norm_act(act, ch, "n1", KD, T, h_hi, lambda k: a1[:, k:k + 1], lambda k: mod_x[:, k:k + 1])
            reach(act, "n1_lo", KD)
            rms_act(act, ch, "rc", lambda k: ctx_sb[:, k], KD, CTX, D, rs=2)
            proj1_act_q(act, pos, range(2))
            norm_act(act, ch, "nc", KD, CTX, hc_hi, lambda k: a1c[:, k:k + 1], lambda k: mod_c[:, k:k + 1])
            proj1_act(act, pos, ch)
            meet(act, pos, 3)
            na.act(act, pos, ch)
            meet(act, pos, 3)
            act.dma_start(x1[:], x_t).then_inc(sem("x_again"), 16)
            act.dma_start(pos_i[RR], positions.partition_broadcast(P - NOPE)).then_inc(sem("pos_ld"), 16)
            turn_back_act(act, pos, "nt", mix_hi)
            ln_act(act, pos, ch)
            meet(act, pos, 3)
            out1_act(act, pos, ch)
            reach(act, "r2_sqmm", 1)
            root_act(act, "r2", tmp[:, 3, 0:QTR], aux[:, 0:QTR], D, eps_col)
            norm_act(act, ch, "n2", KD, T, h2_hi, lambda k: a2[:, k:k + 1], lambda k: mod_x[:, 24 + k:25 + k])
            mlp_act(act, pos, ch)
            nf_act(act, pos, ch)
            norm_act(act, ch, "n3", KD, T, h2_hi, lambda k: both_g[:, k:k + 1], None)
            lat_act(act, pos, ch)
            reach(act, "rs1_ready", 1)
            for q in range(4):
                act.dma_start(rs_spill[q:q + 1], rs1[32 * q:32 * q + 1]).then_inc(sem("rs1_spill"), 16)
            reach(act, "rs1_spill", 64)
            meet(act, pos)
            qk_heads.act(act, pos, ch)
            uv_act(act, pos, ch)
            meet(act, pos, 3)
            mla.act(act, pos, ch)
            meet(act, pos, 3)
            gate_act(act, pos, ch, "ga", "gattn")
            meet(act, pos, 3)
            branch_act(act, pos, ch, 0)
            act.dma_start(mem_sb[:], mem_t).then_inc(sem("mem_ld"), 16)
            meet(act, pos, 3)
            cv_act(act, pos, ch)
            meet(act, pos, 3)
            reach(act, "mem_ld", 16)
            rms_act(act, ch, "rm", lambda k: mem_sb[:, k], KD, CTX, D, tmp=tmp_m)
            norm_act(act, ch, "nm", KD, CTX, hm_hi, lambda k: sp_("memn", 1, k), None, tmp=tmp_m)
            branch_act(act, pos, ch, 1)
            meet(act, pos, 3)
            mem_heads.act(act, pos, ch)
            mv_act(act, pos)
            meet(act, pos, 3)
            mem_att.act(act, pos, ch)
            meet(act, pos, 3)
            gate_act(act, pos, ch, "gm", "gmem")
            meet(act, pos, 3)
            act.dma_start(x3[:], x_spill).then_inc(sem("x3_ld"), 16)
            act.dma_start(rs1_again[:], rs_spill.rearrange("q t -> (q t)").partition_broadcast(P)).then_inc(sem("x3_ld"), 16)
            branch_act(act, pos, ch, 2)
            meet(act, pos, 3)
            out2_act(act, pos, ch)

        @block.vector
        def _(dve):
            pos = Pos()
            ch = Chain(dve, "vector_step")
            constants_dve(dve, ch)
            rms_dve(dve, ch, "r1", T)
            ada_dve(dve, pos, ch)
            norm_dve(dve, ch, "n1", KD, T, lambda k: x_sb[:, k], h_hi, h_lo)
            rms_dve(dve, ch, "rc", CTX, rs=2)
            norm_dve(dve, ch, "nc", KD, CTX, lambda k: ctx_sb[:, k], hc_hi, hc_lo, rs=tmp[:, 2])
            proj1_dve(dve, pos, ch)
            meet(dve, pos, 3)
            na.dve(dve, pos, ch)
            late_end_dve(dve, pos, ch)
            meet(dve, pos, 3)
            turn_back_dve(dve, pos, "nt", mix_hi, mix_lo)
            ln_dve(dve, pos, ch)
            meet(dve, pos, 3)
            out1_dve(dve, pos, ch)
            rms_dve(dve, ch, "r2", QTR)
            reach(dve, "r2_spread", 1)
            norm_dve(dve, ch, "n2", KD, T, lambda k: x1[:, k], h2_hi, h2_lo, rs=pv_flat)
            mlp_dve(dve, pos, ch)
            nf_dve(dve, pos, ch)
            norm_dve(dve, ch, "n3", KD, T, lambda k: x1[:, k], h2_hi, h2_lo, rs=pv_flat)
            for _ in range(6):
                pos.next_use()
            lat_dve(dve, pos, ch)
            meet(dve, pos)
            qk_heads.dve(dve, pos, ch)
            for _ in range(4):
                pos.next_use()
            meet(dve, pos, 3)
            mla.dve(dve, pos, ch)
            meet(dve, pos, 3)
            gate_dve(dve, pos, ch, "ga")
            meet(dve, pos, 3)
            branch_dve(dve, pos, ch, 0)
            meet(dve, pos, 3)
            cv_dve(dve, pos, ch)
            meet(dve, pos, 3)
            rms_dve(dve, ch, "rm", CTX, tmp_m)
            norm_dve(dve, ch, "nm", KD, CTX, lambda k: mem_sb[:, k], hm_hi, hm_lo, tmp_m, tmp_m[:, 3])
            branch_dve(dve, pos, ch, 1)
            meet(dve, pos, 3)
            mem_heads.dve(dve, pos, ch)
            pos.next_use(), pos.next_use()
            meet(dve, pos, 3)
            mem_att.dve(dve, pos, ch)
            meet(dve, pos, 3)
            gate_dve(dve, pos, ch, "gm")
            meet(dve, pos, 3)
            x3_dve(dve, pos, ch)
            branch_dve(dve, pos, ch, 2)
            meet(dve, pos, 3)
            out2_dve(dve, pos, ch)

        @block.tensor
        def _(pe):
            pos = Pos()

            def tell():
                pe.drain().then_inc(sem("tensor_stage_end"), 1)

            def ended(n):
                reach(pe, "stage_end", 2 * n)

            reach(pe, "consts", 4)
            rms_pe(pe, "r1", KD, T)
            reach(pe, "silu_c", 1)
            ada_pe(pe, pos)
            proj1_pe(pe, pos)
            tell()
            ended(1)
            na.pe(pe, pos)
            late_end_pe(pe, pos)
            tell()
            ended(2)
            turn_back_pe(pe, pos, "nt", o_tok)
            ln_pe(pe, pos)
            tell()
            out1_pe(pe, pos)
            r2_pe(pe, pos)
            mlp_pe(pe, pos)
            nf_pe(pe, pos)
            lat_pe(pe, pos)
            qk_heads.pe(pe, pos, meanwhile=lambda: uv_pe(pe, pos))
            tell()
            ended(5)
            mla.pe(pe, pos)
            tell()
            reach(pe, "mla_stored", HEADS * TT)
            gate_pe(pe, pos, "ga", "gattn", o_tok2)
            tell()
            branch_pe(pe, pos, 0, "ga_lo")
            tell()
            cv_pe(pe, pos)
            tell()
            branch_pe(pe, pos, 1, "cv_lo", beside=lambda: rms_pe(pe, "rm", KD, CTX, tmp_m))
            tell()
            mem_heads.pe(pe, pos)
            mv_pe(pe, pos)
            tell()
            ended(11)
            mem_att.pe(pe, pos)
            tell()
            reach(pe, "ma_stored", MH * TT)
            gate_pe(pe, pos, "gm", "gmem", o_mem)
            tell()
            branch_pe(pe, pos, 2, "gm_lo")
            tell()
            out2_pe(pe, pos)


def _blocks(w, nk, m):
    n = w.shape[1] // m
    return w.reshape(nk, P, n, m).transpose(2, 1, 0, 3).reshape(n, P, nk * m)


def _pad(a, width=1024):
    return np.concatenate([a, np.zeros((*a.shape[:-1], width - a.shape[-1]), np.float32)], axis=-1)


def _features(v):
    return np.ascontiguousarray(v.reshape(-1, P).T)


def _weight_units(a):
    w_in, w_in2 = a["w_in"][0], a["w_in_2"][0]
    parts = [_blocks(w_in[:, 0:512], 8, P), _blocks(w_in[:, 512:1024], 8, P), _blocks(w_in[:, 1024:1536], 8, P)]
    ua, ub = _blocks(w_in[:, 1536:2048], 8, P), _blocks(w_in[:, 2048:2560], 8, P)
    parts.append(np.stack([ub, ua], axis=1).reshape(8, P, 1024))
    parts.append(_blocks(a["w_out"][0], 8, P))
    w1, w2 = _blocks(a["w_mlp1"][0], 8, P), a["w_mlp2"][0]
    for g in range(FF_GROUPS):
        parts += [w1[8 * g:8 * g + 8], _blocks(w2[1024 * g:1024 * (g + 1)], 8, P)]
    at = np.cumsum([0, 384, 256, 32, 512, 512, 512, 512, 512, 512, 512, 3072])
    col = lambda i: w_in2[:, at[i]:at[i + 1]]
    pe_cols = np.concatenate([np.zeros((1024, NOPE), np.float32), col(2), col(2)], axis=1)
    parts += [_blocks(pe_cols, 8, P), _blocks(col(0), 8, P), _blocks(col(1), 8, P)]
    uq = a["w_uq_2"][0].reshape(384, HEADS, QK)
    uq = np.concatenate([uq, uq[:, :, 80:96], uq[:, :, 64:80]], axis=2).reshape(384, HEADS * P)
    uq = _blocks(uq, NQL, P)
    parts += [_pad(np.concatenate(list(uq[i:i + 2]), axis=-1))[None] for i in (0, 2, 4, 6)]
    ukv = a["w_ukv_2"][0].reshape(256, HEADS, 128)
    uk = np.concatenate([ukv[:, :, 0:64], np.zeros((256, HEADS, ROPE), np.float32)], axis=2).reshape(256, HEADS * QK)
    uk = _blocks(uk, NKVL, QK)
    parts += [_pad(np.concatenate(list(uk[i:i + 3]), axis=-1))[None] for i in (0, 3, 6)]
    parts.append(_blocks(np.ascontiguousarray(ukv[:, :, 64:128]).reshape(256, 512), NKVL, 512))
    parts.append(_blocks(col(7), 8, P))
    r = _blocks(col(10), 8, P)

    def branch(b, w):
        br = _blocks(w[0], 4, P)
        out = []
        for p in range(4):
            out += [r[8 * b + 2 * p], r[8 * b + 2 * p + 1], np.concatenate([br[2 * p], br[2 * p + 1]], axis=-1)]
        return np.stack(out)

    parts.append(branch(0, a["w_br_attn_2"]))
    cvs = [_blocks(col(i), 8, P) for i in (4, 5, 3, 8)]
    parts.append(np.stack(cvs, axis=1).reshape(16, P, 1024))
    parts.append(branch(1, a["w_br_conv_2"]))
    mkv = a["w_mkv_2"][0].reshape(1024, MH, 2, P)
    mk, mv = (np.ascontiguousarray(mkv[:, :, i]).reshape(1024, MH * P) for i in (0, 1))
    parts.append(np.stack([_blocks(mk, 8, P), _blocks(col(6), 8, P)], axis=1).reshape(8, P, 1024))
    parts.append(mv.reshape(2, 4, P, 2, 256).transpose(3, 0, 2, 1, 4).reshape(4, P, 1024))
    parts.append(_blocks(col(9), 8, P))
    parts.append(branch(2, a["w_br_mem_2"]))
    parts.append(_blocks(a["w_out_2"][0], 8, P))
    return np.concatenate(parts)


def _late_modulation(w):
    return np.ascontiguousarray(w[:, 2048:].reshape(KD, P, 32, P).transpose(2, 1, 0, 3)).reshape(32, P, 1024)


def _small(a):
    rows = lambda v: np.concatenate([v.reshape(-1), np.zeros(P - v.size, np.float32)])[:, None]
    invf = (np.float32(10000.0) ** (-np.arange(0, ROPE, 2, dtype=np.float32) / np.float32(ROPE))).astype(np.float32)
    inv_col, sign_col = np.zeros((P, 1), np.float32), np.zeros((P, 1), np.float32)
    inv_col[NOPE:, 0] = np.concatenate([invf] * 4)
    sign_col[NOPE:, 0] = ([-1.0] * 16 + [1.0] * 16) * 2
    qh, kh = a["q_head_g_2"].reshape(-1), a["k_head_g_2"].reshape(-1)
    c2 = np.stack([a["c"].reshape(KD, P), a["c_ctx"].reshape(KD, P)], axis=-1)
    cols = {
        "c": c2.transpose(1, 0, 2).reshape(P, 16), "b_ada": _features(a["b_ada"][0]),
        "norm1": _features(a["norm1_g"][0]), "norm2": _features(a["norm2_g"][0]), "final": _features(a["final_g"]),
        "norm_2": _features(a["norm_g_2"][0]), "memn": _features(a["mem_norm_g_2"][0]),
        "ln_g": _features(a["conv_ln_g"][0]), "ln_b": _features(a["conv_ln_b"][0]), "dwb": _features(a["dw_bias"][0]),
        "dww": a["dw_kernel"][0].reshape(TAPS, 4, P).transpose(2, 1, 0).reshape(P, 4 * TAPS),
        "b_gate": _features(a["b_gate_2"][0]), "qn": _features(a["q_norm_g_2"][0]), "kvn": _features(a["kv_norm_g_2"][0]),
        "qh": rows(np.concatenate([qh, qh[80:96], qh[64:80]])),
        "kh": rows(kh),
        "khr": rows(np.concatenate([np.zeros(NOPE, np.float32), kh[NOPE:], kh[NOPE:]])),
        "cw": a["conv_w_2"][0].reshape(3, 4, P).transpose(2, 1, 0).reshape(P, 12), "cb": _features(a["conv_b_2"][0]),
        "mq": rows(a["mem_q_g_2"]), "mk": rows(a["mem_k_g_2"]), "invf": inv_col, "sign": sign_col,
    }
    return np.ascontiguousarray(np.concatenate([cols[n] for n in SMALL], axis=1))


def _tokens(x):
    return np.ascontiguousarray(x.T.reshape(KD, P, -1).transpose(1, 0, 2))


def _grid_tables():
    n = HD // 4
    inv = (np.float32(10000.0) ** (-np.arange(n, dtype=np.float32) / np.float32(n))).astype(np.float32)
    t = np.arange(T)
    pos = np.stack([t // W_GRID, t % W_GRID]).astype(np.float32)
    ang = (pos[:, None, :] * inv[None, :, None]).astype(np.float32).astype(np.float64)
    c, s = np.cos(ang), np.sin(ang)
    c = np.concatenate([c, c], axis=1).reshape(64, T)
    s = np.concatenate([-s, s], axis=1).reshape(64, T)
    return np.concatenate([c, c]).astype(np.float32), np.concatenate([s, s]).astype(np.float32)


def _window_mask():
    tiles = {v: t for t, v in reversed(list(enumerate(VARIANT)))}
    m = np.full((P, 5, 10, W_GRID), -1.0e30, np.float32)
    c = np.arange(W_GRID)
    c0 = np.clip(c - NA_C // 2, 0, W_GRID - NA_C)
    ok = (c[None, :] >= c0[:, None]) & (c[None, :] < c0[:, None] + NA_C)
    for v, t in tiles.items():
        for a in range(2):
            r = 2 * t + a
            r0 = int(np.clip(r - NA_R // 2, 0, ROWS - NA_R))
            for b in range(10):
                if r0 <= 2 * t + SHIFT[v] + b < r0 + NA_R:
                    m[a * 64:a * 64 + 64, v, b] = np.where(ok, 0.0, -1.0e30)
    return m.reshape(P, 5 * KEYS)


def kernel(**inputs):
    import numpy as _np
    import concourse.bacc as _bacc
    from concourse.bass_utils import run_bass_kernel_spmd as _run

    a = {k: _np.asarray(v) for k, v in inputs.items()}
    rope_c, rope_s = _grid_tables()
    rpb_pad = _np.pad(a["rpb"][0], ((0, 0), (2, 2), (48, 48)))
    rpb_pad = _np.tile(rpb_pad, (1, 1, W_GRID))
    arrays = {
        "x_t": _tokens(a["x"][0]), "ctx_t": _tokens(a["ctx"][0]), "mem_t": _tokens(a["mem_2"][0]),
        "w_ada": _np.ascontiguousarray(a["w_ada"][0].reshape(KD, P, 12, HALF)[:, :, 0:4].transpose(2, 1, 0, 3)),
        "w_ada_late": _late_modulation(a["w_ada"][0]),
        "units": _weight_units(a), "small": _small(a), "rope_c": rope_c, "rope_s": rope_s,
        "rpb_pad": rpb_pad, "mask": _window_mask(), "positions": a["positions_2"].reshape(T),
    }
    assert arrays["units"].shape == (N_UNITS, P, 1024)
    nc = _bacc.Bacc("TRN2", target_bir_lowering=False, num_devices=1)
    args = [nc.dram_tensor(n, v.shape, mybir.dt.from_np(v.dtype), kind="ExternalInput").ap() for n, v in arrays.items()]
    out = nc.dram_tensor("out_t", (P, KD, T), F32, kind="ExternalOutput").ap()
    spill = nc.dram_tensor("x_spill", (P, KD, T), F32).ap()
    rs_spill = nc.dram_tensor("rs_spill", (4, T // 4), F32).ap()
    build(nc, *args, out, spill, rs_spill)
    r = _run(nc, [arrays], core_ids=[0])
    got = r.results[0]["out_t"]
    return got.transpose(1, 0, 2).reshape(D, T).T.reshape(1, T, D)
```
